# Optimizing a Trainium2 kernel written in Bass

```python
import math
import jax, jax.numpy as jnp
from jax import lax
import numpy as np

D_MODEL = 1024
BATCH = 1
SEQ = 256
DEPTH = 2
DEC_BATCH = 8
DEC_SEQ = 1
PAST_LEN = 256
PAGE_SIZE = 128

N_MIXERS = 4
GROUP_WIDTH = D_MODEL // N_MIXERS
HEAD_DIM = 64
SSD_HEADS = GROUP_WIDTH // HEAD_DIM
SSD_GROUPS = 2
SSD_STATE = 64
SSD_CHUNK = 128
SSD_XBC = GROUP_WIDTH + 2 * SSD_GROUPS * SSD_STATE
SSD_COLS = GROUP_WIDTH + SSD_XBC + SSD_HEADS
FOX_HEADS = GROUP_WIDTH // HEAD_DIM
FOX_QBLOCK = 128
FOX_COLS = 3 * GROUP_WIDTH + FOX_HEADS
GDN_HEADS = 4
GDN_DK = GROUP_WIDTH // GDN_HEADS
GDN_DV = GROUP_WIDTH // GDN_HEADS
GDN_CHUNK = 128
GDN_QKV = 2 * GDN_HEADS * GDN_DK + GDN_HEADS * GDN_DV
GDN_COLS = GDN_QKV + 2 * GDN_HEADS + GDN_HEADS * GDN_DV
MOBA_HEADS = GROUP_WIDTH // HEAD_DIM
MOBA_BLOCK = 256
MOBA_TOPK = 3
MOBA_QBLOCK = 32
MOBA_COLS = 3 * GROUP_WIDTH
IN_COLS = SSD_COLS + FOX_COLS + GDN_COLS + MOBA_COLS
CONV_W = 4
D_FF = 2816
N_EXPERTS = 8
TOP_K = 2
D_FF_EXPERT = 1792
N_DENSE = (DEPTH + 1) // 2
N_MOE = DEPTH // 2
EPS = 1e-6

kernel_name = 'hymba_ssd_fox_gdn_moba_adaln_step'

def rmsnorm(x, g):
    xf = x.astype(jnp.float32)
    y = xf * lax.rsqrt(jnp.mean(xf * xf, axis=-1, keepdims=True) + EPS)
    return (y * g.astype(jnp.float32)).astype(x.dtype)

def l2norm(x):
    xf = x.astype(jnp.float32)
    return xf * lax.rsqrt(jnp.sum(xf * xf, axis=-1, keepdims=True) + EPS)

def causal_dwconv(u, buf, w, b=None):
    full = jnp.concatenate([buf.astype(u.dtype), u], axis=1)
    out = lax.conv_general_dilated(full, w.astype(u.dtype)[:, None, :], (1,), 'VALID',
                                   dimension_numbers=('NWC', 'WIO', 'NWC'),
                                   feature_group_count=u.shape[-1])
    if b is not None:
        out = out + b.astype(u.dtype)
    return out, full[:, full.shape[1] - (CONV_W - 1):]

def ssd_chunked(x, dt, a_neg, bm, cm, h0):
    bsz, L, H, P = x.shape
    c = SSD_CHUNK if L % SSD_CHUNK == 0 else L
    nc = L // c
    rep = SSD_HEADS // SSD_GROUPS
    bh = jnp.repeat(bm, rep, axis=2).reshape(bsz, nc, c, H, SSD_STATE)
    ch = jnp.repeat(cm, rep, axis=2).reshape(bsz, nc, c, H, SSD_STATE)
    xc = x.reshape(bsz, nc, c, H, P)
    dtc = dt.reshape(bsz, nc, c, H)
    gam = jnp.cumsum(dtc * a_neg, axis=2)
    idx = jnp.arange(c)
    causal = (idx[:, None] >= idx[None, :])[None, None, :, :, None]
    decay = jnp.exp(jnp.where(causal, gam[:, :, :, None, :] - gam[:, :, None, :, :], -jnp.inf))
    scores = jnp.einsum('bkihn,bkjhn->bkijh', ch, bh) * decay
    y_intra = jnp.einsum('bkijh,bkjh,bkjhp->bkihp', scores, dtc, xc)
    w_state = jnp.exp(gam[:, :, -1:, :] - gam) * dtc
    chunk_states = jnp.einsum('bkjh,bkjhp,bkjhn->bkhpn', w_state, xc, bh)
    chunk_decay = jnp.exp(gam[:, :, -1, :])

    def step(h, inp):
        dec, st = inp
        return dec[:, :, None, None] * h + st, h

    h_last, h_in = lax.scan(step, h0, (jnp.moveaxis(chunk_decay, 1, 0), jnp.moveaxis(chunk_states, 1, 0)))
    h_in = jnp.moveaxis(h_in, 0, 1)
    y_inter = jnp.einsum('bkihn,bkhpn->bkihp', ch, h_in) * jnp.exp(gam)[..., None]
    return (y_intra + y_inter).reshape(bsz, L, H, P), h_last

def gated_delta_chunked(q, k, v, beta, g, s0):
    bsz, L, H, DK = q.shape
    DV = v.shape[-1]
    c = GDN_CHUNK if L % GDN_CHUNK == 0 else L
    nc = L // c

    def chunks(t):
        t = t.reshape((bsz, nc, c) + t.shape[2:])
        return jnp.moveaxis(jnp.moveaxis(t, 1, 0), 2, 3)

    qc, kc, vc, bc, gc = chunks(q), chunks(k), chunks(v), chunks(beta), chunks(g)
    gam = jnp.cumsum(gc, axis=-1)
    diff = gam[..., :, None] - gam[..., None, :]
    idx = jnp.arange(c)
    dec_strict = jnp.exp(jnp.where(idx[:, None] > idx[None, :], diff, -jnp.inf))
    dec_incl = jnp.exp(jnp.where(idx[:, None] >= idx[None, :], diff, -jnp.inf))
    kk = jnp.einsum('nbhid,nbhjd->nbhij', kc, kc)
    amat = jnp.eye(c, dtype=kc.dtype) + bc[..., :, None] * kk * dec_strict
    rhs = jnp.concatenate([bc[..., None] * vc, (bc * jnp.exp(gam))[..., None] * kc], axis=-1)
    sol = lax.linalg.triangular_solve(amat, rhs, left_side=True, lower=True, unit_diagonal=True)
    u, wk = sol[..., :DV], sol[..., DV:]
    qk = jnp.einsum('nbhid,nbhjd->nbhij', qc, kc) * dec_incl
    g_last = gam[..., -1]
    k_tail = kc * jnp.exp(g_last[..., None] - gam)[..., None]
    q_head = qc * jnp.exp(gam)[..., None]

    def step(s, inp):
        u_, wk_, qk_, qh_, kt_, gl_ = inp
        w = u_ - jnp.einsum('bhcd,bhde->bhce', wk_, s)
        o = jnp.einsum('bhcd,bhde->bhce', qh_, s) + jnp.einsum('bhij,bhje->bhie', qk_, w)
        s = jnp.exp(gl_)[..., None, None] * s + jnp.einsum('bhcd,bhce->bhde', kt_, w)
        return s, o

    s_last, o = lax.scan(step, s0, (u, wk, qk, q_head, k_tail, g_last))
    o = jnp.moveaxis(jnp.moveaxis(o, 3, 2), 0, 1).reshape(bsz, L, H, DV)
    return o, s_last

def fox_attend(q, k, v, logf):
    bsz, Lq, H, D = q.shape
    T = k.shape[1]
    q_start = T - Lq
    cum = jnp.cumsum(logf.astype(jnp.float32), axis=1)
    ck = jnp.moveaxis(cum, 1, 2)
    cq = cum[:, q_start:]
    qb = FOX_QBLOCK if Lq % FOX_QBLOCK == 0 else Lq
    nqb = Lq // qb
    scale = HEAD_DIM ** -0.5
    kpos = jnp.arange(T)

    def block(args):
        qi, ci, pos = args
        s = jnp.einsum('bqhd,bkhd->bhqk', qi, k).astype(jnp.float32) * scale
        s = s + (jnp.moveaxis(ci, 1, 2)[..., :, None] - ck[:, :, None, :])
        s = jnp.where(kpos[None, :] <= pos[:, None], s, -jnp.inf)
        p = jax.nn.softmax(s, axis=-1)
        return jnp.einsum('bhqk,bkhd->bqhd', p.astype(v.dtype), v)

    qs = jnp.moveaxis(q.reshape(bsz, nqb, qb, H, D), 1, 0)
    cs = jnp.moveaxis(cq.reshape(bsz, nqb, qb, H), 1, 0)
    ps = (q_start + jnp.arange(Lq)).reshape(nqb, qb)
    out = lax.map(block, (qs, cs, ps))
    return jnp.moveaxis(out, 0, 1).reshape(bsz, Lq, H, D)

def moba_attend(q, k, v):
    bsz, Lq, H, D = q.shape
    T = k.shape[1]
    q_start = T - Lq
    nb = -(-T // MOBA_BLOCK)
    pad = nb * MOBA_BLOCK - T
    kp = jnp.pad(k, ((0, 0), (0, pad), (0, 0), (0, 0)))
    vp = jnp.pad(v, ((0, 0), (0, pad), (0, 0), (0, 0)))
    kb = jnp.moveaxis(kp.reshape(bsz, nb, MOBA_BLOCK, H, D), 3, 1)
    vb = jnp.moveaxis(vp.reshape(bsz, nb, MOBA_BLOCK, H, D), 3, 1)
    kmean = jnp.mean(kb.astype(jnp.float32), axis=3)
    n_sel = min(MOBA_TOPK, nb)
    slopes = jnp.exp2(-8.0 * jnp.arange(1, H + 1, dtype=jnp.float32) / H)
    blk_ids = jnp.arange(nb)
    offs = jnp.arange(MOBA_BLOCK)
    scale = HEAD_DIM ** -0.5
    gather = jax.vmap(jax.vmap(lambda t, ix: t[ix]))
    qb = MOBA_QBLOCK if Lq % MOBA_QBLOCK == 0 else Lq
    nqb = Lq // qb

    def block(args):
        qi, pos = args
        qh = jnp.moveaxis(qi, 1, 2)
        own = pos // MOBA_BLOCK
        gate = jnp.einsum('bhqd,bhnd->bhqn', qh.astype(jnp.float32), kmean)
        gate = jnp.where(blk_ids[None, :] < own[:, None], gate, -jnp.inf)
        top_v, top_i = lax.top_k(gate, n_sel)
        valid = jnp.isfinite(top_v)
        own_b = jnp.broadcast_to(own[None, None, :, None], top_i.shape[:3] + (1,)).astype(top_i.dtype)
        sel = jnp.concatenate([top_i, own_b], axis=-1)
        kg = gather(kb, sel)
        vg = gather(vb, sel)
        kpos = sel[..., None] * MOBA_BLOCK + offs
        s = jnp.einsum('bhqd,bhqnsd->bhqns', qh, kg).astype(jnp.float32) * scale
        dist = (pos[None, None, :, None, None] - kpos).astype(jnp.float32)
        s = s - slopes[None, :, None, None, None] * dist
        keep = jnp.concatenate([
            jnp.broadcast_to(valid[..., None], valid.shape + (MOBA_BLOCK,)),
            kpos[..., -1:, :] <= pos[None, None, :, None, None]], axis=3)
        s = jnp.where(keep, s, -jnp.inf)
        p = jax.nn.softmax(s.reshape(s.shape[:3] + (-1,)), axis=-1).reshape(s.shape)
        return jnp.einsum('bhqns,bhqnsd->bqhd', p.astype(vg.dtype), vg)

    qs = jnp.moveaxis(q.reshape(bsz, nqb, qb, H, D), 1, 0)
    ps = (q_start + jnp.arange(Lq)).reshape(nqb, qb)
    out = lax.map(block, (qs, ps))
    return jnp.moveaxis(out, 0, 1).reshape(bsz, Lq, H, D)

def token_mixers(h, lp, past):
    f32 = jnp.float32
    bsz, L, _ = h.shape
    proj = h @ lp['w_in']
    pa, pb, pc, pd = jnp.split(proj, [SSD_COLS, SSD_COLS + FOX_COLS, SSD_COLS + FOX_COLS + GDN_COLS], axis=-1)

    z_a, xbc, dt_raw = jnp.split(pa, [GROUP_WIDTH, GROUP_WIDTH + SSD_XBC], axis=-1)
    xbc, ssm_buf = causal_dwconv(xbc, past['ssm_buf'], lp['ssd_conv_w'], lp['ssd_conv_b'])
    xbc = jax.nn.silu(xbc).astype(f32)
    xa, b_a, c_a = jnp.split(xbc, [GROUP_WIDTH, GROUP_WIDTH + SSD_GROUPS * SSD_STATE], axis=-1)
    xa = xa.reshape(bsz, L, SSD_HEADS, HEAD_DIM)
    b_a = b_a.reshape(bsz, L, SSD_GROUPS, SSD_STATE)
    c_a = c_a.reshape(bsz, L, SSD_GROUPS, SSD_STATE)
    dt = jax.nn.softplus(dt_raw.astype(f32) + lp['ssd_dt_bias'].astype(f32))
    a_neg = -jnp.exp(lp['ssd_a_log'].astype(f32))
    y_a, ssm_h = ssd_chunked(xa, dt, a_neg, b_a, c_a, past['ssm_h'].astype(f32))
    y_a = (y_a + lp['ssd_d'].astype(f32)[:, None] * xa).reshape(bsz, L, GROUP_WIDTH)
    y_a = rmsnorm(y_a * jax.nn.silu(z_a.astype(f32)), lp['ssd_norm'])

    fq, fk, fv, ff = jnp.split(pb, [GROUP_WIDTH, 2 * GROUP_WIDTH, 3 * GROUP_WIDTH], axis=-1)
    fq = rmsnorm(fq.reshape(bsz, L, FOX_HEADS, HEAD_DIM), lp['fox_q_norm'])
    fk = rmsnorm(fk.reshape(bsz, L, FOX_HEADS, HEAD_DIM), lp['fox_k_norm'])
    fv = fv.reshape(bsz, L, FOX_HEADS, HEAD_DIM)
    logf = jax.nn.log_sigmoid(ff.astype(f32) + lp['fox_b_f'].astype(f32))
    if past['fox'] is None:
        fk_all, fv_all, lf_all = fk, fv, logf
    else:
        pk, pv, plf = past['fox']
        fk_all = jnp.concatenate([pk.astype(fk.dtype), fk], axis=1)
        fv_all = jnp.concatenate([pv.astype(fv.dtype), fv], axis=1)
        lf_all = jnp.concatenate([plf.astype(f32), logf], axis=1)
    y_b = fox_attend(fq, fk_all, fv_all, lf_all).reshape(bsz, L, GROUP_WIDTH)

    qkv, beta_raw, a_raw, z_c = jnp.split(pc, [GDN_QKV, GDN_QKV + GDN_HEADS, GDN_QKV + 2 * GDN_HEADS], axis=-1)
    qkv, gdn_buf = causal_dwconv(qkv, past['gdn_buf'], lp['gdn_conv_w'])
    qkv = jax.nn.silu(qkv)
    gq, gk, gv = jnp.split(qkv, [GDN_HEADS * GDN_DK, 2 * GDN_HEADS * GDN_DK], axis=-1)
    gq = l2norm(gq.reshape(bsz, L, GDN_HEADS, GDN_DK)) * (GDN_DK ** -0.5)
    gk = l2norm(gk.reshape(bsz, L, GDN_HEADS, GDN_DK))
    gv = gv.reshape(bsz, L, GDN_HEADS, GDN_DV).astype(f32)
    beta = jax.nn.sigmoid(beta_raw.astype(f32))
    g_log = -jnp.exp(lp['gdn_a_log'].astype(f32)) * jax.nn.softplus(a_raw.astype(f32) + lp['gdn_dt_bias'].astype(f32))
    o_c, gdn_s = gated_delta_chunked(gq, gk, gv, beta, g_log, past['gdn_s'].astype(f32))
    o_c = rmsnorm(o_c, lp['gdn_norm']) * jax.nn.silu(z_c.reshape(bsz, L, GDN_HEADS, GDN_DV).astype(f32))
    y_c = o_c.reshape(bsz, L, GROUP_WIDTH)

    mq, mk, mv = jnp.split(pd, 3, axis=-1)
    mq = rmsnorm(mq.reshape(bsz, L, MOBA_HEADS, HEAD_DIM), lp['moba_q_norm'])
    mk = rmsnorm(mk.reshape(bsz, L, MOBA_HEADS, HEAD_DIM), lp['moba_k_norm'])
    mv = mv.reshape(bsz, L, MOBA_HEADS, HEAD_DIM)
    if past['moba'] is None:
        mk_all, mv_all = mk, mv
    else:
        pk, pv = past['moba']
        mk_all = jnp.concatenate([pk.astype(mk.dtype), mk], axis=1)
        mv_all = jnp.concatenate([pv.astype(mv.dtype), mv], axis=1)
    y_d = moba_attend(mq, mk_all, mv_all).reshape(bsz, L, GROUP_WIDTH)

    y = jnp.concatenate([y_a.astype(h.dtype), y_b.astype(h.dtype), y_c.astype(h.dtype), y_d.astype(h.dtype)], axis=-1)
    y = y @ lp['w_out']
    return y, (fk, fv, logf, mk, mv, ssm_h, ssm_buf, gdn_s, gdn_buf)

def swiglu(h, w_gate, w_up, w_down):
    return (jax.nn.silu(h @ w_gate) * (h @ w_up)) @ w_down

def moe_swiglu(h, router, w_gate, w_up, w_down):
    logits = (h @ router).astype(jnp.float32)
    top_v, top_i = lax.top_k(logits, TOP_K)
    wts = jax.nn.softmax(top_v, axis=-1)
    gates = jnp.sum(jax.nn.one_hot(top_i, N_EXPERTS, dtype=jnp.float32) * wts[..., None], axis=-2)
    out = jnp.zeros_like(h)
    for e in range(N_EXPERTS):
        out = out + (gates[..., e:e + 1] * swiglu(h, w_gate[e], w_up[e], w_down[e]).astype(jnp.float32)).astype(h.dtype)
    return out

def trunk_layer(x, mod, g_mix, g_ffn, lp, past, ffn):
    sh1, sc1, gt1, sh2, sc2, gt2 = [m[:, None, :] for m in jnp.split(mod.astype(x.dtype), 6, axis=-1)]
    h = rmsnorm(x, g_mix) * (1 + sc1) + sh1
    y, state = token_mixers(h, lp, past)
    x = x + gt1 * y
    h = rmsnorm(x, g_ffn) * (1 + sc2) + sh2
    x = x + gt2 * ffn(h)
    return x, state

def setup_inputs(seed: int = 0) -> dict:
    key = jax.random.key(seed)
    ks = iter(jax.random.split(key, 64))
    f32 = jnp.float32
    n_pages = PAST_LEN // PAGE_SIZE
    n_used = DEC_BATCH * n_pages
    n_pool = n_used + max(1, n_used // 4)

    def nrm(shape, scale):
        return scale * jax.random.normal(next(ks), shape, f32)

    def gain(shape):
        return 1.0 + nrm(shape, 0.02)

    def dt_bias(shape):
        dt = jnp.exp(jax.random.uniform(next(ks), shape, f32, math.log(1e-3), math.log(1e-1)))
        return dt + jnp.log(-jnp.expm1(-dt))

    def a_log(shape):
        return jnp.log(jax.random.uniform(next(ks), shape, f32, 1.0, 16.0))

    d = D_MODEL
    inputs = {}
    inputs['x_prompt'] = nrm((BATCH, SEQ, d), 1.0)
    inputs['x_sample'] = nrm((DEC_BATCH, DEC_SEQ, d), 1.0)
    inputs['cache_fox_k'] = nrm((DEPTH, n_pool, PAGE_SIZE, FOX_HEADS, HEAD_DIM), 1.0)
    inputs['cache_fox_v'] = nrm((DEPTH, n_pool, PAGE_SIZE, FOX_HEADS, HEAD_DIM), 1.0)
    inputs['cache_fox_logf'] = jax.nn.log_sigmoid(4.0 + nrm((DEPTH, n_pool, PAGE_SIZE, FOX_HEADS), 1.0))
    inputs['cache_moba_k'] = nrm((DEPTH, n_pool, PAGE_SIZE, MOBA_HEADS, HEAD_DIM), 1.0)
    inputs['cache_moba_v'] = nrm((DEPTH, n_pool, PAGE_SIZE, MOBA_HEADS, HEAD_DIM), 1.0)
    inputs['state_ssm'] = nrm((DEPTH, DEC_BATCH, SSD_HEADS, HEAD_DIM, SSD_STATE), 0.1)
    inputs['state_ssm_conv'] = nrm((DEPTH, DEC_BATCH, CONV_W - 1, SSD_XBC), 1.0)
    inputs['state_gdn'] = nrm((DEPTH, DEC_BATCH, GDN_HEADS, GDN_DK, GDN_DV), 0.1)
    inputs['state_gdn_conv'] = nrm((DEPTH, DEC_BATCH, CONV_W - 1, GDN_QKV), 1.0)
    inputs['page_table'] = jax.random.permutation(next(ks), n_pool)[:n_used].reshape(DEC_BATCH, n_pages).astype(jnp.int32)
    inputs['c_prompt'] = nrm((BATCH, d), 1.0)
    inputs['c_sample'] = nrm((DEC_BATCH, d), 1.0)
    inputs['w_ada'] = nrm((DEPTH, d, 6 * d), 0.5 * d ** -0.5)
    inputs['b_ada'] = nrm((DEPTH, 6 * d), 0.02)
    inputs['norm_mix'] = gain((DEPTH, d))
    inputs['norm_ffn'] = gain((DEPTH, d))
    inputs['w_in'] = nrm((DEPTH, d, IN_COLS), d ** -0.5)
    inputs['w_out'] = nrm((DEPTH, d, d), d ** -0.5)
    inputs['ssd_conv_w'] = nrm((DEPTH, CONV_W, SSD_XBC), CONV_W ** -0.5)
    inputs['ssd_conv_b'] = nrm((DEPTH, SSD_XBC), 0.02)
    inputs['ssd_dt_bias'] = dt_bias((DEPTH, SSD_HEADS))
    inputs['ssd_a_log'] = a_log((DEPTH, SSD_HEADS))
    inputs['ssd_d'] = 1.0 + nrm((DEPTH, SSD_HEADS), 0.1)
    inputs['ssd_norm'] = gain((DEPTH, GROUP_WIDTH))
    inputs['fox_b_f'] = 4.0 + nrm((DEPTH, FOX_HEADS), 0.5)
    inputs['fox_q_norm'] = gain((DEPTH, HEAD_DIM))
    inputs['fox_k_norm'] = gain((DEPTH, HEAD_DIM))
    inputs['gdn_conv_w'] = nrm((DEPTH, CONV_W, GDN_QKV), CONV_W ** -0.5)
    inputs['gdn_a_log'] = a_log((DEPTH, GDN_HEADS))
    inputs['gdn_dt_bias'] = dt_bias((DEPTH, GDN_HEADS))
    inputs['gdn_norm'] = gain((DEPTH, GDN_DV))
    inputs['moba_q_norm'] = gain((DEPTH, HEAD_DIM))
    inputs['moba_k_norm'] = gain((DEPTH, HEAD_DIM))
    inputs['ffn_w_gate'] = nrm((N_DENSE, d, D_FF), d ** -0.5)
    inputs['ffn_w_up'] = nrm((N_DENSE, d, D_FF), d ** -0.5)
    inputs['ffn_w_down'] = nrm((N_DENSE, D_FF, d), D_FF ** -0.5)
    inputs['moe_router'] = nrm((N_MOE, d, N_EXPERTS), d ** -0.5)
    inputs['moe_w_gate'] = nrm((N_MOE, N_EXPERTS, d, D_FF_EXPERT), d ** -0.5)
    inputs['moe_w_up'] = nrm((N_MOE, N_EXPERTS, d, D_FF_EXPERT), d ** -0.5)
    inputs['moe_w_down'] = nrm((N_MOE, N_EXPERTS, D_FF_EXPERT, d), D_FF_EXPERT ** -0.5)
    return inputs

def reference(x_prompt, x_sample, cache_fox_k, cache_fox_v, cache_fox_logf, cache_moba_k, cache_moba_v,
              state_ssm, state_ssm_conv, state_gdn, state_gdn_conv, page_table, c_prompt, c_sample,
              w_ada, b_ada, norm_mix, norm_ffn, w_in, w_out,
              ssd_conv_w, ssd_conv_b, ssd_dt_bias, ssd_a_log, ssd_d, ssd_norm,
              fox_b_f, fox_q_norm, fox_k_norm,
              gdn_conv_w, gdn_a_log, gdn_dt_bias, gdn_norm,
              moba_q_norm, moba_k_norm,
              ffn_w_gate, ffn_w_up, ffn_w_down,
              moe_router, moe_w_gate, moe_w_up, moe_w_down):
    bp = x_prompt.shape[0]
    past_len = page_table.shape[1] * PAGE_SIZE

    def paged_rows(cache):
        rows = cache[page_table]
        return rows.reshape((rows.shape[0], past_len) + rows.shape[3:])

    cp = jax.nn.silu(c_prompt)
    cs = jax.nn.silu(c_sample)
    xp, xs = x_prompt, x_sample
    st_prompt, st_sample = [], []
    for l in range(DEPTH):
        lp = dict(w_in=w_in[l], w_out=w_out[l],
                  ssd_conv_w=ssd_conv_w[l], ssd_conv_b=ssd_conv_b[l], ssd_dt_bias=ssd_dt_bias[l],
                  ssd_a_log=ssd_a_log[l], ssd_d=ssd_d[l], ssd_norm=ssd_norm[l],
                  fox_b_f=fox_b_f[l], fox_q_norm=fox_q_norm[l], fox_k_norm=fox_k_norm[l],
                  gdn_conv_w=gdn_conv_w[l], gdn_a_log=gdn_a_log[l], gdn_dt_bias=gdn_dt_bias[l],
                  gdn_norm=gdn_norm[l], moba_q_norm=moba_q_norm[l], moba_k_norm=moba_k_norm[l])
        i = l // 2
        if l % 2 == 0:
            ffn = lambda t, i=i: swiglu(t, ffn_w_gate[i], ffn_w_up[i], ffn_w_down[i])
        else:
            ffn = lambda t, i=i: moe_swiglu(t, moe_router[i], moe_w_gate[i], moe_w_up[i], moe_w_down[i])
        past_p = dict(fox=None, moba=None,
                      ssm_h=jnp.zeros((bp, SSD_HEADS, HEAD_DIM, SSD_STATE), jnp.float32),
                      ssm_buf=jnp.zeros((bp, CONV_W - 1, SSD_XBC), x_prompt.dtype),
                      gdn_s=jnp.zeros((bp, GDN_HEADS, GDN_DK, GDN_DV), jnp.float32),
                      gdn_buf=jnp.zeros((bp, CONV_W - 1, GDN_QKV), x_prompt.dtype))
        past_s = dict(fox=(paged_rows(cache_fox_k[l]), paged_rows(cache_fox_v[l]), paged_rows(cache_fox_logf[l])),
                      moba=(paged_rows(cache_moba_k[l]), paged_rows(cache_moba_v[l])),
                      ssm_h=state_ssm[l], ssm_buf=state_ssm_conv[l],
                      gdn_s=state_gdn[l], gdn_buf=state_gdn_conv[l])
        xp, sp = trunk_layer(xp, cp @ w_ada[l] + b_ada[l], norm_mix[l], norm_ffn[l], lp, past_p, ffn)
        xs, ss = trunk_layer(xs, cs @ w_ada[l] + b_ada[l], norm_mix[l], norm_ffn[l], lp, past_s, ffn)
        st_prompt.append(sp)
        st_sample.append(ss)

    def stack(states, j):
        return jnp.stack([s[j] for s in states], axis=0)

    fox_k_p, fox_v_p, fox_logf_p = stack(st_prompt, 0), stack(st_prompt, 1), stack(st_prompt, 2)
    moba_k_p, moba_v_p = stack(st_prompt, 3), stack(st_prompt, 4)
    ssm_p, ssm_conv_p = stack(st_prompt, 5), stack(st_prompt, 6)
    gdn_p, gdn_conv_p = stack(st_prompt, 7), stack(st_prompt, 8)
    fox_k_s, fox_v_s, fox_logf_s = stack(st_sample, 0), stack(st_sample, 1), stack(st_sample, 2)
    moba_k_s, moba_v_s = stack(st_sample, 3), stack(st_sample, 4)
    ssm_s, ssm_conv_s = stack(st_sample, 5), stack(st_sample, 6)
    gdn_s, gdn_conv_s = stack(st_sample, 7), stack(st_sample, 8)
    return (xp, xs,
            fox_k_p, fox_v_p, fox_logf_p, moba_k_p, moba_v_p, ssm_p, ssm_conv_p, gdn_p, gdn_conv_p,
            fox_k_s, fox_v_s, fox_logf_s, moba_k_s, moba_v_s, ssm_s, ssm_conv_s, gdn_s, gdn_conv_s)


_drawn_inputs = setup_inputs


def setup_inputs(seed=0):
    import zlib

    import numpy as np

    out = dict(_drawn_inputs(seed))
    spreads = {}
    factors = {'cache_fox_logf': 24.835,
     'norm_ffn': 3.447,
     'ssd_d': 3.697,
     'ssd_norm': 7.199,
     'fox_q_norm': 22.929,
     'fox_k_norm': 2.835,
     'gdn_norm': 8.0,
     'moba_q_norm': 8.0,
     'moba_k_norm': 7.975}
    for name, (base, spread) in spreads.items():
        noise = np.random.default_rng([zlib.crc32(name.encode()), seed]).standard_normal(out[name].shape)
        drawn = base * np.exp(spread * noise) if base else spread * noise
        out[name] = __import__('jax').numpy.asarray(drawn.astype(out[name].dtype))
    for name, factor in factors.items():
        out[name] = (out[name] * factor).astype(out[name].dtype)
    return out
```

```python
from contextlib import ExitStack

import numpy as np
import concourse.bass as bass
from concourse import mybir

F32 = mybir.dt.float32
I32 = mybir.dt.int32
ALU = mybir.AluOpType
ACT = mybir.ActivationFunctionType
AX = mybir.AxisListType

P = 128
D = 1024
KD = D // P
SEQ = 256
NS = 8
NT = SEQ + NS
DEPTH = 2
PAST = 256
PAGE = 128
PAGES = PAST // PAGE
POOL = 20
HD = 64
H = 4
GW = 256
CW = 4
XBC = 512
QKV = 768
IN_COLS = 3344
FF = 2816
FE = 1792
NE = 8
EPS = 1e-6
NEG = -1e30
CH = P
NG = SEQ // CH
SC = P // NS
SP_ = PAST // SC
SLOT = 4096
NSLOT = 4
LEVELS = [1, 2, 4, 8, 16, 32, 64]
UW = 3 + SEQ + CW * NS
CVW = UW - 3
G_SLABS = [(1544, 384), (1928, 384), (2320, 256)]
S_SLABS = [(0, 384), (384, 384)]
F_SLABS = [(772, 384), (1156, 384)]
M_SLABS = [(2576, 384), (2960, 384)]
IN_SLABS = G_SLABS + S_SLABS + F_SLABS + M_SLABS
SMALL = [(768, 4, 0), (1540, 4, 4), (2312, 8, 8)]


def consts():
    i = np.arange(P)
    parts = {}
    parts["ident"] = np.eye(P)
    parts["ones"] = np.ones((P, P))
    parts["upper"] = (i[:, None] <= i[None, :])
    parts["blk"] = (i[:, None] // HD == i[None, :] // HD)
    parts["causal_t"] = np.where(i[None, :] >= i[:, None], 0.0, NEG)
    causal = np.where(i[None, :] <= i[:, None], 0.0, NEG)
    parts["mask3"] = np.concatenate([causal, np.zeros((P, P)), causal], 1)
    for h in range(H):
        s = 2.0 ** (-8.0 * (h + 1) / H)
        own = -s * (i[:, None] - i[None, :]) + causal
        before = -s * (i[:, None] + P - i[None, :])
        parts[f"alibi{h}"] = np.concatenate([own, before, own], 1)
    for s in LEVELS:
        parts[f"level{s}"] = ((i[:, None] // (2 * s) == i[None, :] // (2 * s)) & ((i[:, None] // s) % 2 == 1)
                              & ((i[None, :] // s) % 2 == 0))
    parts["later"] = (i[:, None] // SC == i[None, :] // SC) & (i[:, None] > i[None, :])
    parts["own_col"] = (i[:, None] // SC == np.arange(NS)[None, :])
    own_row = np.zeros((P, P))
    own_row[:NS] = (np.arange(NS)[:, None] == i[None, :] // SC)
    parts["own_row"] = own_row
    one = np.zeros((P, NS * P))
    for b in range(NS):
        one[b, b * P:(b + 1) * P] = 1.0
    parts["one_row"] = one
    pos = (i[:, None] % SC) * SP_ + np.arange(SP_)[None, :]
    sl = 2.0 ** (-8.0 * (np.arange(H) + 1) / H)
    parts["alibi_dec"] = (-(PAST - pos)[:, :, None] * sl).reshape(P, -1)
    e = np.arange(NE)
    parts["tie"] = np.broadcast_to((e[None, None, :] < e[None, :, None]), (P, NE, NE)).reshape(P, -1)
    at, off = {}, 0
    for k, v in parts.items():
        at[k] = (off, v.shape[1])
        off += v.shape[1]
    return np.concatenate([np.asarray(v, np.float32) for v in parts.values()], 1), at


MIX_CHUNKS = 4
ADA_CHUNKS = 6 * D // 512
MIXER_ADA = [[(0, c) for c in range(MIX_CHUNKS, ADA_CHUNKS)] + [(1, c) for c in range(MIX_CHUNKS)],
             [(1, c) for c in range(MIX_CHUNKS, ADA_CHUNKS)]]
ADA_UNITS = [
    {"gdn": 4, "ssd": 2, "att0": 2, **{f"att{n}": 1 for n in range(1, 8)}, "att8": 2, "v_rows": 1, "ks": 2, "keys": 4},
    {"gdn": 0, "ssd": 2, **{f"att{n}": 1 for n in range(9)}, "v_rows": 1, "ks": 0, "keys": 4}]
for _l in range(DEPTH):
    assert sum(ADA_UNITS[_l].values()) == 2 * len(MIXER_ADA[_l])


def ada_units(l, place):
    names = list(ADA_UNITS[l])
    first = sum(ADA_UNITS[l][n] for n in names[:names.index(place)])
    return range(first, first + ADA_UNITS[l][place])


def plan_stream():
    out = [("ada", 0, (c,), 2) for c in range(MIX_CHUNKS)]
    for l in range(DEPTH):
        out += [("in", l, s, s[1] // P) for s in IN_SLABS]
        ada = [("ada", la, (c,), 2) for la, c in MIXER_ADA[l]]
        out += ada[:-2] + [("k", l, (m,), 0) for m in range(2)] + ada[-2:] + [("v", l, (m,), 1) for m in range(2)]
        out += [("out", l, (c,), 4) for c in range(2)]
        if l == 0:
            out += [("gu", l, (c,), 4) for c in range(FF // 256)]
            out += [("down", l, (c, h), 2 if h else 1) for c in range(4) for h in range(2)]
    return out


def build(nc, A, O, const_at, NCONST):
    ctx = ExitStack()
    with ctx:
        def sb(name, shape, dt=F32):
            return ctx.enter_context(nc.sbuf_tensor(name, shape, dt))

        sems = {}

        def sem(name):
            if name not in sems:
                sems[name] = ctx.enter_context(nc.semaphore(name))
            return sems[name]

        cst = sb("cst", [P, NCONST])

        def C(name):
            o, n = const_at[name]
            return cst[:, o:o + n]

        ring = [sb(f"ring{i}", [P, SLOT]) for i in range(NSLOT)]
        xT = sb("xT", [P, KD, NT])
        hT = sb("hT", [P, KD, NT])
        yT = hT
        prm1 = sb("prm1", [P, P])
        prm2 = sb("prm2", [P, 102])
        modT = sb("modT", [P, 48, 9])
        gain1 = sb("gain1", [P, KD, 9])
        cT = sb("cT", [P, KD, 9])
        w_small = sb("w_small", [P, DEPTH, KD, 16])
        brow = sb("brow", [P, DEPTH, 16])
        alog = sb("alog", [P, DEPTH, 8])
        nega = sb("nega", [P, DEPTH, 8])
        dcol = sb("dcol", [P, DEPTH, 2])
        router = sb("router", [P, KD, NE])
        pt = sb("pt", [1, NS * PAGES], I32)
        rstd = sb("rstd", [P, 4, NT])
        epsc = sb("epsc", [P, 1])
        yd16 = sb("yd16", [P, 16])
        sxy = sb("sxy", [P, NS])

        ARENA = 25400
        arena = sb("arena", [P, ARENA])
        top = [0]

        def carve(shape, at=None, parts=P):
            n = int(np.prod(shape))
            o = top[0] if at is None else at
            if at is None:
                top[0] += n
            assert o + n <= ARENA, (o, n)
            v = arena[0:parts, o:o + n]
            if len(shape) == 2:
                v = v.rearrange("p (a b) -> p a b", a=shape[0])
            elif len(shape) == 3:
                v = v.rearrange("p (a b c) -> p a b c", a=shape[0], b=shape[1])
            return v

        u = carve((10, UW))
        states_at = 0
        hst = carve((NS * 2, HD), at=0)
        gst = carve((NS * 2, HD), at=1024)
        cv = carve((2, CVW))
        act = carve((10, NT))
        zz = carve((4, NT))
        fm = carve((12, NT))
        sq = carve((4, NT))
        sm = carve((3, 16))
        sma = carve((3, 16))
        sme = carve((3, 16))
        smp = carve((3, 16))
        beta = carve((3, 4))
        cin = carve((3, 12))
        cum = carve((NG, 12))
        stq = carve((16,))
        fmj = carve((8, NS))
        nlf = carve((3, 4))
        rowF = carve((H, SEQ))
        oT = carve((2, NT))
        yA = carve((2, NT))
        convrow = carve((XBC + QKV,))
        tail = carve((10, 27))
        phase = top[0]
        egG = carve((NG * H, CH))
        decG = carve((NG * H, CH))
        AT = carve((NG * H, CH))
        X = carve((NG * H, CH))
        XT = carve((NG * H, CH))
        Qs = carve((NG * H, CH))
        kvt = carve((NG * 4, P))
        Rv = carve((NG * H, HD))
        Rk = carve((NG * H, HD))
        ktail = carve((NG * H, HD))
        wkT = carve((2, CH))
        wtok = carve((H, HD))
        S0 = carve((2, HD))
        S1 = carve((2, HD))
        qh = carve((2, CH))
        sc4 = carve((NG, 4))
        be = carve((NG, 4))
        end1 = top[0]
        top[0] = phase
        egS = carve((NG * H, CH))
        MT = carve((NG * H, CH))
        xt = carve((3, P))
        xdt = carve((H, HD))
        xw = carve((H, HD))
        ws = carve((NG, 4))
        Cg = carve((2, CH))
        hs0 = carve((2, HD))
        hs1 = carve((2, HD))
        s3 = carve((2, 3 * CH), at=phase)
        PT = carve((2, 3 * CH), at=phase + 6 * CH)
        nmx = carve((8, 2))
        rsum = carve((8, 2))
        kvp = carve((NG * 4, GW))
        stok = carve((6, GW))
        dtok = carve((4, P))
        hsout = carve((P,))
        qbc = carve((2, GW))
        tmpA = carve((16, HD), at=phase)
        tmpB = carve((16, HD), at=phase + 1024)
        lf = carve((SP_, H))
        lfb = carve((SP_, H))
        scd = carve((SP_, 8))
        mcol = carve((8,))
        mtok = carve((8,))
        ms8 = carve((8,))
        sself = carve((8,))
        rden = carve((8,))
        psums = carve((8,))
        Pd = carve((2 * SP_, NS * H))
        psb = carve((4, NS))
        kb = carve((NS, 2))
        end2 = top[0]
        top[0] = 0
        hid = carve((FF // P, NT))
        acc = carve((KD, NT))
        gbc = carve((NE, NT))
        sg = carve((2, NT))
        sgg = carve((2, NT))
        lg = carve((3, NE))
        gates = carve((3, NE))
        cmp = carve((3 * NE, NE))
        cmp2 = carve((3 * NE, NE))
        rank = carve((3, NE))
        v1 = carve((3,))
        stage = carve((3, D))
        cstage = carve((D,))
        prow1 = carve((P,))
        prow2 = carve((P,))
        assert max(end1, end2, top[0]) <= ARENA, (end1, end2, top[0])

        bank = [ctx.enter_context(nc.psum_tensor(f"bank{i}", [P, 512], F32)) for i in range(8)]

        plan = plan_stream()
        n_pre = len(plan)
        first_slot = (2 - (n_pre - 1)) % NSLOT
        slot_of = [(i + first_slot) % NSLOT for i in range(n_pre)]
        dmas_of = {"ada": 1, "in": 1, "k": NS * PAGES, "v": NS * PAGES, "out": 1, "gu": 2, "down": 1}
        landed = [sem(f"slot{i}_landed") for i in range(NSLOT)]
        tile_done = sem("tile_done")
        k_used = sem("k_used")
        slot_count = [0] * NSLOT
        landed_at, done_at, kdone_at = [], [], []
        ticks = kticks = 0
        for i, (kind, l, a, t) in enumerate(plan):
            s = slot_of[i]
            slot_count[s] += 16 * dmas_of[kind]
            landed_at.append(slot_count[s])
            ticks += t
            kticks += kind == "k"
            done_at.append(ticks)
            kdone_at.append(kticks)
        ticks_pre = ticks
        index = {(kind, l) + tuple(a): i for i, (kind, l, a, t) in enumerate(plan)}
        E_GU, E_DN = FE // 256, 4
        E_SLABS = [("gu", c) for c in range(E_GU)] + [("down", c) for c in range(E_DN)]
        e_slot = [i % NSLOT for i in range(len(E_SLABS))]
        e_ticks, e_landed, per_slot, t = [], [], [0] * NSLOT, 0
        for i, (kind, c) in enumerate(E_SLABS):
            t += 4 if kind == "gu" else 2
            e_ticks.append(t)
            per_slot[e_slot[i]] += 32 if kind == "gu" else 16
            e_landed.append(per_slot[e_slot[i]])
        E_TICKS = t

        def ticks_before(i):
            return done_at[i] - plan[i][3]

        class Order:

            def __init__(self, eng, chain):
                self.eng, self.chain = eng, chain
                self.seen, self.made, self.last = {}, {}, None

            def need(self, name, n=1):
                self.seen[name] = self.seen.get(name, 0) + n
                self.eng.wait_ge(sem(name), self.seen[name])

            def go(self, ins, name=None):
                s = sem(self.chain if name is None else name)
                self.made[s.name] = self.made.get(s.name, 0) + 1
                ins.then_inc(s, 1)
                self.last = (s, self.made[s.name])

            def settle(self):
                self.eng.wait_ge(*self.last)

        STORES = 20
        STARTS, PARAMS = 6, DEPTH * 14

        block = ctx.enter_context(nc.Block())

        @block.sync
        def _(sp):
            def load(dst, src, name):
                sp.dma_start(dst, src).then_inc(sem(name), 16)

            load(cstage[0:1, :], A["c_prompt"], "c_landed")
            load(cstage[1:9, :], A["c_sample"], "c_landed")
            load(cst[:, :], A["consts"], "c_landed")

            def slab(i):
                kind, l, a, _ = plan[i]
                s = slot_of[i]
                if i >= NSLOT:
                    if plan[i - NSLOT][0] == "k":
                        sp.wait_ge(k_used, kdone_at[i - NSLOT])
                    else:
                        sp.wait_ge(tile_done, done_at[i - NSLOT])
                r = ring[s]
                if kind == "ada":
                    sp.dma_start(r[:, :].rearrange("p (k n) -> p k n", k=KD),
                                 A["w_ada"][l].rearrange("(k p) n -> p k n", p=P)[:, :, a[0] * 512:a[0] * 512 + 512]
                                 ).then_inc(landed[s], 16)
                elif kind == "in":
                    sp.dma_start(r[:, 0:KD * a[1]].rearrange("p (k n) -> p k n", k=KD),
                                 A["w_in"][l].rearrange("(k p) n -> p k n", p=P)[:, :, a[0]:a[0] + a[1]]
                                 ).then_inc(landed[s], 16)
                elif kind == "out":
                    sp.dma_start(r[:, :].rearrange("p (k n) -> p k n", k=KD),
                                 A["w_out"][l].rearrange("(k p) n -> p k n", p=P)[:, :, a[0] * 512:a[0] * 512 + 512]
                                 ).then_inc(landed[s], 16)
                elif kind == "gu":
                    for n, name in enumerate(("ffn_w_gate", "ffn_w_up")):
                        sp.dma_start(r[:, n * 2048:(n + 1) * 2048].rearrange("p (k n) -> p k n", k=KD),
                                     A[name][0].rearrange("(k p) n -> p k n", p=P)[:, :, a[0] * 256:a[0] * 256 + 256]
                                     ).then_inc(landed[s], 16)
                elif kind == "down":
                    kt = FF // P // 2
                    sp.dma_start(r[:, 0:kt * 256].rearrange("p (k n) -> p k n", k=kt),
                                 A["ffn_w_down"][0].rearrange("(k p) n -> p k n", p=P)[
                                     :, a[1] * kt:(a[1] + 1) * kt, a[0] * 256:a[0] * 256 + 256]
                                 ).then_inc(landed[s], 16)
                else:
                    name = f"cache_{('fox', 'moba')[a[0]]}_{kind}"
                    src = A[name][l].rearrange("n (c s) h d -> n c (s h d)", s=SP_)
                    for b in range(NS):
                        for g in range(PAGES):
                            q = b * SC + g * (PAGE // SP_)
                            sp.dma_start(r[q:q + PAGE // SP_, :], src[bass.ds(page[b * PAGES + g], 1), :, :]
                                         .rearrange("o c f -> (o c) f")).then_inc(landed[s], 16)

            slab(0)
            load(stage[:, 0:2, :], A["x_prompt"][0].rearrange("(g p) d -> p g d", p=P), "start_landed")
            load(stage[0:NS, 2, :], A["x_sample"].rearrange("b s d -> (b s) d"), "start_landed")
            load(pt[:, :], A["page_table"].rearrange("(o b) n -> o (b n)", o=1), "start_landed")
            slab(1)
            load(prow1[0:96, :], A["b_ada"].rearrange("l (m p) -> (l m) p", p=P), "start_landed")
            load(prow1[96:112, :], A["norm_mix"].rearrange("l (m p) -> (l m) p", p=P), "start_landed")
            load(prow1[112:128, :], A["norm_ffn"].rearrange("l (m p) -> (l m) p", p=P), "start_landed")
            slab(2)
            slab(3)
            sp.wait_ge(sem("start_landed"), 16 * STARTS)
            page = [sp.value_load(pt[0:1, i:i + 1], min_val=0, max_val=POOL - 1) for i in range(NS * PAGES)]

            for l in range(DEPTH):
                lo = index[("in", l) + IN_SLABS[0]]
                if l:
                    sp.wait_ge(sem("tails_packed"), 1)
                    sp.wait_ge(sem("stored"), 16 * STORES)
                if l == 0:
                    sp.wait_ge(sem("params_used"), 2)
                    sp.wait_ge(sem("c_copied"), 1)
                    sp.wait_ge(sem("x_copied0"), 4)
                    sp.wait_ge(sem("x_copied1"), 4)
                load(convrow[0:24, 0:QKV], A["state_gdn_conv"][l].rearrange("b k c -> (b k) c"), "convrow_landed")
                load(convrow[0:24, QKV:QKV + XBC], A["state_ssm_conv"][l].rearrange("b k c -> (b k) c"),
                     "convrow_landed")
                n_l = (index[("in", 1) + IN_SLABS[0]] if l == 0 else n_pre) - lo
                for i in range(lo, lo + n_l):
                    slab(i)
                    if i == index[("k", l, 0)] - 1:
                        sp.wait_ge(sem("tails_packed"), l + 1)
                        for r in range(2):
                            load(hst[r * HD:(r + 1) * HD, :, :],
                                 A["state_ssm"][l].rearrange("b (t r) p n -> r p (b t) n", r=2)[r], "state_landed")
                            load(gst[r * HD:(r + 1) * HD, :, :],
                                 A["state_gdn"][l].rearrange("b (t r) p n -> r p (b t) n", r=2)[r], "state_landed")
                    if i == index[("k", l, 0)]:
                        sp.wait_ge(sem("phase2"), l + 1)
                        for b in range(NS):
                            for g in range(PAGES):
                                q = b * SC + g * (PAGE // SP_)
                                load(lf[q:q + PAGE // SP_, :, :],
                                     A["cache_fox_logf"][l].rearrange("n (c s) h -> n c s h", s=SP_)[
                                         bass.ds(page[b * PAGES + g], 1)].rearrange("o c s h -> (o c) s h"),
                                     "lf_landed")

            with sp.Fori(0, NE) as e:
                for i, (kind, c) in enumerate(E_SLABS):
                    s = e_slot[i]
                    if i >= NSLOT:
                        sp.wait_ge(tile_done, e * E_TICKS + (ticks_pre + e_ticks[i - NSLOT]))
                    else:
                        prev = max(j for j in range(len(E_SLABS)) if e_slot[j] == s)
                        sp.wait_ge(tile_done, e * E_TICKS + (ticks_pre - E_TICKS + e_ticks[prev]))
                    if kind == "gu":
                        for n, name in enumerate(("moe_w_gate", "moe_w_up")):
                            sp.dma_start(ring[s][:, n * 2048:(n + 1) * 2048].rearrange("p (k n) -> p k n", k=KD),
                                         A[name][0][bass.ds(e, 1)].rearrange("o (k p) n -> p (o k) n", p=P)[
                                             :, :, c * 256:c * 256 + 256]).then_inc(landed[s], 16)
                    else:
                        kt = FE // P
                        sp.dma_start(ring[s][:, 0:kt * 256].rearrange("p (k n) -> p k n", k=kt),
                                     A["moe_w_down"][0][bass.ds(e, 1)].rearrange("o (k p) n -> p (o k) n", p=P)[
                                         :, :, c * 256:c * 256 + 256]).then_inc(landed[s], 16)

        @block.tensor
        def _(pe):
            o = Order(pe, "pe_chain")
            mm = pe.matmul
            owner, drains = {}, {}

            def fill(b, drained):
                if b in owner:
                    pe.wait_ge(*owner[b])
                drains[drained] = drains.get(drained, 0) + 1
                owner[b] = (sem(drained), drains[drained])
                return bank[b]

            def tp(out, in_, last=None):
                k = in_.shape[0]
                ins = pe.transpose(out, in_, C("ident")[0:k, 0:k])
                if last:
                    ins.then_inc(sem(last), 1)

            tiles = [0]

            def tick(ins):
                ins.then_inc(tile_done, 1)
                tiles[0] += 1

            def use(i):
                pe.wait_ge(landed[slot_of[i]], landed_at[i])
                assert tiles[0] == ticks_before(i), (plan[i], tiles[0], ticks_before(i))
                return ring[slot_of[i]]

            def start_c():
                pe.wait_ge(sem("c_landed"), 48)
                o.need("c_silu")
                b = fill(2, "c_copied")
                for k in range(KD):
                    tp(b[:, k * 9:k * 9 + 9], cstage[0:9, k * P:(k + 1) * P], "turned" if k == KD - 1 else None)

            def start():
                pe.wait_ge(sem("start_landed"), 16 * STARTS)
                tp(fill(7, "params_used")[:, 0:P], prow1[:, :], "params_turned")
                for k in range(KD):
                    b = fill(3 + k % 4, f"x_copied{k % 2}")
                    for g in range(NG):
                        tp(b[:, g * P:(g + 1) * P], stage[:, g, k * P:(k + 1) * P])
                    tp(b[:, SEQ:NT], stage[0:NS, 2, k * P:(k + 1) * P], "x_turned")
                pe.wait_ge(sem("params_landed"), 16 * PARAMS)
                tp(fill(2, "params_used")[:, 0:102], prow2[0:102, :], "params_turned")

            def ada_unit(l, c, half):
                w = ring[slot_of[index[("ada", l, c)]]][:, :].rearrange("p (k n) -> p k n", k=KD)
                if half == 0:
                    use(index[("ada", l, c)])
                b = fill(0, "mod_rows") if half == 0 else bank[0]
                for k in range(4 * half, 4 * half + 4):
                    ins = mm(b[0:9, :], cT[:, k, :], w[:, k, :], start=k == 0, stop=k == KD - 1)
                if half:
                    tick(ins)

            def ada_turn(l, c):
                o.need("mod_rows")
                b = fill(1, "mod_ready")
                rows_ = ring[slot_of[index[("ada", l, c)]]]
                for m in range(4):
                    ins = pe.transpose(b[:, m * 9:m * 9 + 9], rows_[0:9, m * P:(m + 1) * P], C("ident")[0:9, 0:9])
                tick(ins)

            def ada_fill(l, place):
                for i in ada_units(l, place):
                    if i % 2 == 0 and i:
                        ada_turn(*MIXER_ADA[l][i // 2 - 1])
                    ada_unit(*MIXER_ADA[l][i // 2], i % 2)

            def norm():
                o.need("squares")
                b = fill(0, "rms_read")
                for k in range(KD):
                    ins = mm(b[:, 0:NT], C("ones"), hT[:, k, :], start=k == 0, stop=k == KD - 1)
                ins.then_inc(sem("rms_summed"), 1)
                o.need("h_ready")

            def small(l):
                if l == 0:
                    pe.wait_ge(sem("small_landed"), 16 * (6 + 5 + 4 + 1))
                b = fill(1, "small_copied")
                for g in range(3):
                    n = CH if g < 2 else NS
                    for k in range(KD):
                        ins = mm(b[0:n, g * 16:g * 16 + 16], hT[:, k, g * CH:g * CH + n], w_small[:, l, k, :],
                                 start=k == 0, stop=k == KD - 1)
                ins.then_inc(sem("small_done"), 1)

            def conv_rows(l):
                pe.wait_ge(sem("convrow_landed"), 32 * (l + 1))
                b = fill(2, "convrow_used")
                for i in range(10):
                    tp(b[:, i * 24:i * 24 + 24], convrow[0:24, i * P:(i + 1) * P], "convrow_turned" if i == 9 else None)

            def sums(l):
                o.need("cin_ready")
                b = fill(3, "cum_ready")
                for g in range(NG):
                    mm(b[:, g * 12:g * 12 + 4], C("upper"), cin[:, g, 0:4], start=True, stop=True)
                    mm(b[:, g * 12 + 8:g * 12 + 12], C("upper"), cin[:, g, 8:12], start=True, stop=True)
                    ins = mm(b[:, g * 12 + 4:g * 12 + 8], C("upper"), cin[:, g, 4:8], start=True, stop=g == 0)
                    if g:
                        ins = mm(b[:, g * 12 + 4:g * 12 + 8], C("ones"), cin[:, 0, 4:8], start=False, stop=True)
                ins.then_inc(sem("cum_summed"), 1)

            def spread(col, g):
                return cin[:, g, col:col + 1].broadcast_to([P, P])

            def rows_fox():
                for g in range(NG):
                    b = fill(4 + g, "rows_copied")
                    for h in range(H):
                        ins = mm(b[:, h * CH:(h + 1) * CH], spread(4 + h, g), C("upper"), start=True, stop=g == 0)
                        if g:
                            ins = mm(b[:, h * CH:(h + 1) * CH], spread(4 + h, 0), C("ones"), start=False, stop=True)
                    ins.then_inc(sem("rows_done"), 1)

            def rows(col, b0, done, copied):
                for g in range(NG):
                    b = fill(b0 + g, copied)
                    for h in range(H):
                        ins = mm(b[:, h * CH:(h + 1) * CH], spread(col + h, g), C("upper"), start=True, stop=True)
                    ins.then_inc(sem(done), 1)

            def project(l, slabs):
                for s in slabs:
                    w = use(index[("in", l) + s])[:, 0:KD * s[1]].rearrange("p (k n) -> p k n", k=KD)
                    for m in range(s[1] // P):
                        b = fill(tiles[0] % 2, "tile_copied")
                        for k in range(KD):
                            ins = mm(b[:, 0:NT], w[:, k, m * P:(m + 1) * P], hT[:, k, :], start=k == 0,
                                     stop=k == KD - 1)
                        tick(ins)

            def head_norms(n, src_ready, copied, done):
                o.need(src_ready)
                for i in range(n):
                    b = fill(2 + i, copied)
                    mm(b[:, 0:NT], C("blk"), sq[:, i, :], start=True, stop=True).then_inc(sem(done), 1)

            def tails():
                o.need("tails_packed")
                for c in range(3):
                    b = fill(2 + c, "tail_copied")
                    n = min(4, 10 - 4 * c)
                    for i in range(n):
                        tp(b[0:27, i * P:(i + 1) * P], tail[:, 4 * c + i, :], "turned" if i == n - 1 else None)

            def gdn_scores():
                o.need("gdn_normed")
                for g in range(NG):
                    for r in range(2):
                        b = fill(2 + 2 * g + r, "gdn_scaled")
                        q = slice(r * HD, (r + 1) * HD)
                        for j, first in enumerate((2, 0)):
                            for t in range(2):
                                ins = mm(b[:, (2 * j + t) * CH:(2 * j + t + 1) * CH],
                                         act[q, 2 + t, g * CH:(g + 1) * CH],
                                         act[q, first + t, g * CH:(g + 1) * CH], start=True, stop=True)
                        ins.then_inc(sem("gdn_scored"), 1)

            def gdn_beta_rows():
                for g in range(NG):
                    b = fill(6 + g, "AT_beta")
                    for h in range(H):
                        ins = mm(b[:, h * CH:(h + 1) * CH], beta[:, g, h:h + 1].broadcast_to([P, P]), C("ident"),
                                 start=True, stop=True)
                    ins.then_inc(sem("beta_rows"), 1)

            def gdn_turn():
                for g in range(NG):
                    b = fill(6 + g, "kvt_copied")
                    for i in range(4):
                        tp(b[:, i * P:(i + 1) * P], act[:, 2 + i, g * CH:(g + 1) * CH], "turned" if i == 3 else None)

            def gdn_invert():
                for n, s in enumerate(LEVELS):
                    for g in range(NG):
                        o.need("X_ready")
                        if n == 0:
                            drains["X_ready"] = drains.get("X_ready", 0) + 1
                        b = fill(2 + g, "Q_ready")
                        for h in range(H):
                            ins = mm(b[:, h * CH:(h + 1) * CH], AT[:, g * H + h, :], X[:, g * H + h, :], start=True,
                                     stop=True)
                        ins.then_inc(sem("Q_done"), 1)
                    for g in range(NG):
                        o.need("Q_ready")
                        if n < len(LEVELS) - 1:
                            b = fill(4 + g, "X_ready")
                            for h in range(H):
                                ins = mm(b[:, h * CH:(h + 1) * CH], XT[:, g * H + h, :], Qs[:, g * H + h, :],
                                         start=True, stop=True)
                            ins.then_inc(sem("XQ_done"), 1)
                        b = fill(6 + g, "XT_ready")
                        for h in range(H):
                            ins = mm(b[:, h * CH:(h + 1) * CH], Qs[:, g * H + h, :], XT[:, g * H + h, :], start=True,
                                     stop=True)
                        ins.then_inc(sem("QX_done"), 1)

            def gdn_chain(l):
                for g in range(NG):
                    o.need("R_ready")
                    pe.wait_ge(sem("XT_ready"), 2 * len(LEVELS) * l + 2 * len(LEVELS) - 1 + g)
                    b = fill(2, "wkT_ready")
                    for t in range(2):
                        for r in range(2):
                            h = 2 * t + r
                            ins = mm(b[r * HD:(r + 1) * HD, t * CH:(t + 1) * CH], Rk[:, g * H + h, :],
                                     XT[:, g * H + h, :], start=True, stop=True)
                    ins.then_inc(sem("wkT_done"), 1)
                    o.need("wkT_ready")
                    if g:
                        pe.wait_ge(sem("S_ready"), 2 * l + 1)
                    for r in range(2):
                        b = fill(4 + r, "w_ready")
                        for t in range(2):
                            h = 2 * t + r
                            ins = mm(b[:, t * HD:(t + 1) * HD], XT[:, g * H + h, :], Rv[:, g * H + h, :], start=True,
                                     stop=g == 0)
                            if g:
                                q = slice(r * HD, (r + 1) * HD)
                                ins = mm(b[:, t * HD:(t + 1) * HD], wkT[q, t, :], S0[q, t, :], start=False, stop=True)
                        ins.then_inc(sem("w_done"), 1)
                    o.need("w_ready", 2)
                    b = fill(3, "oT_ready")
                    for t in range(2):
                        for r in range(2):
                            h = 2 * t + r
                            q = slice(r * HD, (r + 1) * HD)
                            ins = mm(b[q, t * CH:(t + 1) * CH], wtok[:, h, :], decG[:, g * H + h, :], start=True,
                                     stop=g == 0)
                            if g:
                                ins = mm(b[q, t * CH:(t + 1) * CH], S0[q, t, :], qh[q, t, :], start=False, stop=True)
                    ins.then_inc(sem("oT_done"), 1)
                    b = fill(6, "S_ready")
                    for t in range(2):
                        for r in range(2):
                            h = 2 * t + r
                            ins = mm(b[r * HD:(r + 1) * HD, t * HD:(t + 1) * HD], ktail[:, g * H + h, :], wtok[:, h, :],
                                     start=True, stop=True)
                    ins.then_inc(sem("S_done"), 1)

            def ssd(l):
                for g in range(NG):
                    G = slice(g * CH, (g + 1) * CH)
                    for t in range(2):
                        q = slice(t * HD, (t + 1) * HD)
                        b = fill(2 + t, "MT_ready")
                        mm(b[:, 0:CH], act[q, 8, G], act[q, 9, G], start=True, stop=True).then_inc(sem("ssd_scored"), 1)
                    b = fill(4, "xt_copied")
                    for i in range(3):
                        tp(b[:, i * P:(i + 1) * P], act[:, 6 + i, G], "turned" if i == 2 else None)
                    if g == 0:
                        ada_fill(l, "ssd")
                    o.need("MT_ready", 2)
                    o.need("xw_ready")
                    if g:
                        o.need("Cg_ready")
                        pe.wait_ge(sem("hs_ready"), 2 * l + 1)
                    for t in range(2):
                        b = fill(5 + t, "yA_copied")
                        for r in range(2):
                            q = slice(t * HD, (t + 1) * HD)
                            ins = mm(b[r * HD:(r + 1) * HD, 0:CH], xdt[:, 2 * t + r, :], MT[:, g * H + 2 * t + r, :],
                                     start=True, stop=g == 0)
                            if g:
                                ins = mm(b[r * HD:(r + 1) * HD, 0:CH], hs0[q, r, :], Cg[q, r, :], start=False,
                                         stop=True)
                        ins.then_inc(sem("yA_done"), 1)
                    b = fill(7, "hs_ready")
                    for t in range(2):
                        ins = mm(b[t * HD:(t + 1) * HD, 0:P], xt[:, 2, t * HD:(t + 1) * HD],
                                 xw[:, 2 * t:2 * t + 2, :], start=True, stop=True)
                    ins.then_inc(sem("hs_done"), 1)
                o.need("hs_ready", 2)
                tp(fill(4, "hsout_copied")[:, 0:P], hs1[:, :, :], "turned")

            def kv_turn():
                for i in range(4):
                    b = fill(2 + i, "kvp_copied")
                    for g in range(NG):
                        for t in range(2):
                            tp(b[:, g * GW + t * P:g * GW + (t + 1) * P], fm[:, 4 + 2 * i + t, g * CH:(g + 1) * CH],
                               "turned" if g == 1 and t == 1 else None)
                for i in range(3):
                    b = fill(6 + i % 2, "stok_copied")
                    for j in range(4):
                        tp(b[0:NS, j * P:(j + 1) * P], fm[:, 4 * i + j, SEQ:NT], "turned" if j == 3 else None)

            def attention(l):
                o.need("kvp_copied", 4)
                for n in range(8):
                    m, t, r = n // 4, (n % 4) // 2, n % 2
                    q = slice(r * HD, (r + 1) * HD)
                    b = fill(2 + n % 2, "s_read")
                    qq, kk = fm[q, 2 * m + t, :], fm[q, 4 + 2 * m + t, :]
                    mm(b[:, 0:CH], qq[:, 0:CH], kk[:, 0:CH], start=True, stop=True)
                    mm(b[:, CH:3 * CH], qq[:, CH:SEQ], kk[:, 0:SEQ], start=True, stop=True).then_inc(sem("s_done"), 1)
                    ada_fill(l, f"att{n}")
                    if n:
                        attend(n - 1)
                ada_fill(l, "att8")
                attend(7)

            def attend(n):
                m, t, r = n // 4, (n % 4) // 2, n % 2
                o.need("P_ready")
                b = fill(4 + n % 2, "PT_copied")
                for i in range(3):
                    tp(b[:, i * CH:(i + 1) * CH], s3[:, n % 2, i * CH:(i + 1) * CH], "PT_turned" if i == 2 else None)
                o.need("PT_copied")
                b = fill(6 + (n // 2) % 2, "yBD_copied") if r == 0 else bank[6 + (n // 2) % 2]
                q = slice(r * HD, (r + 1) * HD)
                h = 2 * t + r

                def v(g):
                    return kvp[:, (2 + m) * NG + g, h * HD:(h + 1) * HD]
                mm(b[q, 0:CH], v(0), PT[:, n % 2, 0:CH], start=True, stop=True)
                mm(b[q, CH:SEQ], v(0), PT[:, n % 2, CH:2 * CH], start=True, stop=False)
                ins = mm(b[q, CH:SEQ], v(1), PT[:, n % 2, 2 * CH:3 * CH], start=False, stop=True)
                if r:
                    ins.then_inc(sem("yBD_done"), 1)

            def decode_spread():
                for i in range(4):
                    tp(bank[2][0:NS, i * P:(i + 1) * P] if i else fill(2, "dtok_copied")[0:NS, 0:P],
                       act[:, (8, 9, 4, 5)[i], SEQ:NT], "turned" if i == 3 else None)
                o.need("stq_ready")
                b = fill(3, "fmj_copied")
                for j in range(8):
                    for r in range(2):
                        ins = mm(b[r * HD:(r + 1) * HD, j * NS:(j + 1) * NS],
                                 stq[0:NS, 2 * j + r:2 * j + r + 1].broadcast_to([NS, HD]),
                                 C("ident")[0:NS, 0:NS], start=True, stop=True)
                ins.then_inc(sem("fmj_done"), 1)

            def decode_ssd():
                o.need("dtok_copied")
                for j in range(4):
                    b = fill(4 + j % 2, "hst_step")
                    for i in range(2):
                        ins = mm(b[:, i * 256:(i + 1) * 256],
                                 C("one_row")[0:NS, (2 * j + i) * P:(2 * j + i + 1) * P], dtok[0:NS, 0:2, :],
                                 start=True, stop=True)
                    ins.then_inc(sem("bc_rows"), 1)

            def decode_gdn(l):
                vt = dtok[0:NS, 2:4, :]
                for j in range(2):
                    b = fill(6 + j, "v_copied")
                    for i in range(4):
                        for r in range(2):
                            ins = mm(b[r * HD:(r + 1) * HD, i * P:(i + 1) * P],
                                     C("one_row")[0:NS, (4 * j + i) * P:(4 * j + i) * P + HD],
                                     vt[:, :, r * HD:(r + 1) * HD], start=True, stop=True)
                    ins.then_inc(sem("v_rows"), 1)
                ada_fill(l, "v_rows")
                o.need("Sk_ready")
                for j in range(2):
                    b = fill(2 + j, "ks_read")
                    mm(b[:, :], C("blk"), tmpB[:, 8 * j:8 * j + 8, :], start=True, stop=True).then_inc(sem("ks_done"), 1)
                ada_fill(l, "ks")
                o.need("gst_ready")
                b = fill(4, "oTs_copied")
                for t in range(2):
                    for r in range(2):
                        q = slice(r * HD, (r + 1) * HD)
                        for i in range(NS):
                            ins = mm(b[q, t * NS + i:t * NS + i + 1], gst[q, 2 * i + t, :],
                                     act[q, t, SEQ + i:SEQ + i + 1], start=True, stop=True)
                ins.then_inc(sem("oTs_done"), 1)

            def decode_attention(l):
                o.need("stok_copied", 3)
                b = fill(2, "qbc_copied")
                mm(b[:, :], C("own_row")[0:NS, :], stok[0:NS, 0:2, :], start=True, stop=True).then_inc(sem("qbc_done"), 1)
                o.need("lf_ready")
                b = fill(3, "bias_added")
                mm(b[:, 0:H], C("later"), lf[:, 0, :], start=True, stop=False)
                mm(b[:, 0:H], C("own_row")[0:NS, :], nlf[0:NS, 2, :], start=False, stop=True).then_inc(sem("bias_done"), 1)
                ada_fill(l, "keys")
                ada_turn(*MIXER_ADA[l][-1])
                o.need("max_ready")
                b = fill(4, "mcol_ready")
                tp(b[0:8, 0:P], mcol[:, :])
                tp(b[0:8, P:P + NS], sself[0:NS, :], "max_turned")
                o.need("mcol_ready")
                tp(fill(5, "mtok_copied")[0:NS, 0:8], ms8[0:8, 0:NS], "m_turned")
                o.need("mtok_copied")
                b = fill(6, "m_spread_read")
                mm(b[:, 0:8], C("own_row")[0:NS, :], mtok[0:NS, :], start=True, stop=True).then_inc(sem("m_spread"), 1)
                o.need("psums_ready")
                b = fill(7, "rden_ready")
                mm(b[0:NS, 0:8], C("own_col"), psums[:, :], start=True, stop=True).then_inc(sem("den_done"), 1)
                o.need("rden_ready")
                b = fill(2, "Pd_scaled")
                mm(b[:, 0:8], C("own_row")[0:NS, :], rden[0:NS, :], start=True, stop=True).then_inc(sem("rden_spread"), 1)
                b = fill(3, "psb_copied")
                for j in range(4):
                    for r in range(2):
                        ins = mm(b[r * HD:(r + 1) * HD, j * NS:(j + 1) * NS],
                                 sself[0:NS, 2 * j + r:2 * j + r + 1].broadcast_to([NS, HD]),
                                 C("ident")[0:NS, 0:NS], start=True, stop=True)
                ins.then_inc(sem("psb_done"), 1)
                o.need("Pd_ready")
                b = fill(4, "yd_read")
                for m in range(2):
                    w = use(index[("v", l, m)])[:, :].rearrange("p (s f) -> p s f", s=SP_)
                    for t in range(2):
                        for s in range(SP_):
                            ins = mm(b[:, (2 * m + t) * 16:(2 * m + t + 1) * 16], w[:, s, t * P:(t + 1) * P],
                                     Pd[:, m * SP_ + s, :].rearrange("p (b h) -> p b h", b=NS)[:, :, 2 * t:2 * t + 2],
                                     start=s == 0, stop=s == SP_ - 1)
                    tick(ins)

            def norm2(src, b0, ready, read, done):
                o.need(ready)
                b = fill(b0, read)
                for i in range(2):
                    ins = mm(b[:, 0:NT], C("ones"), sq[:, i, :], start=i == 0, stop=i == 1)
                ins.then_inc(sem(done), 1)

            def w_out(l):
                o.need("yT_ready")
                for c in range(2):
                    w = use(index[("out", l, c)])[:, :].rearrange("p (k n) -> p k n", k=KD)
                    for m in range(4):
                        b = fill(m, "x_added")
                        for k in range(KD):
                            ins = mm(b[:, 0:NT], w[:, k, m * P:(m + 1) * P], yT[:, k, :], start=k == 0, stop=k == KD - 1)
                        tick(ins)

            def gate_up(w, f, wait_pair):
                w = w[:, :].rearrange("p (z k n) -> p z k n", z=2, k=KD)
                wait_pair()
                for z in range(2):
                    for k in range(KD):
                        ins = mm(bank[2 * f + z][:, 0:NT], w[:, z, k, f * P:(f + 1) * P], hT[:, k, :], start=k == 0,
                                 stop=k == KD - 1)
                    ins.then_inc(tile_done, 1)

            def dense():
                for c in range(FF // 256):
                    w = use(index[("gu", 0, c)])
                    for f in range(2):
                        def wait_pair():
                            if c:
                                pe.wait_ge(sem("hid_ready"), 2 * c + f - 1)
                            else:
                                for z in range(2):
                                    pe.wait_ge(*owner[2 * f + z])
                        gate_up(w, f, wait_pair)
                    tiles[0] += 4
                pe.wait_ge(sem("hid_ready"), FF // P)
                kt = FF // P // 2
                for c in range(4):
                    for half in range(2):
                        w = use(index[("down", 0, c, half)])[:, 0:kt * 256].rearrange("p (k n) -> p k n", k=kt)
                        for m in range(2):
                            b = fill(4 + (2 * c + m) % 4, "acc_ready") if half == 0 else bank[4 + (2 * c + m) % 4]
                            for k in range(kt):
                                ins = mm(b[:, 0:NT], w[:, k, m * P:(m + 1) * P], hid[:, half * kt + k, :],
                                         start=half == 0 and k == 0, stop=half == 1 and k == kt - 1)
                            if half or m:
                                tick(ins)
                for z in range(4):
                    owner[z] = (sem("hid_ready"), FF // P)

            def route():
                b = fill(0, "gates_ready")
                for g in range(3):
                    n = CH if g < 2 else NS
                    for k in range(KD):
                        ins = mm(b[0:n, g * NE:(g + 1) * NE], hT[:, k, g * CH:g * CH + n], router[:, k, :],
                                 start=k == 0, stop=k == KD - 1)
                ins.then_inc(sem("lg_done"), 1)
                o.need("gates_ready")
                for e in range(NE):
                    b = fill(e % 4, "gbc_copied")
                    for g in range(3):
                        n = CH if g < 2 else NS
                        ins = mm(b[:, g * CH:g * CH + n], gates[0:n, g, e:e + 1].broadcast_to([n, P]),
                                 C("ident")[0:n, 0:n], start=True, stop=True)
                    ins.then_inc(sem("gbc_done"), 1)
                pe.wait_ge(sem("gbc_copied"), NE)

            def experts():
                base = [slot_count[s] for s in range(NSLOT)]
                hid0, acc0 = FF // P, KD
                for z in range(4, 8):
                    pe.wait_ge(*owner[z])
                with pe.Fori(0, NE) as e:
                    for i, (kind, c) in enumerate(E_SLABS):
                        s = e_slot[i]
                        pe.wait_ge(landed[s], e * per_slot[s] + (base[s] + e_landed[i]))
                        if kind == "gu":
                            for f in range(2):
                                gate_up(ring[s], f, lambda: pe.wait_ge(
                                    sem("hid_ready"), e * (FE // P) + (hid0 + 2 * c + f - 1)))
                        else:
                            kt = FE // P
                            if c == 0:
                                pe.wait_ge(sem("hid_ready"), e * kt + (hid0 + kt))
                            w = ring[s][:, 0:kt * 256].rearrange("p (k n) -> p k n", k=kt)
                            for m in range(2):
                                j = 2 * c + m
                                pe.wait_ge(sem("acc_ready"), e * KD + (acc0 + j - 3))
                                for k in range(kt):
                                    ins = mm(bank[4 + j % 4][:, 0:NT], w[:, k, m * P:(m + 1) * P], hid[:, k, :],
                                             start=k == 0, stop=k == kt - 1)
                                ins.then_inc(tile_done, 1)

            def finish():
                o.need("x_final")
                for g in range(3):
                    n = CH if g < 2 else NS
                    for half in range(2):
                        b = fill((2 * g + half) % 4, "out_copied")
                        for k in range(4):
                            tp(b[0:n, k * P:(k + 1) * P], xT[:, 4 * half + k, g * CH:g * CH + n],
                               "out_turned" if k == 3 else None)

            start_c()
            o.need("c_copied")
            for c in range(MIX_CHUNKS):
                if c == 2:
                    start()
                for half in range(2):
                    ada_unit(0, c, half)
                ada_turn(0, c)
            for l in range(DEPTH):
                norm()
                small(l)
                conv_rows(l)
                project(l, G_SLABS)
                sums(l)
                rows_fox()
                head_norms(4, "head_squares", "head_ss_read", "head_ss")
                project(l, S_SLABS)
                tails()
                project(l, F_SLABS)
                head_norms(4, "head_squares", "head_ss_read", "head_ss")
                project(l, M_SLABS)
                head_norms(4, "head_squares", "head_ss_read", "head_ss")
                rows(8, 6, "rows_done", "rows_copied")
                ada_fill(l, "gdn")
                gdn_scores()
                gdn_beta_rows()
                gdn_turn()
                gdn_invert()
                gdn_chain(l)
                rows(0, 6, "rows_done", "rows_copied")
                ssd(l)
                kv_turn()
                attention(l)
                decode_spread()
                decode_ssd()
                decode_gdn(l)
                decode_attention(l)
                norm2(yA, 5, "head_squares", "head_ss_read", "head_ss")
                head_norms(2, "head_squares", "head_ss_read", "head_ss")
                w_out(l)
                norm()
                if l == 0:
                    dense()
                else:
                    route()
                    experts()
            finish()

        @block.scalar
        def _(act_e):
            o = Order(act_e, "act_chain")
            A_ = act_e.activation

            def copy(out, in_, name=None):
                o.go(A_(out, in_, ACT.Copy), name)

            def rms(src, dst, scale, read, eps=EPS):
                o.go(A_(dst, src, ACT.Ln, bias=epsc[:, 0:1], scale=scale), read)
                o.settle()
                return A_(dst, dst, ACT.Exp, scale=-0.5)

            def mod_rows(l, c):
                i = index[("ada", l, c)]
                act_e.wait_ge(tile_done, ticks_before(i) + 1)
                copy(ring[slot_of[i]][0:9, 0:512], bank[0][0:9, :], "mod_rows")

            def mod_columns(l, c):
                act_e.wait_ge(tile_done, done_at[index[("ada", l, c)]])
                copy(modT[:, 4 * c:4 * c + 4, :], bank[1][:, 0:36].rearrange("p (m j) -> p m j", m=4), "mod_ready")

            def ada_drain(l, place):
                for i in ada_units(l, place):
                    if i % 2 == 0 and i:
                        mod_columns(*MIXER_ADA[l][i // 2 - 1])
                    if i % 2:
                        mod_rows(*MIXER_ADA[l][i // 2])

            act_e.wait_ge(sem("c_landed"), 48)
            o.go(A_(cstage[0:9, :], cstage[0:9, :], ACT.Silu), "c_silu")
            o.need("turned")
            copy(cT[:, :, :], bank[2][:, 0:72].rearrange("p (k n) -> p k n", k=KD), "c_copied")
            for c in range(MIX_CHUNKS):
                if c == 2:
                    for k in range(0, KD, 2):
                        act_e.wait_ge(sem("x_turned"), k + 1)
                        copy(xT[:, k, :], bank[3 + k % 4][:, 0:NT], "x_copied0")
                mod_rows(0, c)
                mod_columns(0, c)
            act_e.wait_ge(sem("small_landed"), 256)
            o.go(A_(nega[:, :, :], alog[:, :, :], ACT.Exp), "nega_exp")

            def norm():
                act_e.wait_ge(sem("x_copied1"), 4)
                o.need("x_whole")
                o.go(A_(hT[:, :, :], xT[:, :, :], ACT.Square), "squares")
                o.need("rms_summed")
                o.go(rms(bank[0][:, 0:NT], rstd[:, 0, :], 1.0 / D, "rms_read"), "rstd_ready")

            dst_of = {}
            for l in range(DEPTH):
                order = [("u", i) for i in range(6)] + [("z", 2), ("z", 3), ("z", 0), ("z", 1)]
                order += [("u", i) for i in (6, 7, 8, 9)]
                order += [("f", i) for i in (0, 1, 4, 5, 8, 9)] + [("f", i) for i in (2, 3, 6, 7, 10, 11)]
                dst_of[l] = order

            def drain(l, first, n):
                i0 = ticks_before(index[("in", l) + IN_SLABS[0]])
                for j in range(first, first + n):
                    act_e.wait_ge(tile_done, i0 + j + 1)
                    b = bank[(i0 + j) % 2]
                    kind, i = dst_of[l][j]
                    if kind == "u":
                        o.go(A_(u[:, i, 3:3 + SEQ], b[:, 0:SEQ], ACT.Copy))
                        copy(u[:, i, 3 + SEQ + 3:UW:CW], b[:, SEQ:NT], "tile_copied")
                    elif kind == "z":
                        copy(zz[:, i, :], b[:, 0:NT], "tile_copied")
                    else:
                        copy(fm[:, i, :], b[:, 0:NT], "tile_copied")

            def head_rms(n, done, read, ready, scale):
                for i in range(n):
                    o.need(done)
                    o.go(rms(bank[2 + i][:, 0:NT], rstd[:, i, :], scale, read), ready)

            for l in range(DEPTH):
                norm()
                o.need("sma_ready")
                o.go(A_(sme[:, :, :], sma[:, :, :], ACT.Exp, scale=-1.0))
                o.go(A_(beta[:, :, :], sm[:, :, 8:12], ACT.Exp, scale=-1.0))
                o.settle()
                o.go(A_(sme[:, :, :], sme[:, :, :], ACT.Ln, bias=1.0), "softplus_ln")
                drain(l, 0, 8)
                for g in range(NG):
                    o.need("rows_done")
                    copy(rowF[:, :, g * CH:(g + 1) * CH], bank[4 + g][:, :].rearrange("p (h i) -> p h i", h=H),
                         "rows_copied")
                def silus(first, n):
                    for i in range(first, first + n):
                        o.need("cv_ready")
                        o.go(A_(act[:, i, 0:SEQ], cv[:, i % 2, 0:SEQ], ACT.Silu))
                        o.go(A_(act[:, i, SEQ:NT], cv[:, i % 2, SEQ + 3:CVW:CW], ACT.Silu), "cv_used")
                silus(0, 6)
                o.settle()
                o.go(A_(sq[:, :, :], act[:, 0:4, :], ACT.Square), "head_squares")
                head_rms(4, "head_ss", "head_ss_read", "head_rstd", 1.0)
                drain(l, 8, 6)
                silus(6, 4)
                for c in range(3):
                    o.need("turned")
                    n = min(512, 1280 - 512 * c)
                    copy(convrow[0:27, c * 512:c * 512 + n], bank[2 + c][0:27, 0:n], "tail_copied")
                o.go(A_(zz[:, :, :], zz[:, :, :], ACT.Silu), "zz_ready")
                drain(l, 14, 6)
                o.settle()
                o.need("gdn_normed")
                o.go(A_(sq[:, 0:2, :], fm[:, 0:2, :], ACT.Square))
                o.go(A_(sq[:, 2:4, :], fm[:, 4:6, :], ACT.Square), "head_squares")
                head_rms(4, "head_ss", "head_ss_read", "head_rstd", 1.0 / HD)
                drain(l, 20, 6)
                o.settle()
                o.need("fm_normed")
                o.go(A_(sq[:, 0:2, :], fm[:, 2:4, :], ACT.Square))
                o.go(A_(sq[:, 2:4, :], fm[:, 6:8, :], ACT.Square), "head_squares")
                head_rms(4, "head_ss", "head_ss_read", "head_rstd", 1.0 / HD)

                for g in range(NG):
                    o.need("rows_done")
                    copy(egG[:, g * H:(g + 1) * H, :], bank[6 + g][:, :].rearrange("p (h i) -> p h i", h=H),
                         "rows_copied")
                o.need("decG_diff")
                o.go(A_(decG[:, :, :], decG[:, :, :], ACT.Exp))
                o.go(A_(egG[:, :, :], egG[:, :, :], ACT.Exp))
                o.go(A_(be[:, :, :], cum[:, :, 8:12], ACT.Exp))
                o.go(A_(sc4[:, :, :], sc4[:, :, :], ACT.Exp), "decG_ready")
                ada_drain(l, "gdn")
                for g in range(NG):
                    o.need("turned")
                    copy(kvt[:, g * 4:(g + 1) * 4, :], bank[6 + g][:, :].rearrange("p (i j) -> p i j", i=4),
                         "kvt_copied")
                for g in range(NG):
                    o.need("wkT_done")
                    o.go(A_(wkT[:, :, :], bank[2][:, 0:SEQ].rearrange("p (t i) -> p t i", t=2), ACT.Copy, scale=-1.0),
                         "wkT_ready")
                    for r in range(2):
                        o.need("w_done")
                        copy(wtok[:, r::2, :], bank[4 + r][:, 0:P].rearrange("p (t d) -> p t d", t=2), "w_ready")
                    o.need("oT_done")
                    copy(oT[:, :, g * CH:(g + 1) * CH], bank[3][:, 0:SEQ].rearrange("p (t i) -> p t i", t=2),
                         "oT_ready")

                for g in range(NG):
                    o.need("rows_done")
                    if g == 0:
                        o.need("phase2")
                    copy(egS[:, g * H:(g + 1) * H, :], bank[6 + g][:, :].rearrange("p (h i) -> p h i", h=H),
                         "rows_copied")
                o.need("MT_diff")
                o.go(A_(MT[:, :, :], MT[:, :, :], ACT.Exp))
                o.go(A_(egS[:, :, :], egS[:, :, :], ACT.Exp))
                o.go(A_(ws[:, :, :], ws[:, :, :], ACT.Exp), "decS_ready")
                for g in range(NG):
                    o.need("turned")
                    if g:
                        act_e.wait_ge(sem("hs_ready"), 2 * l + 1)
                    copy(xt[:, :, :], bank[4][:, 0:3 * P].rearrange("p (i j) -> p i j", i=3), "xt_copied")
                    if g == 0:
                        ada_drain(l, "ssd")
                o.need("turned")
                copy(hsout[:, :], bank[4][:, 0:P], "hsout_copied")
                for i in range(4):
                    o.need("turned")
                    copy(kvp[:, i * NG:(i + 1) * NG, :], bank[2 + i][:, :].rearrange("p (g f) -> p g f", g=NG),
                         "kvp_copied")
                for i in range(3):
                    o.need("turned")
                    copy(stok[0:NS, 2 * i:2 * i + 2, :], bank[6 + i % 2][0:NS, :].rearrange("p (a f) -> p a f", a=2),
                         "stok_copied")
                def soften(n):
                    o.need("nmx_ready")
                    o.go(A_(s3[:, n % 2, 0:CH], s3[:, n % 2, 0:CH], ACT.Exp, bias=nmx[:, n, 0:1],
                            accum_out=rsum[:, n, 0:1]))
                    o.go(A_(s3[:, n % 2, CH:], s3[:, n % 2, CH:], ACT.Exp, bias=nmx[:, n, 1:2],
                            accum_out=rsum[:, n, 1:2]), "exp_done")

                def copy_pt(n):
                    o.need("PT_turned")
                    copy(PT[:, n % 2, :], bank[4 + n % 2][:, 0:3 * CH], "PT_copied")
                    if n % 2:
                        o.need("yBD_done")
                        m, t = n // 4, (n % 4) // 2
                        copy(yT[:, (2, 6)[m] + t, 0:SEQ], bank[6 + (n // 2) % 2][:, 0:SEQ], "yBD_copied")
                for n in range(8):
                    soften(n)
                    ada_drain(l, f"att{n}")
                    if n:
                        copy_pt(n - 1)
                ada_drain(l, "att8")
                copy_pt(7)

                o.need("stq_logs")
                o.go(A_(stq[0:NS, 4:12], stq[0:NS, 4:12], ACT.Exp), "stq_ready")
                o.need("turned")
                copy(dtok[0:NS, :, :], bank[2][0:NS, :].rearrange("p (i j) -> p i j", i=4), "dtok_copied")
                o.need("fmj_done")
                copy(fmj[:, :, :], bank[3][:, 0:8 * NS].rearrange("p (j b) -> p j b", j=8), "fmj_copied")
                o.need("tmpA_free")
                for j in range(2):
                    o.need("v_rows")
                    copy(tmpA[:, 8 * j:8 * j + 8, :], bank[6 + j][:, :].rearrange("p (a d) -> p a d", a=8), "v_copied")
                ada_drain(l, "v_rows")
                ada_drain(l, "ks")
                o.need("oTs_done")
                copy(oT[:, :, SEQ:NT], bank[4][:, 0:2 * NS].rearrange("p (t b) -> p t b", t=2), "oTs_copied")
                o.need("qbc_done")
                copy(qbc[:, :, :], bank[2][:, :].rearrange("p (m f) -> p m f", m=2), "qbc_copied")
                ada_drain(l, "keys")
                mod_columns(*MIXER_ADA[l][-1])
                o.need("m_spread_read")
                o.go(A_(scd[:, :, :], scd[:, :, :], ACT.Exp))
                o.go(A_(sself[0:NS, :], sself[0:NS, :], ACT.Exp), "scd_exp")
                o.need("psb_done")
                copy(psb[:, :, :], bank[3][:, 0:4 * NS].rearrange("p (j b) -> p j b", j=4), "psb_copied")

                o.need("yA_gated")
                o.go(A_(sq[:, 0:2, :], yA[:, :, :], ACT.Square), "head_squares")
                o.need("head_ss")
                o.go(rms(bank[5][:, 0:NT], rstd[:, 2, :], 1.0 / GW, "head_ss_read"), "head_rstd")
                o.settle()
                o.go(A_(sq[:, 0:2, :], oT[:, :, :], ACT.Square), "head_squares")
                for i in range(2):
                    o.need("head_ss")
                    o.go(rms(bank[2 + i][:, 0:NT], rstd[:, i, :], 1.0 / HD, "head_ss_read"), "head_rstd")
                norm()
                if l == 0:
                    t0 = ticks_before(index[("gu", 0, 0)])
                    for f in range(FF // P):
                        act_e.wait_ge(tile_done, t0 + 2 * f + 1)
                        if f >= 2:
                            act_e.wait_ge(sem("hid_ready"), f - 1)
                        else:
                            act_e.wait_ge(sem("ffn_phase"), 1)
                        o.go(A_(sg[:, f % 2, :], bank[2 * (f % 2)][:, 0:NT], ACT.Silu), "sg_ready")
                else:
                    act_e.wait_ge(sem("ffn_phase"), 2)
                    o.need("lg_shift")
                    o.go(A_(gates[:, :, :], lg[:, :, :], ACT.Exp), "lg_exp")
                    for e in range(NE):
                        o.need("gbc_done")
                        copy(gbc[:, e, :], bank[e % 4][:, 0:NT], "gbc_copied")
                    with act_e.Fori(0, NE) as e:
                        for f in range(FE // P):
                            act_e.wait_ge(tile_done, e * E_TICKS + (ticks_pre + 2 * f + 1))
                            act_e.wait_ge(sem("hid_ready"), e * (FE // P) + (FF // P + f - 1))
                            A_(sg[:, f % 2, :], bank[2 * (f % 2)][:, 0:NT], ACT.Silu).then_inc(sem("sg_ready"), 1)
            for i in range(6):
                g, half = i // 2, i % 2
                n = CH if g < 2 else NS
                act_e.wait_ge(sem("out_turned"), i + 1)
                if i == 0:
                    act_e.wait_ge(sem("x_final"), 1)
                A_(stage[0:n, g, half * 512:half * 512 + 512], bank[i % 4][0:n, :], ACT.Copy).then_inc(
                    sem("out_copied"), 1)

        @block.vector
        def _(ve):
            o = Order(ve, "ve_chain")
            TT, TS, STT, CP, RED = (ve.tensor_tensor, ve.tensor_scalar, ve.scalar_tensor_tensor, ve.tensor_copy,
                                    ve.tensor_reduce)

            def v(ins, name=None):
                o.go(ins, name)

            def vs(ins, name=None):
                o.go(ins, name)
                o.settle()

            vs(ve.memset(epsc[:, :], EPS))
            vs(ve.memset(brow[:, :, 8:12], 0.0))
            ve.wait_ge(sem("start_landed"), 16 * STARTS)
            o.need("params_turned", 1)
            v(CP(prm1[:, :], bank[7][:, 0:P]), "params_used")
            for k in range(1, KD, 2):
                ve.wait_ge(sem("x_turned"), k + 1)
                v(CP(xT[:, k, :], bank[3 + k % 4][:, 0:NT]), "x_copied1")
            o.need("params_turned", 1)
            v(CP(prm2[:, :], bank[2][:, 0:102]), "params_used")
            ve.wait_ge(sem("small_landed"), 256)
            o.need("nega_exp")
            vs(TS(nega[:, :, :], nega[:, :, :], -1.0, None, ALU.mult))
            ve.wait_ge(sem("x_copied0"), 4)
            vs(ve.memset(sq[:, 0, 0:1], 0.0), "x_whole")

            def col(m, part=slice(0, P)):
                return modT[part, m, 0:1]

            def modulate(first_shift, gains):
                v(STT(gain1[:, :, :], modT[:, first_shift + 8:first_shift + 16, :], 1.0,
                      gains.unsqueeze(2).broadcast_to([P, KD, 9]), ALU.add, ALU.mult))
                o.need("rstd_ready")
                vs(TT(hT[:, :, :], xT[:, :, :], rstd[:, 0:1, :].broadcast_to([P, KD, NT]), ALU.mult))
                for k in range(KD):
                    v(TS(hT[:, k, 0:SEQ], hT[:, k, 0:SEQ], gain1[:, k, 0:1], modT[:, first_shift + k, 0:1],
                         ALU.mult, ALU.add))
                vs(TT(hT[:, :, SEQ:NT], hT[:, :, SEQ:NT], gain1[:, :, 1:9], ALU.mult))
                v(TT(hT[:, :, SEQ:NT], hT[:, :, SEQ:NT], modT[:, first_shift:first_shift + KD, 1:9], ALU.add),
                  "h_ready")

            def add_bias(l, lo, hi):
                ve.wait_ge(sem("mod_ready"), hi // 4 + ADA_CHUNKS * l)
                vs(TT(modT[:, lo:hi, :], modT[:, lo:hi, :],
                      prm1[:, 48 * l + lo:48 * l + hi].unsqueeze(2).broadcast_to([P, hi - lo, 9]), ALU.add))

            def convolve(l, first, n, w0, wn, bias):
                p0 = 46 * l
                for i in range(first, first + n):
                    j = i - first
                    if not (l == 0 and i < 2):
                        o.need("cv_used")
                    c = cv[:, i % 2, :]
                    w = [prm2[:, p0 + w0 + wn * k + j:p0 + w0 + wn * k + j + 1] for k in range(CW)]
                    if bias is None:
                        vs(TS(c, u[:, i, 0:CVW], w[0], None, ALU.mult))
                    else:
                        vs(TS(c, u[:, i, 0:CVW], w[0], prm2[:, p0 + bias + j:p0 + bias + j + 1], ALU.mult, ALU.add))
                    for k in range(1, CW):
                        if k < CW - 1:
                            vs(STT(c, u[:, i, k:k + CVW], w[k], c, ALU.mult, ALU.add))
                        else:
                            v(STT(c, u[:, i, k:k + CVW], w[k], c, ALU.mult, ALU.add), "cv_ready")

            def qk_norm(tiles, gains, name):
                for j, i in enumerate(tiles):
                    o.need("head_rstd")
                    v(STT(fm[:, i, :], fm[:, i, :], gains[j], rstd[:, j, :], ALU.mult, ALU.mult), name if j == 3 else None)

            for l in range(DEPTH):
                heads = 92 + 5 * l
                add_bias(l, 0, 4 * MIX_CHUNKS)
                if l == 0:
                    for ll in range(DEPTH):
                        v(TS(prm2[:, 92 + 5 * ll:94 + 5 * ll], prm2[:, 92 + 5 * ll:94 + 5 * ll], HD ** -0.5, None,
                             ALU.mult))
                modulate(0, prm1[:, 96 + 8 * l:104 + 8 * l])
                if l == 0:
                    v(ve.memset(u[:, :, 0:3], 0.0))
                    v(ve.memset(sm[:, 2, :], 0.0))
                else:
                    ve.wait_ge(sem("stored"), 16 * STORES)
                    v(ve.memset(u[:, :, 0:3], 0.0))
                    v(ve.memset(sm[:, 2, :], 0.0))
                o.need("small_done")
                o.settle()
                v(CP(sm[:, 0:2, :], bank[1][:, 0:32].rearrange("p (g c) -> p g c", g=2)))
                vs(CP(sm[0:NS, 2, :], bank[1][0:NS, 32:48]), "small_copied")
                vs(TT(sm[:, :, :], sm[:, :, :], brow[:, l, :].unsqueeze(1).broadcast_to([P, 3, 16]), ALU.add))
                vs(TS(sm[:, :, 4:8], sm[:, :, 4:8], -1.0, None, ALU.mult))
                vs(STT(sma[:, :, :], sm[:, :, :], -1.0, sm[:, :, :], ALU.mult, ALU.max), "sma_ready")
                o.need("softplus_ln")
                vs(STT(smp[:, :, :], sm[:, :, :], 0.0, sme[:, :, :], ALU.max, ALU.add))
                vs(TS(beta[:, :, :], beta[:, :, :], 1.0, None, ALU.add))
                v(ve.reciprocal(beta[:, :, :], beta[:, :, :]))
                v(TT(cin[:, :, 0:4], smp[:, :, 0:4], nega[:, l, 0:4].unsqueeze(1).broadcast_to([P, 3, 4]), ALU.mult))
                v(TT(cin[:, :, 8:12], smp[:, :, 12:16], nega[:, l, 4:8].unsqueeze(1).broadcast_to([P, 3, 4]), ALU.mult))
                v(TS(nlf[:, :, :], smp[:, :, 4:8], -1.0, None, ALU.mult))
                v(CP(cin[:, :, 4:8], smp[:, :, 4:8]), "cin_ready")
                o.need("convrow_turned")
                v(CP(u[:, :, 3 + SEQ:UW].rearrange("p i (b k) -> p i b k", k=CW)[:, :, :, 0:3],
                     bank[2][:, 0:240].rearrange("p (i b k) -> p i b k", i=10, k=3)), "convrow_used")
                ve.wait_ge(sem("tile_copied"), 26 * l + 6)
                o.settle()
                convolve(l, 0, 6, 22, 6, None)
                o.need("cum_summed")
                v(CP(cum[:, :, :], bank[3][:, 0:24].rearrange("p (g c) -> p g c", g=NG)), "cum_ready")
                for i in range(4):
                    o.need("head_rstd")
                    if i < 2:
                        v(STT(act[:, i, :], act[:, i, :], HD ** -0.5, rstd[:, i, :], ALU.mult, ALU.mult))
                    else:
                        v(TT(act[:, i, :], act[:, i, :], rstd[:, i, :], ALU.mult),
                          "gdn_normed" if i == 3 else None)
                ve.wait_ge(sem("tile_copied"), 26 * l + 14)
                convolve(l, 6, 4, 2, 4, 18)
                v(CP(tail[:, :, 0:3], u[:, :, SEQ:SEQ + 3]))
                v(CP(tail[:, :, 3:27].rearrange("p i (b k) -> p i b k", k=3),
                     u[:, :, 3 + SEQ:UW].rearrange("p i (b k) -> p i b k", k=CW)[:, :, :, 1:4]), "tails_packed")
                g_ = [prm2[:, heads + i:heads + i + 1] for i in range(5)]
                qk_norm((0, 1, 4, 5), (g_[0], g_[0], g_[2], g_[2]), "fm_normed")
                qk_norm((2, 3, 6, 7), (g_[1], g_[1], g_[3], g_[3]), None)

                o.need("rows_copied", NG)
                for g in range(NG):
                    o.need("rows_copied")
                    for h in range(H):
                        v(STT(decG[:, g * H + h, :], egG[:, g * H + h, :], cum[:, g, 8 + h:9 + h], C("causal_t"),
                              ALU.subtract, ALU.add), None)
                for g in range(NG):
                    v(TT(sc4[:, g, :], egG[:, g * H:(g + 1) * H, CH - 1], cum[:, g, 8:12], ALU.subtract),
                      "decG_diff" if g else None)
                o.need("decG_ready")
                for g in range(NG):
                    o.need("beta_rows")
                    v(TT(AT[:, g * H:(g + 1) * H, :], decG[:, g * H:(g + 1) * H, :],
                         bank[6 + g][:, :].rearrange("p (h i) -> p h i", h=H), ALU.mult), "AT_beta")
                o.settle()
                for g in range(NG):
                    for r in range(2):
                        o.need("gdn_scored")
                        b = bank[2 + 2 * g + r][:, :].rearrange("p (j t i) -> p j t i", j=2, t=2)
                        hh = slice(g * H + r, g * H + H, 2)
                        v(TT(AT[:, hh, :], AT[:, hh, :], b[:, 0], ALU.mult))
                        v(TT(decG[:, hh, :], decG[:, hh, :], b[:, 1], ALU.mult), "gdn_scaled")
                for g in range(NG):
                    idb = C("ident").unsqueeze(1).broadcast_to([P, H, CH])
                    v(CP(XT[:, g * H:(g + 1) * H, :], idb))
                    v(CP(X[:, g * H:(g + 1) * H, :], idb), "X_ready")
                v(TT(be[:, :, :], be[:, :, :], beta[:, 0:2, :], ALU.mult))
                for g in range(NG):
                    o.need("kvt_copied")
                    kk = kvt[:, g * 4:g * 4 + 2, :].rearrange("p a (b d) -> p (a b) d", d=HD)
                    vv = kvt[:, g * 4 + 2:g * 4 + 4, :].rearrange("p a (b d) -> p (a b) d", d=HD)
                    o.settle()
                    gh = slice(g * H, (g + 1) * H)
                    v(TT(ktail[:, gh, :], kk, sc4[:, g, :].unsqueeze(2).broadcast_to([P, H, HD]), ALU.mult))
                    v(TT(Rk[:, gh, :], kk, be[:, g, :].unsqueeze(2).broadcast_to([P, H, HD]), ALU.mult))
                    v(TT(Rv[:, gh, :], vv, beta[:, g, :].unsqueeze(2).broadcast_to([P, H, HD]), ALU.mult), "R_ready")
                for r in range(2):
                    q = slice(r * HD, (r + 1) * HD)
                    v(TT(qh[q, :, :], act[q, 0:2, CH:SEQ], egG[q, H + r:2 * H:2, :], ALU.mult))
                for n, s in enumerate(LEVELS):
                    last = n == len(LEVELS) - 1
                    for g in range(NG):
                        gh = slice(g * H, (g + 1) * H)
                        o.need("Q_done")
                        v(TT(Qs[:, gh, :], bank[2 + g][:, :].rearrange("p (h i) -> p h i", h=H),
                             C(f"level{s}").unsqueeze(1).broadcast_to([P, H, CH]), ALU.mult), "Q_ready")
                    for g in range(NG):
                        gh = slice(g * H, (g + 1) * H)
                        o.need("QX_done")
                        v(TT(XT[:, gh, :], XT[:, gh, :], bank[6 + g][:, :].rearrange("p (h i) -> p h i", h=H),
                             ALU.subtract), "XT_ready")
                        if not last:
                            o.need("XQ_done")
                            v(TT(X[:, gh, :], X[:, gh, :], bank[4 + g][:, :].rearrange("p (h i) -> p h i", h=H),
                                 ALU.subtract), "X_ready")
                for g in range(NG):
                    o.need("S_done")
                    b = bank[6][:, 0:P].rearrange("p (t d) -> p t d", t=2)
                    if g == 0:
                        v(CP(S0[:, :, :], b), "S_ready")
                    else:
                        o.settle()
                        for t in range(2):
                            for r in range(2):
                                q = slice(r * HD, (r + 1) * HD)
                                h = 2 * t + r
                                v(STT(S1[q, t, :], S0[q, t, :], egG[q, H + h, CH - 1:CH], b[q, t, :], ALU.mult,
                                      ALU.add), "S_ready" if h == 3 else None)
                        ve.wait_ge(sem("oT_ready"), 2 * (l + 1))

                ve.wait_ge(sem("gdn_p_stored"), 32 * (l + 1))
                v(ve.memset(sme[:, 0, 0:1], 0.0), "phase2")
                for g in range(NG):
                    o.need("rows_copied")
                    for h in range(H):
                        v(STT(MT[:, g * H + h, :], egS[:, g * H + h, :], cum[:, g, h:h + 1], C("causal_t"),
                              ALU.subtract, ALU.add))
                    v(TT(ws[:, g, :], egS[:, g * H:(g + 1) * H, CH - 1], cum[:, g, 0:4], ALU.subtract),
                      "MT_diff" if g else None)
                o.need("decS_ready")
                v(TT(Cg[0:HD, :, :], act[0:HD, 9:10, CH:SEQ].broadcast_to([HD, 2, CH]), egS[0:HD, H:H + 2, :], ALU.mult))
                v(TT(Cg[HD:P, :, :], act[HD:P, 9:10, CH:SEQ].broadcast_to([HD, 2, CH]), egS[HD:P, H + 2:H + 4, :],
                     ALU.mult), "Cg_ready")
                for g in range(NG):
                    for t in range(2):
                        o.need("ssd_scored")
                        gh = slice(g * H + 2 * t, g * H + 2 * t + 2)
                        v(TT(MT[:, gh, :], MT[:, gh, :],
                             bank[2 + t][:, 0:CH].unsqueeze(1).broadcast_to([P, 2, CH]), ALU.mult), "MT_ready")
                    o.need("xt_copied")
                    if g:
                        ve.wait_ge(sem("hs_done"), 2 * l + 1)
                    vs(TT(xdt[:, :, :], xt[:, 0:2, :].rearrange("p a (b d) -> p (a b) d", d=HD),
                          smp[:, g, 0:4].unsqueeze(2).broadcast_to([P, H, HD]), ALU.mult))
                    v(TT(xw[:, :, :], xdt[:, :, :], ws[:, g, :].unsqueeze(2).broadcast_to([P, H, HD]), ALU.mult),
                      "xw_ready")
                    for t in range(2):
                        o.need("yA_done")
                        v(STT(yA[:, t, g * CH:(g + 1) * CH], act[:, 6 + t, g * CH:(g + 1) * CH], dcol[:, l, t:t + 1],
                              bank[5 + t][:, 0:CH], ALU.mult, ALU.add), "yA_copied")
                    o.need("hs_done")
                    b = bank[7][:, 0:P].rearrange("p (r d) -> p r d", r=2)
                    if g == 0:
                        v(CP(hs0[:, :, :], b), "hs_ready")
                    else:
                        o.settle()
                        for t in range(2):
                            for r in range(2):
                                q = slice(t * HD, (t + 1) * HD)
                                v(STT(hs1[q, r, :], hs0[q, r, :], egS[q, H + 2 * t + r, CH - 1:CH], b[q, r, :],
                                      ALU.mult, ALU.add), "hs_ready" if t + r == 2 else None)


                def scores(n):
                    m, h = n // 4, n % 4
                    o.need("s_done")
                    s, b = s3[:, n % 2, :], bank[2 + n % 2]
                    if n >= 2:
                        ve.wait_ge(sem("PT_turned"), 8 * l + n - 1)
                    if m == 0:
                        v(STT(s[:, 0:CH], rowF[:, h, 0:CH], cum[:, 0, 4 + h:5 + h], b[:, 0:CH], ALU.subtract, ALU.add))
                        vs(STT(s[:, CH:3 * CH], rowF[:, h, :], cum[:, 1, 4 + h:5 + h], b[:, CH:3 * CH],
                               ALU.subtract, ALU.add), "s_read")
                        vs(TT(s, s, C("mask3"), ALU.add))
                    else:
                        vs(TT(s, b[:, 0:3 * CH], C(f"alibi{h}"), ALU.add), "s_read")
                    v(RED(nmx[:, n, 0:1], s[:, 0:CH], AX.X, ALU.max))
                    vs(RED(nmx[:, n, 1:2], s[:, CH:3 * CH], AX.X, ALU.max))
                    v(TS(nmx[:, n, :], nmx[:, n, :], -1.0, None, ALU.mult), "nmx_ready")

                def shares(n):
                    o.need("exp_done")
                    s = s3[:, n % 2, :]
                    vs(ve.reciprocal(rsum[:, n, :], rsum[:, n, :]))
                    v(TS(s[:, 0:CH], s[:, 0:CH], rsum[:, n, 0:1], None, ALU.mult))
                    v(TS(s[:, CH:3 * CH], s[:, CH:3 * CH], rsum[:, n, 1:2], None, ALU.mult), "P_ready")

                for n in range(8):
                    scores(n)
                    if n:
                        shares(n - 1)
                shares(7)

                v(CP(stq[0:NS, 0:4], smp[0:NS, 2, 0:4]))
                v(CP(stq[0:NS, 4:8], cin[0:NS, 2, 0:4]))
                v(CP(stq[0:NS, 8:12], cin[0:NS, 2, 8:12]))
                v(CP(stq[0:NS, 12:16], beta[0:NS, 2, :]), "stq_logs")
                o.need("fmj_copied")
                ve.wait_ge(sem("state_landed"), 64 * (l + 1))

                def spread_bt(q):
                    return fmj[:, 2 * q:2 * q + 2, :].rearrange("p t b -> p b t").unsqueeze(3).broadcast_to(
                        [P, NS, 2, HD])

                h4 = hst.rearrange("p (b t) n -> p b t n", t=2)
                g4 = gst.rearrange("p (b t) n -> p b t n", t=2)
                a4 = tmpA.rearrange("p (b t) n -> p b t n", t=2)
                b4 = tmpB.rearrange("p (b t) n -> p b t n", t=2)
                v(TT(h4, h4, spread_bt(1), ALU.mult))
                vs(TT(kb[:, :, :].rearrange("p b t -> p t b"), act[:, 6:8, SEQ:NT], fmj[:, 0:2, :], ALU.mult))
                for j in range(4):
                    o.need("bc_rows")
                    bc = bank[4 + j % 2][:, :].rearrange("p (b z t n) -> p b z t n", b=2, z=2, t=2)
                    for i in range(2):
                        b = 2 * j + i
                        vs(TT(a4[:, b], bc[:, i, 0], kb[:, b, :].unsqueeze(2).broadcast_to([P, 2, HD]), ALU.mult))
                        vs(TT(h4[:, b], h4[:, b], a4[:, b], ALU.add))
                        v(TT(b4[:, b], bc[:, i, 1], h4[:, b], ALU.mult), "hst_step" if i else None)
                o.settle()
                vs(RED(yd16[:, :], tmpB[:, :, :], AX.X, ALU.add))
                for t in range(2):
                    v(STT(yA[:, t, SEQ:NT], act[:, 6 + t, SEQ:NT], dcol[:, l, t:t + 1],
                          yd16[:, :].rearrange("p (b t) -> p t b", t=2)[:, t, :], ALU.mult, ALU.add))
                vs(TT(g4, g4, spread_bt(2), ALU.mult), "tmpA_free")
                kbc = act[:, 2:4, SEQ:NT].rearrange("p t b -> p b t").unsqueeze(3).broadcast_to([P, NS, 2, HD])
                v(TT(b4, g4, kbc, ALU.mult), "Sk_ready")
                vs(TT(kb[:, :, :].rearrange("p b t -> p t b"), act[:, 2:4, SEQ:NT], fmj[:, 6:8, :], ALU.mult))
                for j in range(2):
                    o.need("v_copied")
                    o.need("ks_done")
                    vs(TT(tmpA[:, 8 * j:8 * j + 8, :], tmpA[:, 8 * j:8 * j + 8, :],
                          bank[2 + j][:, :].rearrange("p (a d) -> p a d", a=8), ALU.subtract), "ks_read")
                vs(TT(a4, a4, kb[:, :, :].unsqueeze(3).broadcast_to([P, NS, 2, HD]), ALU.mult))
                v(TT(g4, g4, a4, ALU.add), "gst_ready")

                ve.wait_ge(sem("lf_landed"), 256 * (l + 1))
                src, dst = lf, lfb
                for step in (1, 2, 4, 8):
                    v(TT(dst[:, 0:SP_ - step, :], src[:, 0:SP_ - step, :], src[:, step:SP_, :], ALU.add))
                    vs(CP(dst[:, SP_ - step:SP_, :], src[:, SP_ - step:SP_, :]))
                    src, dst = dst, src
                assert src is lf
                v(ve.memset(sme[:, 0, 0:1], 0.0), "lf_ready")
                o.need("qbc_copied")
                for m in range(2):
                    i = index[("k", l, m)]
                    ve.wait_ge(landed[slot_of[i]], landed_at[i])
                    kk = ring[slot_of[i]][:, :].rearrange("p (s f) -> p s f", s=SP_)
                    vs(TT(kk, kk, qbc[:, m:m + 1, :].broadcast_to([P, SP_, GW]), ALU.mult))
                    v(RED(scd[:, :, 4 * m:4 * m + 4], kk.rearrange("p s (h d) -> p s h d", h=H), AX.X, ALU.add), "k_used")
                o.settle()
                v(TT(scd[:, 0:SP_ - 1, 0:4], scd[:, 0:SP_ - 1, 0:4], lf[:, 1:SP_, :], ALU.add))
                v(TT(scd[:, :, 4:8], scd[:, :, 4:8], C("alibi_dec").rearrange("p (s h) -> p s h", h=H), ALU.add))
                o.settle()
                o.need("bias_done")
                vs(TT(scd[:, :, 0:4], scd[:, :, 0:4], bank[3][:, 0:H].unsqueeze(1).broadcast_to([P, SP_, H]),
                      ALU.add), "bias_added")
                vs(RED(mcol[:, :], scd[:, :, :].rearrange("p s h -> p h s"), AX.X, ALU.max))
                ve.wait_ge(sem("stok_copied"), 3 * (l + 1))
                tw = tmpA[0:NS, 0:8, :]
                vs(TT(tw, stok[0:NS, 0:2, :].rearrange("p m (h d) -> p (m h) d", d=HD),
                      stok[0:NS, 2:4, :].rearrange("p m (h d) -> p (m h) d", d=HD), ALU.mult))
                v(RED(sself[0:NS, :], tw, AX.X, ALU.add), "max_ready")
                o.need("max_turned")
                vs(RED(ms8[0:8, :], bank[4][0:8, 0:P].rearrange("p (b c) -> p b c", b=NS), AX.X, ALU.max))
                vs(TT(ms8[0:8, :], ms8[0:8, :], bank[4][0:8, P:P + NS], ALU.max), "mcol_ready")
                o.need("m_turned")
                vs(CP(mtok[0:NS, :], bank[5][0:NS, 0:8]), "mtok_copied")
                vs(TT(sself[0:NS, :], sself[0:NS, :], mtok[0:NS, :], ALU.subtract))
                o.need("m_spread")
                v(TT(scd[:, :, :], scd[:, :, :], bank[6][:, 0:8].unsqueeze(1).broadcast_to([P, SP_, 8]),
                     ALU.subtract), "m_spread_read")
                o.need("scd_exp")
                v(RED(psums[:, :], scd[:, :, :].rearrange("p s h -> p h s"), AX.X, ALU.add), "psums_ready")
                o.need("den_done")
                vs(TT(rden[0:NS, :], sself[0:NS, :], bank[7][0:NS, 0:8], ALU.add))
                vs(ve.reciprocal(rden[0:NS, :], rden[0:NS, :]))
                v(TT(sself[0:NS, :], sself[0:NS, :], rden[0:NS, :], ALU.mult), "rden_ready")
                o.need("rden_spread")
                vs(TT(scd[:, :, :], scd[:, :, :], bank[2][:, 0:8].unsqueeze(1).broadcast_to([P, SP_, 8]), ALU.mult),
                   "Pd_scaled")
                for m in range(2):
                    v(TT(Pd[:, m * SP_:(m + 1) * SP_, :].rearrange("p s (b h) -> p s b h", b=NS),
                         scd[:, :, 4 * m:4 * m + 4].unsqueeze(2).broadcast_to([P, SP_, NS, H]),
                         C("own_col").unsqueeze(1).unsqueeze(3).broadcast_to([P, SP_, NS, H]), ALU.mult),
                      "Pd_ready" if m else None)
                o.need("psb_copied")
                ve.wait_ge(tile_done, done_at[index[("v", l, 1)]])
                yd = bank[4][:, 0:64].rearrange("p (j b r) -> p j b r", j=4, r=2)
                for m in range(2):
                    v(TT(psb[:, 2 * m:2 * m + 2, :], psb[:, 2 * m:2 * m + 2, :],
                         fm[:, 8 + 2 * m:10 + 2 * m, SEQ:NT], ALU.mult))
                o.settle()
                for m in range(2):
                    for r in range(2):
                        q = slice(r * HD, (r + 1) * HD)
                        f = (2, 6)[m]
                        v(TT(yT[q, f:f + 2, SEQ:NT], psb[q, 2 * m:2 * m + 2, :], yd[q, 2 * m:2 * m + 2, :, r],
                             ALU.add), "yd_read" if m + r == 2 else None)
                o.settle()
                o.need("zz_ready")
                vs(TT(yA[:, :, :], yA[:, :, :], zz[:, 0:2, :], ALU.mult), "yA_gated")
                o.need("head_rstd")
                for t in range(2):
                    v(STT(yT[:, t, :], yA[:, t, :], prm2[:, 46 * l + t:46 * l + t + 1], rstd[:, 2, :], ALU.mult,
                          ALU.mult))
                for t in range(2):
                    o.need("head_rstd")
                    vs(STT(oT[:, t, :], oT[:, t, :], g_[4], rstd[:, t, :], ALU.mult, ALU.mult))
                ve.wait_ge(sem("yBD_copied"), 4 * (l + 1))
                v(TT(yT[:, 4:6, :], oT[:, :, :], zz[:, 2:4, :], ALU.mult), "yT_ready")

                def add_x(src, m, gate, name):
                    v(STT(xT[:, m, 0:SEQ], src[:, 0:SEQ], modT[:, gate + m, 0:1], xT[:, m, 0:SEQ], ALU.mult, ALU.add))
                    vs(TT(sxy[:, :], src[:, SEQ:NT], modT[:, gate + m, 1:9], ALU.mult), name)
                    vs(TT(xT[:, m, SEQ:NT], xT[:, m, SEQ:NT], sxy[:, :], ALU.add))

                add_bias(l, 4 * MIX_CHUNKS, 48)
                t0 = ticks_before(index[("out", l, 0)])
                for m in range(KD):
                    ve.wait_ge(tile_done, t0 + m + 1)
                    add_x(bank[m % 4], m, 16, "x_added")
                v(ve.memset(sme[:, 0, 0:1], 0.0), "x_whole")
                modulate(24, prm1[:, 112 + 8 * l:120 + 8 * l])
                ve.wait_ge(sem("stored"), 16 * STORES * (l + 1))
                if l == 0:
                    v(ve.memset(sg[:, :, 0:1], 0.0), "ffn_phase")
                    t0 = ticks_before(index[("gu", 0, 0)])
                    for f in range(FF // P):
                        ve.wait_ge(tile_done, t0 + 2 * f + 2)
                        o.need("sg_ready")
                        v(TT(hid[:, f, :], sg[:, f % 2, :], bank[2 * (f % 2) + 1][:, 0:NT], ALU.mult), "hid_ready")
                    for m in range(KD):
                        ve.wait_ge(tile_done, done_at[index[("down", 0, m // 2, 1)]] - 1 + m % 2)
                        add_x(bank[4 + m % 4], m, 40, "acc_ready")
                    v(ve.memset(sxy[:, 0:1], 0.0), "x_whole")
                else:
                    v(ve.memset(sg[:, :, 0:1], 0.0), "ffn_phase")
                    v(ve.memset(lg[:, :, :], 0.0))
                    v(ve.memset(acc[:, :, :], 0.0))
                    o.settle()
                    o.need("lg_done")
                    v(CP(lg[:, 0:2, :], bank[0][:, 0:16].rearrange("p (g e) -> p g e", g=2)))
                    vs(CP(lg[0:NS, 2, :], bank[0][0:NS, 16:24]))
                    mine = lg[:, :, :].rearrange("p g e -> p (g e)").unsqueeze(2).broadcast_to([P, 3 * NE, NE])
                    for g in range(3):
                        row = slice(g * NE, (g + 1) * NE)
                        me = lg[:, g, :].unsqueeze(2).broadcast_to([P, NE, NE])
                        ot = lg[:, g, :].unsqueeze(1).broadcast_to([P, NE, NE])
                        v(TT(cmp[:, row, :], ot, me, ALU.is_gt))
                        vs(TT(cmp2[:, row, :], ot, me, ALU.is_equal))
                        v(TT(cmp2[:, row, :], cmp2[:, row, :], C("tie").rearrange("p (a b) -> p a b", a=NE), ALU.mult))
                    o.settle()
                    vs(TT(cmp[:, :, :], cmp[:, :, :], cmp2[:, :, :], ALU.add))
                    v(RED(rank[:, :, :], cmp.rearrange("p (g e) f -> p g e f", g=3), AX.X, ALU.add))
                    vs(RED(v1[:, :], lg[:, :, :], AX.X, ALU.max))
                    vs(TT(lg[:, :, :], lg[:, :, :], v1[:, :].unsqueeze(2).broadcast_to([P, 3, NE]), ALU.subtract),
                       "lg_shift")
                    vs(TS(rank[:, :, :], rank[:, :, :], 1.5, None, ALU.is_lt))
                    o.need("lg_exp")
                    vs(TT(gates[:, :, :], gates[:, :, :], rank[:, :, :], ALU.mult))
                    vs(RED(v1[:, :], gates[:, :, :], AX.X, ALU.add))
                    vs(ve.reciprocal(v1[:, :], v1[:, :]))
                    v(TT(gates[:, :, :], gates[:, :, :], v1[:, :].unsqueeze(2).broadcast_to([P, 3, NE]), ALU.mult),
                      "gates_ready")
                    ve.wait_ge(sem("gbc_copied"), NE)
                    chain = o.made["ve_chain"]
                    with ve.Fori(0, NE) as e:
                        for f in range(FE // P):
                            ve.wait_ge(sem("sg_ready"), e * (FE // P) + (FF // P + f + 1))
                            TT(sgg[:, f % 2, :], sg[:, f % 2, :], gbc[:, bass.ds(e, 1), :].rearrange("p o n -> p (o n)"),
                               ALU.mult).then_inc(sem("ve_chain"), 1)
                            ve.wait_ge(tile_done, e * E_TICKS + (ticks_pre + 2 * f + 2))
                            ve.wait_ge(sem("ve_chain"), e * (FE // P) + (chain + f + 1))
                            TT(hid[:, f, :], sgg[:, f % 2, :], bank[2 * (f % 2) + 1][:, 0:NT],
                               ALU.mult).then_inc(sem("hid_ready"), 1)
                        for m in range(KD):
                            ve.wait_ge(tile_done, e * E_TICKS + (ticks_pre + 4 * E_GU + m + 1))
                            TT(acc[:, m, :], acc[:, m, :], bank[4 + m % 4][:, 0:NT], ALU.add).then_inc(
                                sem("acc_ready"), 1)
                    o.made["ve_chain"] += NE * (FE // P)
                    ve.wait_ge(sem("acc_ready"), KD * (NE + 1))
                    for m in range(KD):
                        add_x(acc[:, m, :], m, 40, None)
                    v(ve.memset(sxy[:, 0:1], 0.0), "x_final")

        @block.gpsimd
        def _(pool):
            o = Order(pool, "pool_chain")
            stores = [0]

            def store(dst, src):
                pool.dma_start(dst, src).then_inc(sem("stored"), 16)
                stores[0] += 1

            def halves(dst, src, l):
                for r in range(2):
                    store(O[dst][l].rearrange("b (t r) p n -> r p (b t) n", r=2)[r], src[r * HD:(r + 1) * HD])

            def load(dst, src, name):
                pool.dma_start(dst, src).then_inc(sem(name), 16)

            for l in range(DEPTH):
                r = 46 * l
                load(prow2[r:r + 2, :], A["ssd_norm"][l].rearrange("(m p) -> m p", p=P), "params_landed")
                load(prow2[r + 2:r + 18, :], A["ssd_conv_w"][l].rearrange("k (m p) -> (k m) p", p=P), "params_landed")
                load(prow2[r + 18:r + 22, :], A["ssd_conv_b"][l].rearrange("(m p) -> m p", p=P), "params_landed")
                load(prow2[r + 22:r + 46, :], A["gdn_conv_w"][l].rearrange("k (m p) -> (k m) p", p=P), "params_landed")
                for n, name in enumerate(("fox_q_norm", "moba_q_norm", "fox_k_norm", "moba_k_norm", "gdn_norm")):
                    for r in range(2):
                        q = 92 + 5 * l + n
                        load(prow2[q:q + 1, r * HD:(r + 1) * HD], A[name][l:l + 1, :], "params_landed")
            with nc.allow_non_contiguous_dma(reason="small per-head columns"):
                for l in range(DEPTH):
                    for col, n, at in SMALL:
                        load(w_small[:, l, :, at:at + n],
                             A["w_in"][l].rearrange("(k p) n -> p k n", p=P)[:, :, col:col + n], "small_landed")
                for name, at in (("ssd_dt_bias", 0), ("fox_b_f", 4), ("gdn_dt_bias", 12)):
                    load(brow[:, :, at:at + 4], A[name].partition_broadcast(P), "small_landed")
                for name, at in (("ssd_a_log", 0), ("gdn_a_log", 4)):
                    load(alog[:, :, at:at + 4], A[name].partition_broadcast(P), "small_landed")
                for r in range(2):
                    for l in range(DEPTH):
                        load(dcol[r * HD:(r + 1) * HD, l, :],
                             A["ssd_d"][l].rearrange("(t r) -> r t", r=2)[r].partition_broadcast(HD), "small_landed")
                load(router[:, :, :], A["moe_router"][0].rearrange("(k p) e -> p k e", p=P), "small_landed")

            for l in range(DEPTH):
                at = stores[0]
                with nc.allow_non_contiguous_dma(reason="forget gates of four heads"):
                    pool.wait_ge(sem("cin_ready"), l + 1)
                    store(O["fox_logf_p"][l, 0].rearrange("(g p) h -> p g h", p=P), nlf[:, 0:2, :])
                    store(O["fox_logf_s"][l].rearrange("b s h -> (b s) h"), nlf[0:NS, 2, :])
                pool.wait_ge(sem("tail_copied"), 3 * (l + 1))
                for lo, n, name in ((0, QKV, "gdn_conv"), (QKV, XBC, "ssm_conv")):
                    store(O[name + "_p"][l, 0], convrow[0:3, lo:lo + n])
                    store(O[name + "_s"][l].rearrange("b k c -> (b k) c"), convrow[3:27, lo:lo + n])
                pool.wait_ge(sem("S_ready"), 2 * (l + 1))
                for r in range(2):
                    pool.dma_start(O["gdn_p"][l, 0].rearrange("(t r) p n -> r p t n", r=2)[r],
                                   S1[r * HD:(r + 1) * HD]).then_inc(sem("gdn_p_stored"), 16)
                pool.wait_ge(sem("hsout_copied"), l + 1)
                for r in range(2):
                    store(O["ssm_p"][l, 0].rearrange("(t r) p n -> r p t n", r=2)[r],
                          hsout[r * HD:(r + 1) * HD, :].rearrange("p (t n) -> p t n", t=2))
                for i, name in enumerate(("fox_k", "moba_k", "fox_v", "moba_v")):
                    pool.wait_ge(sem("kvp_copied"), 4 * l + i + 1)
                    store(O[name + "_p"][l, 0].rearrange("(g p) h d -> p g (h d)", p=P), kvp[:, i * NG:(i + 1) * NG, :])
                pool.wait_ge(sem("stok_copied"), 3 * (l + 1))
                for i, name in enumerate(("fox_k", "moba_k", "fox_v", "moba_v")):
                    store(O[name + "_s"][l].rearrange("b s h d -> (b s) (h d)"), stok[0:NS, 2 + i, :])
                pool.wait_ge(sem("hst_step"), 4 * (l + 1))
                halves("ssm_s", hst, l)
                pool.wait_ge(sem("gst_ready"), l + 1)
                halves("gdn_s", gst, l)
                assert stores[0] - at == STORES, stores[0] - at
            pool.wait_ge(sem("out_copied"), 6)
            store(O["y_prompt"][0].rearrange("(g p) d -> p g d", p=P), stage[:, 0:2, :])
            store(O["y_sample"].rearrange("b s d -> (b s) d"), stage[0:NS, 2, :])
            pool.wait_ge(sem("stored"), 16 * stores[0])
            pool.wait_ge(sem("gdn_p_stored"), 32 * DEPTH)


_INS = ["x_prompt", "x_sample", "cache_fox_k", "cache_fox_v", "cache_fox_logf", "cache_moba_k", "cache_moba_v",
        "state_ssm", "state_ssm_conv", "state_gdn", "state_gdn_conv", "page_table", "c_prompt", "c_sample",
        "w_ada", "b_ada", "norm_mix", "norm_ffn", "w_in", "w_out", "ssd_conv_w", "ssd_conv_b", "ssd_dt_bias",
        "ssd_a_log", "ssd_d", "ssd_norm", "fox_b_f", "fox_q_norm", "fox_k_norm", "gdn_conv_w", "gdn_a_log",
        "gdn_dt_bias", "gdn_norm", "moba_q_norm", "moba_k_norm", "ffn_w_gate", "ffn_w_up", "ffn_w_down",
        "moe_router", "moe_w_gate", "moe_w_up", "moe_w_down"]


def _outs():
    outs = [("y_prompt", (1, SEQ, D)), ("y_sample", (NS, 1, D))]
    for s, b, n in (("p", 1, SEQ), ("s", NS, 1)):
        outs += [(f"fox_k_{s}", (DEPTH, b, n, H, HD)), (f"fox_v_{s}", (DEPTH, b, n, H, HD)),
                 (f"fox_logf_{s}", (DEPTH, b, n, H)), (f"moba_k_{s}", (DEPTH, b, n, H, HD)),
                 (f"moba_v_{s}", (DEPTH, b, n, H, HD)), (f"ssm_{s}", (DEPTH, b, H, HD, HD)),
                 (f"ssm_conv_{s}", (DEPTH, b, CW - 1, XBC)), (f"gdn_{s}", (DEPTH, b, H, HD, HD)),
                 (f"gdn_conv_{s}", (DEPTH, b, CW - 1, QKV))]
    return outs


def kernel(**inputs):
    import concourse.bacc as bacc
    from concourse.bass_utils import run_bass_kernel_spmd

    nc = bacc.Bacc("TRN2", target_bir_lowering=False, num_devices=1)
    arrays, A, O = {}, {}, {}
    table, const_at = consts()
    for name in _INS + ["consts"]:
        a = table if name == "consts" else np.ascontiguousarray(inputs[name])
        arrays[f"in_{name}"] = a
        A[name] = nc.dram_tensor(f"in_{name}", a.shape, mybir.dt.from_np(a.dtype), kind="ExternalInput").ap()
    outs = _outs()
    for name, shape in outs:
        O[name] = nc.dram_tensor(f"out_{name}", shape, F32, kind="ExternalOutput").ap()
    build(nc, A, O, const_at, table.shape[1])
    r = run_bass_kernel_spmd(nc, [arrays], core_ids=[0])
    return tuple(r.results[0][f"out_{name}"] for name, _ in outs)
```

```python
from contextlib import ExitStack
from itertools import product

import numpy as np
import concourse.bass as bass
from concourse import mybir

F32 = mybir.dt.float32
F32R = mybir.dt.float32r
I32 = mybir.dt.int32
ALU = mybir.AluOpType
ACT = mybir.ActivationFunctionType
AX = mybir.AxisListType

P = 128
D = 1024
KD = D // P
SEQ = 256
NS = 8
NT = SEQ + NS
DEPTH = 2
PAST = 256
PAGE = 128
PAGES = PAST // PAGE
POOL = 20
HD = 64
H = 4
GW = 256
CW = 4
XBC = 512
QKV = 768
IN_COLS = 3344
FF = 2816
FE = 1792
NE = 8
EPS = 1e-6
NEG = -1e30
CH = P
NG = SEQ // CH
SC = P // NS
SP_ = PAST // SC
SLOT = 4096
NSLOT = 4
CAP = P
ROUNDS = -(-NT // CAP)
LEVELS = [1, 2, 4, 8, 16, 32, 64]
UW = 3 + SEQ + CW * NS
CVW = UW - 3
G_SLABS = [(1544, 384), (1928, 384), (2320, 256)]
S_SLABS = [(0, 384), (384, 384)]
F_SLABS = [(772, 384), (1156, 384)]
M_SLABS = [(2576, 384), (2960, 384)]
IN_SLABS = G_SLABS + S_SLABS + F_SLABS + M_SLABS
SMALL = [(768, 4, 0), (1540, 4, 4), (2312, 8, 8)]


def consts():
    i = np.arange(P)
    parts = {}
    parts["ident"] = np.eye(P)
    parts["ones"] = np.ones((P, P))
    parts["upper"] = (i[:, None] <= i[None, :])
    parts["blk"] = (i[:, None] // HD == i[None, :] // HD)
    parts["causal_t"] = np.where(i[None, :] >= i[:, None], 0.0, NEG)
    causal = np.where(i[None, :] <= i[:, None], 0.0, NEG)
    parts["mask3"] = np.concatenate([causal, np.zeros((P, P)), causal], 1)
    for h in range(H):
        s = 2.0 ** (-8.0 * (h + 1) / H)
        own = -s * (i[:, None] - i[None, :]) + causal
        before = -s * (i[:, None] + P - i[None, :])
        parts[f"alibi{h}"] = np.concatenate([own, before, own], 1)
    for s in LEVELS:
        parts[f"level{s}"] = ((i[:, None] // (2 * s) == i[None, :] // (2 * s)) & ((i[:, None] // s) % 2 == 1)
                              & ((i[None, :] // s) % 2 == 0))
    parts["later"] = (i[:, None] // SC == i[None, :] // SC) & (i[:, None] > i[None, :])
    parts["own_col"] = (i[:, None] // SC == np.arange(NS)[None, :])
    own_row = np.zeros((P, P))
    own_row[:NS] = (np.arange(NS)[:, None] == i[None, :] // SC)
    parts["own_row"] = own_row
    one = np.zeros((P, NS * P))
    for b in range(NS):
        one[b, b * P:(b + 1) * P] = 1.0
    parts["one_row"] = one
    pos = (i[:, None] % SC) * SP_ + np.arange(SP_)[None, :]
    sl = 2.0 ** (-8.0 * (np.arange(H) + 1) / H)
    parts["alibi_dec"] = (-(PAST - pos)[:, :, None] * sl).reshape(P, -1)
    e = np.arange(NE)
    parts["tie"] = np.broadcast_to((e[None, None, :] < e[None, :, None]), (P, NE, NE)).reshape(P, -1)
    at, off = {}, 0
    for k, v in parts.items():
        at[k] = (off, v.shape[1])
        off += v.shape[1]
    return np.concatenate([np.asarray(v, np.float32) for v in parts.values()], 1), at


MIX_CHUNKS = 4
ADA_CHUNKS = 6 * D // 512
NORM_ADA = {("mix", 0): (0, MIX_CHUNKS), ("ffn", 0): (1, MIX_CHUNKS - 1), ("mix", 1): (1, MIX_CHUNKS)}
MIXER_ADA = [[(0, c) for c in range(MIX_CHUNKS + 1, ADA_CHUNKS)] + [(1, c) for c in range(MIX_CHUNKS - 1)],
             [(1, c) for c in range(MIX_CHUNKS + 1, ADA_CHUNKS)]]
ADA_UNITS = [
    {"gdn": 0, "ssd": 2, "att0": 2, **{f"att{n}": 1 for n in range(1, 8)}, "att8": 2, "v_rows": 1, "ks": 2, "keys": 4},
    {"gdn": 0, "ssd": 1, **{f"att{n}": 1 for n in range(8)}, "att8": 0, "v_rows": 1, "ks": 0, "keys": 4}]
for _l in range(DEPTH):
    assert sum(ADA_UNITS[_l].values()) == 2 * len(MIXER_ADA[_l])


def ada_units(l, place):
    names = list(ADA_UNITS[l])
    first = sum(ADA_UNITS[l][n] for n in names[:names.index(place)])
    return range(first, first + ADA_UNITS[l][place])


def plan_stream():
    out = [("ada", 0, (c,), 2) for c in range(MIX_CHUNKS)]
    for l in range(DEPTH):
        out += [("ada",) + (NORM_ADA["mix", l][0], (NORM_ADA["mix", l][1],), 2)]
        out += [("in", l, s, s[1] // P) for s in IN_SLABS]
        ada = [("ada", la, (c,), 2) for la, c in MIXER_ADA[l]]
        out += ada[:-2] + [("k", l, (m,), 0) for m in range(2)] + ada[-2:] + [("v", l, (m,), 1) for m in range(2)]
        out += [("out", l, (c,), 4) for c in range(2)]
        if l == 0:
            out += [("ada",) + (NORM_ADA["ffn", l][0], (NORM_ADA["ffn", l][1],), 2)]
            out += [("gu", l, (c,), 4) for c in range(FF // 256)]
            out += [("down", l, (c, h), 4) for c in range(4) for h in range(2)]
    return out


def build(nc, A, O, const_at, NCONST):
    ctx = ExitStack()
    with ctx:
        def sb(name, shape, dt=F32):
            return ctx.enter_context(nc.sbuf_tensor(name, shape, dt))

        sems = {}
        REUSED = {"places_read": "stq_ready", "places_done": "m_spread", "rounds_ready": "rden_ready",
                  "pbc_done": "psb_done", "pbc_copied": "psb_copied", "htok_done": "fmj_done",
                  "htok_copied": "fmj_copied", "G_ready": "mcol_ready", "hc_done": "max_turned",
                  "hc_copied": "mtok_copied", "hidT_done": "m_turned", "hidT_copied": "dtok_copied",
                  "yc_ready": "max_ready", "part_done": "den_done", "iota_done": "rden_spread",
                  "iota_copied": "hsout_copied", "shifted": "lf_ready", "hc_high": "qbc_done",
                  "hidT_high": "qbc_copied", "w_high_ready": "bias_done", "w_low_ready": "bias_added"}

        REUSED_EARLY = {"ypv_copied": ("x_copied0", KD // 2), "ypv_turned": ("x_turned", KD),
                        "split_high": ("c_silu", 1), "split_low": ("x_copied1", KD // 2),
                        "f_high": ("params_used", 2), "f_low": ("c_copied", 1),
                        "small_rows": ("params_turned", 2), "small_rows_copied": ("nega_exp", 1)}

        def start_of(name):
            return DEPTH if name in REUSED else REUSED_EARLY.get(name, (name, 0))[1]

        def sem(name):
            name = REUSED.get(name, REUSED_EARLY.get(name, (name, 0))[0])
            if name not in sems:
                sems[name] = ctx.enter_context(nc.semaphore(name))
            return sems[name]

        cst = sb("cst", [P, NCONST])

        def C(name):
            o, n = const_at[name]
            return cst[:, o:o + n]

        ring = [sb(f"ring{i}", [P, SLOT]) for i in range(NSLOT)]
        xT = sb("xT", [P, KD, NT])
        hT = sb("hT", [P, KD, NT])
        yT = hT
        prm1 = sb("prm1", [P, P])
        prm2 = sb("prm2", [P, 102])
        modT = sb("modT", [P, 48, 9])
        gain1 = sb("gain1", [P, KD, 9])
        cT = sb("cT", [P, KD, 9])
        w_small = sb("w_small", [P, DEPTH, KD, 16])
        brow = sb("brow", [P, DEPTH, 16])
        alog = sb("alog", [P, DEPTH, 8])
        nega = sb("nega", [P, DEPTH, 8])
        dcol = sb("dcol", [P, DEPTH, 2])
        router = sb("router", [P, KD, NE])
        pt = sb("pt", [1, NS * PAGES], I32)
        rstd = sb("rstd", [P, 4, NT])
        epsc = sb("epsc", [P, 1])
        yd16 = sb("yd16", [P, 16])
        sxy = sb("sxy", [P, NS])
        rounds = sb("rounds", [P, 1], I32)

        ARENA = 25400
        with nc.sbuf_tensor("arena", [P, ARENA], F32) as arena:
            pass
        PIECE, SPLITS = 1024, 3
        w_high = sb("w_high", [P, SPLITS, PIECE], F32R)
        w_low = sb("w_low", [P, SPLITS, PIECE], F32R)
        with (nc.sbuf_tensor("hH", [P, KD, NT], F32R) as hH, nc.sbuf_tensor("hL", [P, KD, NT], F32R) as hL,
              nc.sbuf_tensor("fH", [P, FF // P, NT], F32R) as fH, nc.sbuf_tensor("fL", [P, FF // P, NT], F32R) as fL):
            pass
        hcH = sb("hcH", [P, KD, 2 * CAP], F32R)
        hcL = sb("hcL", [P, KD, 2 * CAP], F32R)
        hidH = sb("hidH", [P, FE // P, CAP], F32R)
        hidL = sb("hidL", [P, FE // P, CAP], F32R)
        SPLIT = 2 * (SPLITS * PIECE + KD * 2 * CAP + FE // P * CAP)
        top = [0]

        def carve(shape, at=None, parts=P):
            n = int(np.prod(shape))
            o = top[0] if at is None else at
            if at is None:
                top[0] += n
            assert o + n <= ARENA, (o, n)
            v = arena[0:parts, o:o + n]
            if len(shape) == 2:
                v = v.rearrange("p (a b) -> p a b", a=shape[0])
            elif len(shape) == 3:
                v = v.rearrange("p (a b c) -> p a b c", a=shape[0], b=shape[1])
            return v

        u = carve((10, UW))
        states_at = 0
        hst = carve((NS * 2, HD), at=0)
        gst = carve((NS * 2, HD), at=1024)
        cv = carve((2, CVW))
        act = carve((10, NT))
        zz = carve((4, NT))
        fm = carve((12, NT))
        sq = carve((4, NT))
        sm = carve((3, 16))
        sma = carve((3, 16))
        sme = carve((3, 16))
        smp = carve((3, 16))
        beta = carve((3, 4))
        cin = carve((3, 12))
        cum = carve((NG, 12))
        stq = carve((16,))
        fmj = carve((8, NS))
        nlf = carve((3, 4))
        rowF = carve((H, SEQ))
        oT = carve((2, NT))
        yA = carve((2, NT))
        convrow = carve((XBC + QKV,))
        tail = carve((10, 27))
        phase = top[0]
        egG = carve((NG * H, CH))
        decG = carve((NG * H, CH))
        AT = carve((NG * H, CH))
        X = carve((NG * H, CH))
        XT = carve((NG * H, CH))
        Qs = carve((NG * H, CH))
        kvt = carve((NG * 4, P))
        Rv = carve((NG * H, HD))
        Rk = carve((NG * H, HD))
        ktail = carve((NG * H, HD))
        wkT = carve((2, CH))
        wtok = carve((H, HD))
        S0 = carve((2, HD))
        S1 = carve((2, HD))
        qh = carve((2, CH))
        sc4 = carve((NG, 4))
        be = carve((NG, 4))
        end1 = top[0]
        top[0] = phase
        egS = carve((NG * H, CH))
        MT = carve((NG * H, CH))
        xt = carve((3, P))
        xdt = carve((H, HD))
        xw = carve((H, HD))
        ws = carve((NG, 4))
        Cg = carve((2, CH))
        hs0 = carve((2, HD))
        hs1 = carve((2, HD))
        s3 = carve((2, 3 * CH), at=phase)
        PT = carve((2, 3 * CH), at=phase + 6 * CH)
        nmx = carve((8, 2))
        rsum = carve((8, 2))
        kvp = carve((NG * 4, GW))
        stok = carve((6, GW))
        dtok = carve((4, P))
        hsout = carve((P,))
        qbc = carve((2, GW))
        tmpA = carve((16, HD), at=phase)
        tmpB = carve((16, HD), at=phase + 1024)
        ypv = carve((2 * GW,), at=phase + 1024)
        lf = carve((SP_, H))
        lfb = carve((SP_, H))
        scd = carve((SP_, 8))
        mcol = carve((8,))
        mtok = carve((8,))
        ms8 = carve((8,))
        sself = carve((8,))
        rden = carve((8,))
        psums = carve((8,))
        Pd = carve((2 * SP_, NS * H))
        psb = carve((4, NS))
        kb = carve((NS, 2))
        end2 = top[0]
        top[0] = 0
        dense_at = 2 * (SPLITS * PIECE + KD * NT + FF // P * NT)
        sg = carve((2, NT), at=dense_at)
        ft = carve((2, NT), at=dense_at + 2 * NT)
        top[0] = SPLIT
        acc = carve((KD, NT))
        gbc = hT
        htok = carve((3, D))
        pbc = carve((NE, NT))
        place = carve((3, NE + 2))
        iota = carve((P,))
        iota_col = carve((1,))
        G = carve((3, 2, CAP))
        GwT = carve((NT,))
        sgc = carve((2, 256))
        hidc = carve((2, 256))
        yc = carve((D,))
        most = carve((4,))
        lg = carve((3, NE))
        lgT = carve((NT,))
        gates = carve((3, NE))
        cmp = carve((3 * NE, NE))
        cmp2 = carve((3 * NE, NE))
        rank = carve((3, NE))
        v1 = carve((3,))
        stage = carve((3, D), at=0)
        cstage = carve((D,), at=3 * D)
        prow1 = carve((P,), at=4 * D)
        prow2 = carve((P,), at=4 * D + P)
        assert max(end1, end2, top[0]) <= ARENA, (end1, end2, top[0])

        bank = [ctx.enter_context(nc.psum_tensor(f"bank{i}", [P, 512], F32)) for i in range(8)]

        plan = plan_stream()
        n_pre = len(plan)
        first_slot = (2 - (n_pre - 1)) % NSLOT
        slot_of = [(i + first_slot) % NSLOT for i in range(n_pre)]
        dmas_of = {"ada": 1, "in": 1, "k": NS * PAGES, "v": NS * PAGES, "out": 1, "gu": 2, "down": 1}
        landed = [sem(f"slot{i}_landed") for i in range(NSLOT)]
        tile_done = sem("tile_done")
        k_used = sem("k_used")
        slot_count = [0] * NSLOT
        landed_at, done_at, kdone_at = [], [], []
        ticks = kticks = 0
        for i, (kind, l, a, t) in enumerate(plan):
            s = slot_of[i]
            slot_count[s] += 16 * dmas_of[kind]
            landed_at.append(slot_count[s])
            ticks += t
            kticks += kind == "k"
            done_at.append(ticks)
            kdone_at.append(kticks)
        ticks_pre = ticks
        index = {(kind, l) + tuple(a): i for i, (kind, l, a, t) in enumerate(plan)}
        E_GU, E_DN = FE // 256, 4
        E_SLABS = [("gu", c) for c in range(E_GU)] + [("down", c) for c in range(E_DN)]
        e_slot = [i % NSLOT for i in range(len(E_SLABS))]
        pieces_of = {"gu": [(k, 2) for k in range(0, KD, 2)],
                     "down": [(k, min(4, FE // P - k)) for k in range(0, FE // P, 4)]}
        pieces_of_down0 = [(0, 4), (4, 4), (8, 2), (10, 2), (12, 2)]

        def pieces(kind, c):
            return pieces_of_down0 if kind == "down" and c == 0 else pieces_of[kind]

        e_ticks, e_landed, per_slot, t = [], [], [0] * NSLOT, 0
        for i, (kind, c) in enumerate(E_SLABS):
            t += len(pieces(kind, c))
            e_ticks.append(t)
            per_slot[e_slot[i]] += 32 if kind == "gu" else 16
            e_landed.append(per_slot[e_slot[i]])
        E_TICKS = t
        assert E_TICKS % SPLITS == 0
        E_PIECES = [(i, kind, c, k0, nk) for i, (kind, c) in enumerate(E_SLABS) for k0, nk in pieces(kind, c)]

        def piece_view(t, b):
            i, kind, c, k0, nk = E_PIECES[t]
            if kind == "gu":
                return (ring[b][:, :].rearrange("p (z k n) -> p z k n", z=2, k=KD)[:, :, k0:k0 + nk, :],
                        lambda w: w[:, t % SPLITS, :].rearrange("p (z k n) -> p z k n", z=2, k=2))
            return (ring[b][:, 0:FE // P * 256].rearrange("p (k n) -> p k n", k=FE // P)[:, k0:k0 + nk, :],
                    lambda w: w[:, t % SPLITS, 0:nk * 256].rearrange("p (k n) -> p k n", k=nk))

        D_PIECES = [("gu", (c,), f, z, 0, KD) for c in range(FF // 256) for f in range(2) for z in range(2)]
        D_PIECES += [("down", (c, half), m, half, k0, nk) for c in range(4) for half in range(2) for m in range(2)
                     for k0, nk in ((0, 6), (6, 5))]
        N_GU = FF // P * 2
        f_made = {2 * F + 3: F for F in range(FF // P)}
        f_split = {2 * F + 5: F for F in range(FF // P)}
        d_out = [N_GU + 8 * (m // 2) + 6 + 2 * (m % 2) for m in range(KD)]

        def dense_view(t):
            kind, a, col, z, k0, nk = D_PIECES[t]
            r = ring[slot_of[index[(kind, 0) + a]]]
            if kind == "gu":
                src = r[:, :].rearrange("p (z k n) -> p z k n", z=2, k=KD)[:, z, :, col * P:(col + 1) * P]
            else:
                kt = FF // P // 2
                src = r[:, 0:kt * 256].rearrange("p (k n) -> p k n", k=kt)[:, k0:k0 + nk, col * P:(col + 1) * P]
            return src, lambda w: w[:, t % SPLITS, 0:nk * P].rearrange("p (k n) -> p k n", k=nk)

        def count(base, per, extra, r, e, k, n=NE):
            if isinstance(r, int) and r == 0:
                return e * per + (base + k)
            return r * (n * per + extra) + (e * per + (base + k))

        PAIRS = NE // 2
        gu_read = {e_ticks[c] + 1: c for c in range(E_GU)}
        turned_read = {e_ticks[c + 1] + 2: c for c in range(E_GU - 1)}
        turned_read[e_ticks[E_GU] - 1] = E_GU - 1
        down_read = {e_ticks[E_GU + c] + 1: c for c in range(E_DN - 1)}

        def pair_count(name, per, r, p, k):
            return count(start_of(name), per, per, r, p, k, PAIRS)

        def all_rounds(eng, body):
            body(0)
            eng.wait_ge(sem("rounds_ready"), start_of("rounds_ready") + 1)
            n = eng.value_load(rounds[0:1, 0:1], min_val=1, max_val=ROUNDS)
            with eng.Fori(1, ROUNDS) as r:
                with eng.If(n > r):
                    body(r)

        def ticks_before(i):
            return done_at[i] - plan[i][3]

        class Order:

            def __init__(self, eng, chain):
                self.eng, self.chain = eng, chain
                self.seen, self.made, self.last = {}, {}, None

            def need(self, name, n=1):
                self.seen[name] = self.seen.get(name, start_of(name)) + n
                self.eng.wait_ge(sem(name), self.seen[name])

            def go(self, ins, name=None):
                s = sem(self.chain if name is None else name)
                self.made[s.name] = self.made.get(s.name, 0) + 1
                ins.then_inc(s, 1)
                self.last = (s, self.made[s.name])

            def settle(self):
                self.eng.wait_ge(*self.last)

        STORES = 20
        STARTS, PARAMS = 7, DEPTH * 14

        block = ctx.enter_context(nc.Block())

        @block.sync
        def _(sp):
            def load(dst, src, name):
                sp.dma_start(dst, src).then_inc(sem(name), 16)

            load(cstage[0:1, :], A["c_prompt"], "c_landed")
            load(cstage[1:9, :], A["c_sample"], "c_landed")
            load(cst[:, 0:P], A["consts"][:, 0:P], "c_landed")

            def slab(i):
                kind, l, a, _ = plan[i]
                s = slot_of[i]
                if i >= NSLOT:
                    if plan[i - NSLOT][0] == "k":
                        sp.wait_ge(k_used, kdone_at[i - NSLOT])
                    else:
                        sp.wait_ge(tile_done, done_at[i - NSLOT])
                r = ring[s]
                if kind == "ada":
                    sp.dma_start(r[:, :].rearrange("p (k n) -> p k n", k=KD),
                                 A["w_ada"][l].rearrange("(k p) n -> p k n", p=P)[:, :, a[0] * 512:a[0] * 512 + 512]
                                 ).then_inc(landed[s], 16)
                elif kind == "in":
                    sp.dma_start(r[:, 0:KD * a[1]].rearrange("p (k n) -> p k n", k=KD),
                                 A["w_in"][l].rearrange("(k p) n -> p k n", p=P)[:, :, a[0]:a[0] + a[1]]
                                 ).then_inc(landed[s], 16)
                elif kind == "out":
                    sp.dma_start(r[:, :].rearrange("p (k n) -> p k n", k=KD),
                                 A["w_out"][l].rearrange("(k p) n -> p k n", p=P)[:, :, a[0] * 512:a[0] * 512 + 512]
                                 ).then_inc(landed[s], 16)
                elif kind == "gu":
                    for n, name in enumerate(("ffn_w_gate", "ffn_w_up")):
                        sp.dma_start(r[:, n * 2048:(n + 1) * 2048].rearrange("p (k n) -> p k n", k=KD),
                                     A[name][0].rearrange("(k p) n -> p k n", p=P)[:, :, a[0] * 256:a[0] * 256 + 256]
                                     ).then_inc(landed[s], 16)
                elif kind == "down":
                    kt = FF // P // 2
                    sp.dma_start(r[:, 0:kt * 256].rearrange("p (k n) -> p k n", k=kt),
                                 A["ffn_w_down"][0].rearrange("(k p) n -> p k n", p=P)[
                                     :, a[1] * kt:(a[1] + 1) * kt, a[0] * 256:a[0] * 256 + 256]
                                 ).then_inc(landed[s], 16)
                else:
                    name = f"cache_{('fox', 'moba')[a[0]]}_{kind}"
                    src = A[name][l].rearrange("n (c s) h d -> n c (s h d)", s=SP_)
                    for b in range(NS):
                        for g in range(PAGES):
                            q = b * SC + g * (PAGE // SP_)
                            sp.dma_start(r[q:q + PAGE // SP_, :], src[bass.ds(page[b * PAGES + g], 1), :, :]
                                         .rearrange("o c f -> (o c) f")).then_inc(landed[s], 16)

            slab(0)
            load(cst[:, P:], A["consts"][:, P:], "start_landed")
            load(stage[:, 0:2, :], A["x_prompt"][0].rearrange("(g p) d -> p g d", p=P), "start_landed")
            load(stage[0:NS, 2, :], A["x_sample"].rearrange("b s d -> (b s) d"), "start_landed")
            load(pt[:, :], A["page_table"].rearrange("(o b) n -> o (b n)", o=1), "start_landed")
            slab(1)
            load(prow1[0:96, :], A["b_ada"].rearrange("l (m p) -> (l m) p", p=P), "start_landed")
            load(prow1[96:112, :], A["norm_mix"].rearrange("l (m p) -> (l m) p", p=P), "start_landed")
            load(prow1[112:128, :], A["norm_ffn"].rearrange("l (m p) -> (l m) p", p=P), "start_landed")
            slab(2)
            slab(3)
            sp.wait_ge(sem("start_landed"), 16 * STARTS)
            page = [sp.value_load(pt[0:1, i:i + 1], min_val=0, max_val=POOL - 1) for i in range(NS * PAGES)]

            for l in range(DEPTH):
                lo = index[("ada", l, MIX_CHUNKS)]
                n_l = (index[("ada", 1, MIX_CHUNKS)] if l == 0 else n_pre) - lo
                for i in range(lo, lo + n_l):
                    slab(i)
                    if i == lo + NSLOT - 1:
                        if l:
                            sp.wait_ge(sem("tails_packed"), 1)
                            sp.wait_ge(sem("stored"), 16 * STORES)
                            sp.wait_ge(sem("acc_ready"), KD)
                        load(convrow[0:24, 0:QKV], A["state_gdn_conv"][l].rearrange("b k c -> (b k) c"),
                             "convrow_landed")
                        load(convrow[0:24, QKV:QKV + XBC], A["state_ssm_conv"][l].rearrange("b k c -> (b k) c"),
                             "convrow_landed")
                    if i == index[("k", l, 0)] - 1:
                        sp.wait_ge(sem("tails_packed"), l + 1)
                        for r in range(2):
                            load(hst[r * HD:(r + 1) * HD, :, :],
                                 A["state_ssm"][l].rearrange("b (t r) p n -> r p (b t) n", r=2)[r], "state_landed")
                            load(gst[r * HD:(r + 1) * HD, :, :],
                                 A["state_gdn"][l].rearrange("b (t r) p n -> r p (b t) n", r=2)[r], "state_landed")
                    if i == index[("k", l, 0)]:
                        sp.wait_ge(sem("phase2"), l + 1)
                        for b in range(NS):
                            for g in range(PAGES):
                                q = b * SC + g * (PAGE // SP_)
                                load(lf[q:q + PAGE // SP_, :, :],
                                     A["cache_fox_logf"][l].rearrange("n (c s) h -> n c s h", s=SP_)[
                                         bass.ds(page[b * PAGES + g], 1)].rearrange("o c s h -> (o c) s h"),
                                     "lf_landed")

            def expert_loads(r):
                with sp.Fori(0, NE) as e:
                    for i, (kind, c) in enumerate(E_SLABS):
                        s = e_slot[i]
                        if i >= NSLOT:
                            sp.wait_ge(tile_done, count(ticks_pre, E_TICKS, 0, r, e, e_ticks[i - NSLOT]))
                        else:
                            prev = max(j for j in range(len(E_SLABS)) if e_slot[j] == s)
                            sp.wait_ge(tile_done, count(ticks_pre - E_TICKS, E_TICKS, 0, r, e, e_ticks[prev]))
                        if kind == "gu":
                            for n, name in enumerate(("moe_w_gate", "moe_w_up")):
                                sp.dma_start(ring[s][:, n * 2048:(n + 1) * 2048].rearrange("p (k n) -> p k n", k=KD),
                                             A[name][0][bass.ds(e, 1)].rearrange("o (k p) n -> p (o k) n", p=P)[
                                                 :, :, c * 256:c * 256 + 256]).then_inc(landed[s], 16)
                        else:
                            kt = FE // P
                            sp.dma_start(ring[s][:, 0:kt * 256].rearrange("p (k n) -> p k n", k=kt),
                                         A["moe_w_down"][0][bass.ds(e, 1)].rearrange("o (k p) n -> p (o k) n", p=P)[
                                             :, :, c * 256:c * 256 + 256]).then_inc(landed[s], 16)

            all_rounds(sp, expert_loads)

        @block.tensor
        def _(pe):
            o = Order(pe, "pe_chain")
            mm = pe.matmul
            owner, drains = {}, {}

            def fill(b, drained):
                if b in owner:
                    pe.wait_ge(*owner[b])
                drains[drained] = drains.get(drained, start_of(drained)) + 1
                owner[b] = (sem(drained), drains[drained])
                return bank[b]

            def tp(out, in_, last=None):
                k = in_.shape[0]
                ins = pe.transpose(out, in_, C("ident")[0:k, 0:k])
                if last:
                    ins.then_inc(sem(last), 1)

            tiles = [0]

            def tick(ins):
                ins.then_inc(tile_done, 1)
                tiles[0] += 1

            def use(i):
                pe.wait_ge(landed[slot_of[i]], landed_at[i])
                assert tiles[0] == ticks_before(i), (plan[i], tiles[0], ticks_before(i))
                return ring[slot_of[i]]

            def start_c():
                pe.wait_ge(sem("c_landed"), 48)
                o.need("c_silu")
                b = fill(2, "c_copied")
                for k in range(KD):
                    tp(b[:, k * 9:k * 9 + 9], cstage[0:9, k * P:(k + 1) * P], "turned" if k == KD - 1 else None)

            def start():
                pe.wait_ge(sem("start_landed"), 16 * STARTS)
                tp(fill(7, "params_used")[:, 0:P], prow1[:, :], "params_turned")
                for k in range(KD):
                    b = fill(3 + k % 4, f"x_copied{k % 2}")
                    for g in range(NG):
                        tp(b[:, g * P:(g + 1) * P], stage[:, g, k * P:(k + 1) * P])
                    tp(b[:, SEQ:NT], stage[0:NS, 2, k * P:(k + 1) * P], "x_turned")
                pe.wait_ge(sem("params_landed"), 16 * PARAMS)
                tp(fill(2, "params_used")[:, 0:102], prow2[0:102, :], "params_turned")

            def ada_unit(l, c, half):
                w = ring[slot_of[index[("ada", l, c)]]][:, :].rearrange("p (k n) -> p k n", k=KD)
                if half == 0:
                    use(index[("ada", l, c)])
                b = fill(0, "mod_rows") if half == 0 else bank[0]
                for k in range(4 * half, 4 * half + 4):
                    ins = mm(b[0:9, :], cT[:, k, :], w[:, k, :], start=k == 0, stop=k == KD - 1)
                if half:
                    tick(ins)

            def ada_turn(l, c):
                o.need("mod_rows")
                b = fill(1, "mod_ready")
                rows_ = ring[slot_of[index[("ada", l, c)]]]
                for m in range(4):
                    ins = pe.transpose(b[:, m * 9:m * 9 + 9], rows_[0:9, m * P:(m + 1) * P], C("ident")[0:9, 0:9])
                tick(ins)

            def ada_fill(l, place):
                for i in ada_units(l, place):
                    if i % 2 == 0 and i:
                        ada_turn(*MIXER_ADA[l][i // 2 - 1])
                    ada_unit(*MIXER_ADA[l][i // 2], i % 2)

            def norm():
                b = fill(1, "rms_read")
                for k in range(KD):
                    if k % (KD // 2) == 0:
                        o.need("squares")
                    ins = mm(b[:, 0:NT], C("ones"), hT[:, k, :], start=k == 0, stop=k == KD - 1)
                ins.then_inc(sem("rms_summed"), 1)

            def narrow(w, b, copied):
                b = fill(b, copied)
                for k in range(KD):
                    if k % (KD // 2) == 0:
                        o.need("h_ready")
                    ins = mm(b[0:w.shape[2], 0:NT], w[:, k, :], hT[:, k, :], start=k == 0, stop=k == KD - 1)
                ins.then_inc(sem("small_rows"), 1)

            def narrow_turn(rows_, b, copied, done):
                o.need("small_rows_copied")
                b = fill(b, copied)
                m = rows_.shape[0]
                for g in range(3):
                    n = CH if g < 2 else NS
                    tp(b[0:n, g * m:(g + 1) * m], rows_[:, g * CH:g * CH + n], done if g == 2 else None)

            def small(l):
                if l == 0:
                    pe.wait_ge(sem("small_landed"), 16 * (6 + 5 + 4 + 1))
                narrow(w_small[:, l, :, :], 1, "small_rows_copied")

            def conv_rows(l):
                pe.wait_ge(sem("convrow_landed"), 32 * (l + 1))
                b = fill(2, "convrow_used")
                for i in range(10):
                    tp(b[:, i * 24:i * 24 + 24], convrow[0:24, i * P:(i + 1) * P], "convrow_turned" if i == 9 else None)

            def sums(l):
                o.need("cin_ready")
                b = fill(3, "cum_ready")
                for g in range(NG):
                    mm(b[:, g * 12:g * 12 + 4], C("upper"), cin[:, g, 0:4], start=True, stop=True)
                    mm(b[:, g * 12 + 8:g * 12 + 12], C("upper"), cin[:, g, 8:12], start=True, stop=True)
                    ins = mm(b[:, g * 12 + 4:g * 12 + 8], C("upper"), cin[:, g, 4:8], start=True, stop=g == 0)
                    if g:
                        ins = mm(b[:, g * 12 + 4:g * 12 + 8], C("ones"), cin[:, 0, 4:8], start=False, stop=True)
                ins.then_inc(sem("cum_summed"), 1)

            def spread(col, g):
                return cin[:, g, col:col + 1].broadcast_to([P, P])

            def rows_fox():
                for g in range(NG):
                    b = fill(4 + g, "rows_copied")
                    for h in range(H):
                        ins = mm(b[:, h * CH:(h + 1) * CH], spread(4 + h, g), C("upper"), start=True, stop=g == 0)
                        if g:
                            ins = mm(b[:, h * CH:(h + 1) * CH], spread(4 + h, 0), C("ones"), start=False, stop=True)
                    ins.then_inc(sem("rows_done"), 1)

            def rows(col, b0, done, copied):
                for g in range(NG):
                    b = fill(b0 + g, copied)
                    for h in range(H):
                        ins = mm(b[:, h * CH:(h + 1) * CH], spread(col + h, g), C("upper"), start=True, stop=True)
                    ins.then_inc(sem(done), 1)

            def project(l, slabs):
                for s in slabs:
                    w = use(index[("in", l) + s])[:, 0:KD * s[1]].rearrange("p (k n) -> p k n", k=KD)
                    for m in range(s[1] // P):
                        b = fill(tiles[0] % 2, "tile_copied")
                        for k in range(KD):
                            ins = mm(b[:, 0:NT], w[:, k, m * P:(m + 1) * P], hT[:, k, :], start=k == 0,
                                     stop=k == KD - 1)
                        tick(ins)

            def head_norms(n, src_ready, copied, done):
                o.need(src_ready)
                for i in range(n):
                    b = fill(2 + i, copied)
                    mm(b[:, 0:NT], C("blk"), sq[:, i, :], start=True, stop=True).then_inc(sem(done), 1)

            def tails():
                o.need("tails_packed")
                for c in range(3):
                    b = fill(2 + c, "tail_copied")
                    n = min(4, 10 - 4 * c)
                    for i in range(n):
                        tp(b[0:27, i * P:(i + 1) * P], tail[:, 4 * c + i, :], "turned" if i == n - 1 else None)

            def gdn_scores():
                o.need("gdn_normed")
                for g in range(NG):
                    for r in range(2):
                        b = fill(2 + 2 * g + r, "gdn_scaled")
                        q = slice(r * HD, (r + 1) * HD)
                        for j, first in enumerate((2, 0)):
                            for t in range(2):
                                ins = mm(b[:, (2 * j + t) * CH:(2 * j + t + 1) * CH],
                                         act[q, 2 + t, g * CH:(g + 1) * CH],
                                         act[q, first + t, g * CH:(g + 1) * CH], start=True, stop=True)
                        ins.then_inc(sem("gdn_scored"), 1)

            def gdn_beta_rows():
                for g in range(NG):
                    b = fill(6 + g, "AT_beta")
                    for h in range(H):
                        ins = mm(b[:, h * CH:(h + 1) * CH], beta[:, g, h:h + 1].broadcast_to([P, P]), C("ident"),
                                 start=True, stop=True)
                    ins.then_inc(sem("beta_rows"), 1)

            def gdn_turn():
                for g in range(NG):
                    b = fill(6 + g, "kvt_copied")
                    for i in range(4):
                        tp(b[:, i * P:(i + 1) * P], act[:, 2 + i, g * CH:(g + 1) * CH], "turned" if i == 3 else None)

            def gdn_invert():
                for n, s in enumerate(LEVELS):
                    for g in range(NG):
                        o.need("X_ready")
                        if n == 0:
                            drains["X_ready"] = drains.get("X_ready", 0) + 1
                        b = fill(2 + g, "Q_ready")
                        for h in range(H):
                            ins = mm(b[:, h * CH:(h + 1) * CH], AT[:, g * H + h, :], X[:, g * H + h, :], start=True,
                                     stop=True)
                        ins.then_inc(sem("Q_done"), 1)
                    for g in range(NG):
                        o.need("Q_ready")
                        if n == 0:
                            drains["X_ready"] += 1
                        elif n < len(LEVELS) - 1:
                            b = fill(4 + g, "X_ready")
                            for h in range(H):
                                ins = mm(b[:, h * CH:(h + 1) * CH], XT[:, g * H + h, :], Qs[:, g * H + h, :],
                                         start=True, stop=True)
                            ins.then_inc(sem("XQ_done"), 1)
                        b = fill(6 + g, "XT_ready")
                        for h in range(H):
                            ins = mm(b[:, h * CH:(h + 1) * CH], Qs[:, g * H + h, :], XT[:, g * H + h, :], start=True,
                                     stop=True)
                        ins.then_inc(sem("QX_done"), 1)

            def gdn_chain(l):
                for g in range(NG):
                    o.need("R_ready")
                    pe.wait_ge(sem("XT_ready"), 2 * len(LEVELS) * l + 2 * len(LEVELS) - 1 + g)
                    b = fill(2, "wkT_ready")
                    for t in range(2):
                        for r in range(2):
                            h = 2 * t + r
                            ins = mm(b[r * HD:(r + 1) * HD, t * CH:(t + 1) * CH], Rk[:, g * H + h, :],
                                     XT[:, g * H + h, :], start=True, stop=True)
                    ins.then_inc(sem("wkT_done"), 1)
                    o.need("wkT_ready")
                    if g:
                        pe.wait_ge(sem("S_ready"), 2 * l + 1)
                    for r in range(2):
                        b = fill(4 + r, "w_ready")
                        for t in range(2):
                            h = 2 * t + r
                            ins = mm(b[:, t * HD:(t + 1) * HD], XT[:, g * H + h, :], Rv[:, g * H + h, :], start=True,
                                     stop=g == 0)
                            if g:
                                q = slice(r * HD, (r + 1) * HD)
                                ins = mm(b[:, t * HD:(t + 1) * HD], wkT[q, t, :], S0[q, t, :], start=False, stop=True)
                        ins.then_inc(sem("w_done"), 1)
                    o.need("w_ready", 2)
                    b = fill(3, "oT_ready")
                    for t in range(2):
                        for r in range(2):
                            h = 2 * t + r
                            q = slice(r * HD, (r + 1) * HD)
                            ins = mm(b[q, t * CH:(t + 1) * CH], wtok[:, h, :], decG[:, g * H + h, :], start=True,
                                     stop=g == 0)
                            if g:
                                ins = mm(b[q, t * CH:(t + 1) * CH], S0[q, t, :], qh[q, t, :], start=False, stop=True)
                    ins.then_inc(sem("oT_done"), 1)
                    b = fill(6, "S_ready")
                    for t in range(2):
                        for r in range(2):
                            h = 2 * t + r
                            ins = mm(b[r * HD:(r + 1) * HD, t * HD:(t + 1) * HD], ktail[:, g * H + h, :], wtok[:, h, :],
                                     start=True, stop=True)
                    ins.then_inc(sem("S_done"), 1)

            def ssd(l):
                for g in range(NG):
                    G = slice(g * CH, (g + 1) * CH)
                    for t in range(2):
                        q = slice(t * HD, (t + 1) * HD)
                        b = fill(2 + t, "MT_ready")
                        mm(b[:, 0:CH], act[q, 8, G], act[q, 9, G], start=True, stop=True).then_inc(sem("ssd_scored"), 1)
                    b = fill(4, "xt_copied")
                    for i in range(3):
                        tp(b[:, i * P:(i + 1) * P], act[:, 6 + i, G], "turned" if i == 2 else None)
                    if g == 0:
                        ada_fill(l, "ssd")
                    o.need("MT_ready", 2)
                    o.need("xw_ready")
                    if g:
                        o.need("Cg_ready")
                        pe.wait_ge(sem("hs_ready"), 2 * l + 1)
                    for t in range(2):
                        b = fill(5 + t, "yA_copied")
                        for r in range(2):
                            q = slice(t * HD, (t + 1) * HD)
                            ins = mm(b[r * HD:(r + 1) * HD, 0:CH], xdt[:, 2 * t + r, :], MT[:, g * H + 2 * t + r, :],
                                     start=True, stop=g == 0)
                            if g:
                                ins = mm(b[r * HD:(r + 1) * HD, 0:CH], hs0[q, r, :], Cg[q, r, :], start=False,
                                         stop=True)
                        ins.then_inc(sem("yA_done"), 1)
                    b = fill(7, "hs_ready")
                    for t in range(2):
                        ins = mm(b[t * HD:(t + 1) * HD, 0:P], xt[:, 2, t * HD:(t + 1) * HD],
                                 xw[:, 2 * t:2 * t + 2, :], start=True, stop=True)
                    ins.then_inc(sem("hs_done"), 1)
                o.need("hs_ready", 2)
                tp(fill(4, "hsout_copied")[:, 0:P], hs1[:, :, :], "turned")

            def kv_turn():
                for i in range(4):
                    b = fill(2 + i, "kvp_copied")
                    for g in range(NG):
                        for t in range(2):
                            tp(b[:, g * GW + t * P:g * GW + (t + 1) * P], fm[:, 4 + 2 * i + t, g * CH:(g + 1) * CH],
                               "turned" if g == 1 and t == 1 else None)
                for i in range(3):
                    b = fill(6 + i % 2, "stok_copied")
                    for j in range(4):
                        tp(b[0:NS, j * P:(j + 1) * P], fm[:, 4 * i + j, SEQ:NT], "turned" if j == 3 else None)

            def attention(l):
                o.need("kvp_copied", 4)
                for n in range(8):
                    m, t, r = n // 4, (n % 4) // 2, n % 2
                    q = slice(r * HD, (r + 1) * HD)
                    b = fill(2 + n % 2, "s_read")
                    qq, kk = fm[q, 2 * m + t, :], fm[q, 4 + 2 * m + t, :]
                    mm(b[:, 0:CH], qq[:, 0:CH], kk[:, 0:CH], start=True, stop=True)
                    mm(b[:, CH:3 * CH], qq[:, CH:SEQ], kk[:, 0:SEQ], start=True, stop=True).then_inc(sem("s_done"), 1)
                    ada_fill(l, f"att{n}")
                    if n:
                        attend(n - 1)
                ada_fill(l, "att8")
                attend(7)

            def attend(n):
                m, t, r = n // 4, (n % 4) // 2, n % 2
                o.need("P_ready")
                b = fill(4 + n % 2, "PT_copied")
                for i in range(3):
                    tp(b[:, i * CH:(i + 1) * CH], s3[:, n % 2, i * CH:(i + 1) * CH], "PT_turned" if i == 2 else None)
                o.need("PT_copied")
                b = fill(6 + (n // 2) % 2, "yBD_copied") if r == 0 else bank[6 + (n // 2) % 2]
                q = slice(r * HD, (r + 1) * HD)
                h = 2 * t + r

                def v(g):
                    return kvp[:, (2 + m) * NG + g, h * HD:(h + 1) * HD]
                mm(b[q, 0:CH], v(0), PT[:, n % 2, 0:CH], start=True, stop=True)
                mm(b[q, CH:SEQ], v(0), PT[:, n % 2, CH:2 * CH], start=True, stop=False)
                ins = mm(b[q, CH:SEQ], v(1), PT[:, n % 2, 2 * CH:3 * CH], start=False, stop=True)
                if r:
                    ins.then_inc(sem("yBD_done"), 1)

            def decode_spread():
                for i in range(4):
                    tp(bank[2][0:NS, i * P:(i + 1) * P] if i else fill(2, "dtok_copied")[0:NS, 0:P],
                       act[:, (8, 9, 4, 5)[i], SEQ:NT], "turned" if i == 3 else None)
                o.need("stq_ready")
                b = fill(3, "fmj_copied")
                for j in range(8):
                    for r in range(2):
                        ins = mm(b[r * HD:(r + 1) * HD, j * NS:(j + 1) * NS],
                                 stq[0:NS, 2 * j + r:2 * j + r + 1].broadcast_to([NS, HD]),
                                 C("ident")[0:NS, 0:NS], start=True, stop=True)
                ins.then_inc(sem("fmj_done"), 1)

            def decode_ssd():
                o.need("dtok_copied")
                for j in range(4):
                    b = fill(4 + j % 2, "hst_step")
                    for i in range(2):
                        ins = mm(b[:, i * 256:(i + 1) * 256],
                                 C("one_row")[0:NS, (2 * j + i) * P:(2 * j + i + 1) * P], dtok[0:NS, 0:2, :],
                                 start=True, stop=True)
                    ins.then_inc(sem("bc_rows"), 1)

            def decode_gdn(l):
                vt = dtok[0:NS, 2:4, :]
                for j in range(2):
                    b = fill(6 + j, "v_copied")
                    for i in range(4):
                        for r in range(2):
                            ins = mm(b[r * HD:(r + 1) * HD, i * P:(i + 1) * P],
                                     C("one_row")[0:NS, (4 * j + i) * P:(4 * j + i) * P + HD],
                                     vt[:, :, r * HD:(r + 1) * HD], start=True, stop=True)
                    ins.then_inc(sem("v_rows"), 1)
                ada_fill(l, "v_rows")
                o.need("Sk_ready")
                for j in range(2):
                    b = fill(2 + j, "ks_read")
                    mm(b[:, :], C("blk"), tmpB[:, 8 * j:8 * j + 8, :], start=True, stop=True).then_inc(sem("ks_done"), 1)
                ada_fill(l, "ks")
                o.need("gst_ready")
                b = fill(4, "oTs_copied")
                for t in range(2):
                    for r in range(2):
                        q = slice(r * HD, (r + 1) * HD)
                        for i in range(NS):
                            ins = mm(b[q, t * NS + i:t * NS + i + 1], gst[q, 2 * i + t, :],
                                     act[q, t, SEQ + i:SEQ + i + 1], start=True, stop=True)
                ins.then_inc(sem("oTs_done"), 1)

            def decode_attention(l):
                o.need("stok_copied", 3)
                b = fill(2, "qbc_copied")
                mm(b[:, :], C("own_row")[0:NS, :], stok[0:NS, 0:2, :], start=True, stop=True).then_inc(sem("qbc_done"), 1)
                o.need("lf_ready")
                b = fill(3, "bias_added")
                mm(b[:, 0:H], C("later"), lf[:, 0, :], start=True, stop=False)
                mm(b[:, 0:H], C("own_row")[0:NS, :], nlf[0:NS, 2, :], start=False, stop=True).then_inc(sem("bias_done"), 1)
                ada_fill(l, "keys")
                ada_turn(*MIXER_ADA[l][-1])
                o.need("max_ready")
                b = fill(4, "mcol_ready")
                tp(b[0:8, 0:P], mcol[:, :])
                tp(b[0:8, P:P + NS], sself[0:NS, :], "max_turned")
                o.need("mcol_ready")
                tp(fill(5, "mtok_copied")[0:NS, 0:8], ms8[0:8, 0:NS], "m_turned")
                o.need("mtok_copied")
                b = fill(6, "m_spread_read")
                mm(b[:, 0:8], C("own_row")[0:NS, :], mtok[0:NS, :], start=True, stop=True).then_inc(sem("m_spread"), 1)
                o.need("psums_ready")
                b = fill(7, "rden_ready")
                mm(b[0:NS, 0:8], C("own_col"), psums[:, :], start=True, stop=True).then_inc(sem("den_done"), 1)
                o.need("rden_ready")
                b = fill(2, "Pd_scaled")
                mm(b[:, 0:8], C("own_row")[0:NS, :], rden[0:NS, :], start=True, stop=True).then_inc(sem("rden_spread"), 1)
                b = fill(3, "psb_copied")
                for j in range(4):
                    for r in range(2):
                        ins = mm(b[r * HD:(r + 1) * HD, j * NS:(j + 1) * NS],
                                 sself[0:NS, 2 * j + r:2 * j + r + 1].broadcast_to([NS, HD]),
                                 C("ident")[0:NS, 0:NS], start=True, stop=True)
                ins.then_inc(sem("psb_done"), 1)
                o.need("Pd_ready")
                b = fill(4, "ypv_copied")
                for m in range(2):
                    w = use(index[("v", l, m)])[:, :].rearrange("p (s f) -> p s f", s=SP_)
                    for s in range(SP_):
                        ins = mm(b[0:NS * H, m * GW:(m + 1) * GW], Pd[:, m * SP_ + s, :], w[:, s, :], start=s == 0,
                                 stop=s == SP_ - 1)
                    tick(ins)
                o.need("ypv_copied")
                b = fill(6, "yd_read")
                for j in range(4):
                    tp(b[:, j * NS * H:(j + 1) * NS * H], ypv[0:NS * H, j * P:(j + 1) * P],
                       "ypv_turned" if j == 3 else None)

            def norm2(src, b0, ready, read, done):
                o.need(ready)
                b = fill(b0, read)
                for i in range(2):
                    ins = mm(b[:, 0:NT], C("ones"), sq[:, i, :], start=i == 0, stop=i == 1)
                ins.then_inc(sem(done), 1)

            def w_out(l):
                o.need("yT_ready")
                for c in range(2):
                    w = use(index[("out", l, c)])[:, :].rearrange("p (k n) -> p k n", k=KD)
                    for m in range(4):
                        b = fill(m, "x_added")
                        for k in range(KD):
                            ins = mm(b[:, 0:NT], w[:, k, m * P:(m + 1) * P], yT[:, k, :], start=k == 0, stop=k == KD - 1)
                        tick(ins)

            def three(out, still_high, still_low, high, low, start, stop):
                mm(out, still_high, high, start=start, stop=False)
                mm(out, still_high, low, start=False, stop=False)
                return mm(out, still_low, high, start=False, stop=stop)

            def dense():
                o.need("h_ready", 2)
                for t, (kind, a, col, z, k0, nk) in enumerate(D_PIECES):
                    c = a[0]
                    if kind == "gu":
                        out = bank[2 * col + z]
                        if z == 0 and c:
                            pe.wait_ge(sem("hid_ready"), 2 * c + col - 1)
                        elif z == 0:
                            for other in range(2):
                                pe.wait_ge(*owner[2 * col + other])
                        xh, xl = hH, hL
                    else:
                        q = 4 + (2 * c + col) % 4
                        out = fill(q, "acc_ready") if z == 0 and k0 == 0 else bank[q]
                        k1 = z * (FF // P // 2) + k0
                        if c == 0:
                            pe.wait_ge(sem("f_low"), start_of("f_low") + k1 + nk)
                        xh, xl = fH[:, k1:k1 + nk, :], fL[:, k1:k1 + nk, :]
                    pe.wait_ge(sem("split_low"), start_of("split_low") + 2 + t + 1)
                    split = dense_view(t)[1]
                    for k in range(nk):
                        ins = three(out[:, 0:NT], split(w_high)[:, k, :], split(w_low)[:, k, :], xh[:, k, :],
                                    xl[:, k, :], (kind == "gu" or z == 0) and k0 + k == 0,
                                    (kind == "gu" and k == KD - 1) or (kind == "down" and z == 1
                                                                       and k0 + k == FF // P // 2 - 1))
                    tick(ins)
                for z in range(4):
                    owner[z] = (sem("hid_ready"), FF // P)

            def route():
                narrow(router[:, :, :], 6, "small_rows_copied")
                b = fill(1, "iota_copied")
                mm(b[:, 0:P], C("ones"), C("upper"), start=True, stop=True)
                mm(b[:, P:P + 1], C("upper"), C("ones")[:, 0:1], start=True, stop=True).then_inc(sem("iota_done"), 1)
                narrow_turn(lgT[0:NE, :], 0, "gates_ready", "lg_done")
                for g in range(3):
                    n = CH if g < 2 else NS
                    for half in range(2):
                        b = fill(2 + (2 * g + half) % 4, "htok_copied")
                        for k in range(4):
                            tp(b[0:n, k * P:(k + 1) * P], hT[:, 4 * half + k, g * CH:g * CH + n],
                               "htok_done" if k == 3 else None)
                o.need("gates_ready")
                for e in range(NE):
                    b = fill(e % 4, "gbc_copied")
                    for g in range(3):
                        n = CH if g < 2 else NS
                        ins = mm(b[:, g * CH:g * CH + n], gates[0:n, g, e:e + 1].broadcast_to([n, P]),
                                 C("ident")[0:n, 0:n], start=True, stop=True)
                    ins.then_inc(sem("gbc_done"), 1)
                b = fill(4, "places_read")
                for g in range(3):
                    n = CH if g < 2 else NS
                    mm(b[0:n, g * NE:(g + 1) * NE], C("upper")[0:n, 0:n], rank[0:n, g, :], start=True, stop=g == 0)
                    for before in range(g):
                        mm(b[0:n, g * NE:(g + 1) * NE], C("ones")[:, 0:n], rank[:, before, :], start=False,
                           stop=before == g - 1)
                for g in range(3):
                    n = CH if g < 2 else NS
                    ins = mm(b[:, 3 * NE:4 * NE], C("ones")[0:n, :], rank[0:n, g, :], start=g == 0, stop=g == 2)
                ins.then_inc(sem("places_done"), 1)
                o.need("places_read")
                for e in range(NE):
                    b = fill(e % 4, "pbc_copied")
                    for g in range(3):
                        n = CH if g < 2 else NS
                        ins = mm(b[:, g * CH:g * CH + n], place[0:n, g, e:e + 1].broadcast_to([n, P]),
                                 C("ident")[0:n, 0:n], start=True, stop=True)
                    ins.then_inc(sem("pbc_done"), 1)
                for z in range(8):
                    pe.wait_ge(*owner[z])

            def experts():
                base = [slot_count[s] for s in range(NSLOT)]
                hid0, acc0, kt = FF // P, KD, FE // P

                def gather(z, r, q):
                    first = isinstance(r, int) and isinstance(q, int)
                    pe.wait_ge(sem("G_ready"), pair_count("G_ready", 1, r, q, 1))
                    if z >= 2:
                        pe.wait_ge(sem("hc_copied"), pair_count("hc_copied", 4, r, q, z - 1))
                    elif not first:
                        pe.wait_ge(sem("hc_copied"), count(start_of("hc_copied") - 4, 4, 4, r, q, z + 3, PAIRS))
                    for i in range(2):
                        for g in range(3):
                            n = CH if g < 2 else NS
                            k = 2 * z + i
                            ins = mm(bank[6 + z % 2][:, i * 2 * CAP:(i + 1) * 2 * CAP],
                                     htok[0:n, g, k * P:(k + 1) * P], G[0:n, g, :, :], start=g == 0, stop=g == 2)
                    ins.then_inc(sem("hc_done"), 1)

                def turn(r, e, c):
                    pe.wait_ge(sem("hid_ready"), count(hid0, kt // 2, 0, r, e, c + 1))
                    if c >= 2:
                        pe.wait_ge(sem("hidT_copied"), count(start_of("hidT_copied"), kt // 2, 0, r, e, c - 1))
                    else:
                        pe.wait_ge(sem("acc_ready"), count(acc0, KD, 0, r, e, c - 1))
                    for i in range(2):
                        ins = pe.transpose(bank[2 + c % 2][:, i * CAP:(i + 1) * CAP],
                                           hidc[0:CAP, c % 2, i * P:(i + 1) * P], C("ident")[0:CAP, 0:CAP])
                    ins.then_inc(sem("hidT_done"), 1)

                def scatter(r, e, d):
                    pe.wait_ge(sem("yc_ready"), count(start_of("yc_ready"), E_DN, 0, r, e, d // 2 + 1))
                    if d >= 4:
                        pe.wait_ge(sem("acc_ready"), count(acc0, KD, 0, r, e, d - 3))
                    mm(bank[d % 4][:, 0:NT], yc[0:CAP, d * P:(d + 1) * P], GwT[0:CAP, :], start=True,
                       stop=True).then_inc(sem("part_done"), 1)

                def one_round(r):
                    for z in range(4):
                        gather(z, r, 0)
                    with pe.Fori(0, PAIRS) as p:
                        for j, (t, (i, kind, c, k0, nk)) in product(range(2), enumerate(E_PIECES)):
                            e = p * 2 + j
                            last = t + 1 == e_ticks[i]
                            if kind == "gu" and k0 == 0:
                                if c == 0 and j == 0:
                                    pe.wait_ge(sem("hc_copied"), pair_count("hc_copied", 4, r, p, 4))
                                if c >= 2:
                                    pe.wait_ge(sem("hid_ready"), count(hid0, kt // 2, 0, r, e, c - 1))
                                else:
                                    pe.wait_ge(sem("acc_ready"), count(acc0, KD, 0, r, e, c - 3))
                            if kind == "down":
                                if c == 0:
                                    pe.wait_ge(sem("hidT_copied"),
                                               count(start_of("hidT_copied"), kt // 2, 0, r, e, (k0 + nk) // 2))
                                if k0 == 0:
                                    pe.wait_ge(sem("yc_ready"), count(start_of("yc_ready"), E_DN, 0, r, e, c - 1))
                            pe.wait_ge(sem("w_low_ready"), count(start_of("w_low_ready"), E_TICKS, 0, r, e, t + 1))
                            split = piece_view(t, e_slot[i])[1]
                            for k in range(nk):
                                if kind == "gu":
                                    out = bank[c % 2][0:CAP, :]
                                    own = slice(j * CAP, (j + 1) * CAP)
                                    high, low = hcH[:, k0 + k, own], hcL[:, k0 + k, own]
                                    wh, wl = split(w_high)[:, :, k, :], split(w_low)[:, :, k, :]
                                else:
                                    out = bank[4 + c % 2][0:CAP, 0:256]
                                    high, low = hidH[:, k0 + k, :], hidL[:, k0 + k, :]
                                    wh, wl = split(w_high)[:, k, :], split(w_low)[:, k, :]
                                ins = three(out, high, low, wh, wl, k0 + k == 0, last and k == nk - 1)
                            ins.then_inc(tile_done, 1)
                            if kind == "gu" and last and c:
                                turn(r, e, c - 1)
                                if c == E_GU - 1 and j:
                                    gather(0, r, p + 1)
                                    gather(1, r, p + 1)
                            if kind == "down" and c == 0 and k0 == 4:
                                turn(r, e, E_GU - 1)
                            if kind == "down" and last:
                                if c:
                                    for d in (2 * c - 2, 2 * c - 1):
                                        scatter(r, e, d)
                                if c >= E_DN - 2 and j:
                                    gather(c, r, p + 1)
                                if c == E_DN - 1:
                                    for d in (2 * c, 2 * c + 1):
                                        scatter(r, e, d)

                all_rounds(pe, one_round)

            def finish():
                o.need("x_final")
                for g in range(3):
                    n = CH if g < 2 else NS
                    for half in range(2):
                        b = fill((2 * g + half) % 4, "out_copied")
                        for k in range(4):
                            tp(b[0:n, k * P:(k + 1) * P], xT[:, 4 * half + k, g * CH:g * CH + n],
                               "out_turned" if k == 3 else None)

            start_c()
            o.need("c_copied")
            for c in range(MIX_CHUNKS):
                if c == 2:
                    start()
                if c == 3:
                    norm()
                for half in range(2):
                    ada_unit(0, c, half)
                ada_turn(0, c)
            for l in range(DEPTH):
                if l:
                    norm()
                for half in range(2):
                    ada_unit(*NORM_ADA["mix", l], half)
                small(l)
                conv_rows(l)
                ada_turn(*NORM_ADA["mix", l])
                narrow_turn(sq[0:16, 3, :], 3, "small_copied", "small_done")
                project(l, G_SLABS)
                sums(l)
                rows_fox()
                project(l, S_SLABS)
                head_norms(4, "head_squares", "head_ss_read", "head_ss")
                project(l, F_SLABS)
                tails()
                head_norms(4, "head_squares", "head_ss_read", "head_ss")
                project(l, M_SLABS)
                head_norms(4, "head_squares", "head_ss_read", "head_ss")
                rows(8, 6, "rows_done", "rows_copied")
                ada_fill(l, "gdn")
                gdn_scores()
                gdn_beta_rows()
                gdn_turn()
                gdn_invert()
                gdn_chain(l)
                rows(0, 6, "rows_done", "rows_copied")
                ssd(l)
                kv_turn()
                attention(l)
                decode_spread()
                decode_ssd()
                decode_gdn(l)
                decode_attention(l)
                norm2(yA, 5, "head_squares", "head_ss_read", "head_ss")
                head_norms(2, "head_squares", "head_ss_read", "head_ss")
                w_out(l)
                norm()
                if l == 0:
                    for half in range(2):
                        ada_unit(*NORM_ADA["ffn", l], half)
                    ada_turn(*NORM_ADA["ffn", l])
                    dense()
                else:
                    route()
                    experts()
            finish()

        @block.scalar
        def _(act_e):
            o = Order(act_e, "act_chain")
            A_ = act_e.activation

            def copy(out, in_, name=None):
                o.go(A_(out, in_, ACT.Copy), name)

            def rms(src, dst, scale, read, eps=EPS):
                o.go(A_(dst, src, ACT.Ln, bias=epsc[:, 0:1], scale=scale), read)
                o.settle()
                return A_(dst, dst, ACT.Exp, scale=-0.5)

            def mod_rows(l, c):
                i = index[("ada", l, c)]
                act_e.wait_ge(tile_done, ticks_before(i) + 1)
                copy(ring[slot_of[i]][0:9, 0:512], bank[0][0:9, :], "mod_rows")

            def mod_columns(l, c):
                act_e.wait_ge(tile_done, done_at[index[("ada", l, c)]])
                copy(modT[:, 4 * c:4 * c + 4, :], bank[1][:, 0:36].rearrange("p (m j) -> p m j", m=4), "mod_ready")

            def ada_drain(l, place):
                for i in ada_units(l, place):
                    if i % 2 == 0 and i:
                        mod_columns(*MIXER_ADA[l][i // 2 - 1])
                    if i % 2:
                        mod_rows(*MIXER_ADA[l][i // 2])

            def norm():
                act_e.wait_ge(sem("x_copied1"), 4)
                o.need("x_whole")
                for k in (0, KD // 2):
                    o.go(A_(hT[:, k:k + KD // 2, :], xT[:, k:k + KD // 2, :], ACT.Square), "squares")
                o.need("rms_summed")
                o.go(rms(bank[1][:, 0:NT], rstd[:, 0, :], 1.0 / D, "rms_read"), "rstd_ready")

            act_e.wait_ge(sem("c_landed"), 48)
            o.go(A_(cstage[0:9, :], cstage[0:9, :], ACT.Silu), "c_silu")
            o.need("turned")
            copy(cT[:, :, :], bank[2][:, 0:72].rearrange("p (k n) -> p k n", k=KD), "c_copied")
            for c in range(MIX_CHUNKS):
                if c == 2:
                    for k in range(0, KD, 2):
                        act_e.wait_ge(sem("x_turned"), k + 1)
                        copy(xT[:, k, :], bank[3 + k % 4][:, 0:NT], "x_copied0")
                if c == 3:
                    norm()
                mod_rows(0, c)
                mod_columns(0, c)
            act_e.wait_ge(sem("small_landed"), 256)
            o.go(A_(nega[:, :, :], alog[:, :, :], ACT.Exp), "nega_exp")

            dst_of = {}
            for l in range(DEPTH):
                order = [("u", i) for i in range(6)] + [("z", 2), ("z", 3), ("z", 0), ("z", 1)]
                order += [("u", i) for i in (6, 7, 8, 9)]
                order += [("f", i) for i in (0, 1, 4, 5, 8, 9)] + [("f", i) for i in (2, 3, 6, 7, 10, 11)]
                dst_of[l] = order

            def drain(l, first, n):
                i0 = ticks_before(index[("in", l) + IN_SLABS[0]])
                for j in range(first, first + n):
                    act_e.wait_ge(tile_done, i0 + j + 1)
                    b = bank[(i0 + j) % 2]
                    kind, i = dst_of[l][j]
                    if kind == "u":
                        o.go(A_(u[:, i, 3:3 + SEQ], b[:, 0:SEQ], ACT.Copy))
                        copy(u[:, i, 3 + SEQ + 3:UW:CW], b[:, SEQ:NT], "tile_copied")
                    elif kind == "z":
                        copy(zz[:, i, :], b[:, 0:NT], "tile_copied")
                    else:
                        copy(fm[:, i, :], b[:, 0:NT], "tile_copied")

            def head_rms(n, done, read, ready, scale):
                for i in range(n):
                    o.need(done)
                    o.go(rms(bank[2 + i][:, 0:NT], rstd[:, i, :], scale, read), ready)

            for l in range(DEPTH):
                if l:
                    norm()
                mod_rows(*NORM_ADA["mix", l])
                o.need("small_rows")
                copy(sq[0:16, 3, :], bank[1][0:16, 0:NT], "small_rows_copied")
                mod_columns(*NORM_ADA["mix", l])
                o.need("sma_ready")
                o.go(A_(sme[:, :, :], sma[:, :, :], ACT.Exp, scale=-1.0))
                o.go(A_(beta[:, :, :], sm[:, :, 8:12], ACT.Exp, scale=-1.0))
                o.settle()
                o.go(A_(sme[:, :, :], sme[:, :, :], ACT.Ln, bias=1.0), "softplus_ln")
                drain(l, 0, 8)
                for g in range(NG):
                    o.need("rows_done")
                    copy(rowF[:, :, g * CH:(g + 1) * CH], bank[4 + g][:, :].rearrange("p (h i) -> p h i", h=H),
                         "rows_copied")
                def silus(first, n):
                    for i in range(first, first + n):
                        o.need("cv_ready")
                        o.go(A_(act[:, i, 0:SEQ], cv[:, i % 2, 0:SEQ], ACT.Silu))
                        o.go(A_(act[:, i, SEQ:NT], cv[:, i % 2, SEQ + 3:CVW:CW], ACT.Silu), "cv_used")
                for i in range(6):
                    silus(i, 1)
                    drain(l, 8 + i, 1)
                o.settle()
                o.go(A_(sq[:, :, :], act[:, 0:4, :], ACT.Square), "head_squares")
                head_rms(4, "head_ss", "head_ss_read", "head_rstd", 1.0)
                for i in range(4):
                    silus(6 + i, 1)
                    drain(l, 14 + i, 1)
                drain(l, 18, 2)
                for c in range(3):
                    o.need("turned")
                    n = min(512, 1280 - 512 * c)
                    copy(convrow[0:27, c * 512:c * 512 + n], bank[2 + c][0:27, 0:n], "tail_copied")
                o.go(A_(zz[:, :, :], zz[:, :, :], ACT.Silu), "zz_ready")
                o.settle()
                o.need("gdn_normed")
                o.go(A_(sq[:, 0:2, :], fm[:, 0:2, :], ACT.Square))
                o.go(A_(sq[:, 2:4, :], fm[:, 4:6, :], ACT.Square), "head_squares")
                head_rms(4, "head_ss", "head_ss_read", "head_rstd", 1.0 / HD)
                drain(l, 20, 6)
                o.settle()
                o.need("fm_normed")
                o.go(A_(sq[:, 0:2, :], fm[:, 2:4, :], ACT.Square))
                o.go(A_(sq[:, 2:4, :], fm[:, 6:8, :], ACT.Square), "head_squares")
                head_rms(4, "head_ss", "head_ss_read", "head_rstd", 1.0 / HD)

                for g in range(NG):
                    o.need("rows_done")
                    copy(egG[:, g * H:(g + 1) * H, :], bank[6 + g][:, :].rearrange("p (h i) -> p h i", h=H),
                         "rows_copied")
                o.need("decG_diff")
                o.go(A_(decG[:, :, :], decG[:, :, :], ACT.Exp))
                o.go(A_(egG[:, :, :], egG[:, :, :], ACT.Exp))
                o.go(A_(be[:, :, :], cum[:, :, 8:12], ACT.Exp))
                o.go(A_(sc4[:, :, :], sc4[:, :, :], ACT.Exp), "decG_ready")
                ada_drain(l, "gdn")
                for g in range(NG):
                    o.need("turned")
                    copy(kvt[:, g * 4:(g + 1) * 4, :], bank[6 + g][:, :].rearrange("p (i j) -> p i j", i=4),
                         "kvt_copied")
                for g in range(NG):
                    o.need("wkT_done")
                    o.go(A_(wkT[:, :, :], bank[2][:, 0:SEQ].rearrange("p (t i) -> p t i", t=2), ACT.Copy, scale=-1.0),
                         "wkT_ready")
                    for r in range(2):
                        o.need("w_done")
                        copy(wtok[:, r::2, :], bank[4 + r][:, 0:P].rearrange("p (t d) -> p t d", t=2), "w_ready")
                    o.need("oT_done")
                    copy(oT[:, :, g * CH:(g + 1) * CH], bank[3][:, 0:SEQ].rearrange("p (t i) -> p t i", t=2),
                         "oT_ready")

                for g in range(NG):
                    o.need("rows_done")
                    if g == 0:
                        o.need("phase2")
                    copy(egS[:, g * H:(g + 1) * H, :], bank[6 + g][:, :].rearrange("p (h i) -> p h i", h=H),
                         "rows_copied")
                o.need("MT_diff")
                o.go(A_(MT[:, :, :], MT[:, :, :], ACT.Exp))
                o.go(A_(egS[:, :, :], egS[:, :, :], ACT.Exp))
                o.go(A_(ws[:, :, :], ws[:, :, :], ACT.Exp), "decS_ready")
                for g in range(NG):
                    o.need("turned")
                    if g:
                        act_e.wait_ge(sem("hs_ready"), 2 * l + 1)
                    copy(xt[:, :, :], bank[4][:, 0:3 * P].rearrange("p (i j) -> p i j", i=3), "xt_copied")
                    if g == 0:
                        ada_drain(l, "ssd")
                o.need("turned")
                copy(hsout[:, :], bank[4][:, 0:P], "hsout_copied")
                for i in range(4):
                    o.need("turned")
                    copy(kvp[:, i * NG:(i + 1) * NG, :], bank[2 + i][:, :].rearrange("p (g f) -> p g f", g=NG),
                         "kvp_copied")
                for i in range(3):
                    o.need("turned")
                    copy(stok[0:NS, 2 * i:2 * i + 2, :], bank[6 + i % 2][0:NS, :].rearrange("p (a f) -> p a f", a=2),
                         "stok_copied")
                def soften(n):
                    o.need("nmx_ready")
                    o.go(A_(s3[:, n % 2, 0:CH], s3[:, n % 2, 0:CH], ACT.Exp, bias=nmx[:, n, 0:1],
                            accum_out=rsum[:, n, 0:1]))
                    o.go(A_(s3[:, n % 2, CH:], s3[:, n % 2, CH:], ACT.Exp, bias=nmx[:, n, 1:2],
                            accum_out=rsum[:, n, 1:2]), "exp_done")

                def copy_pt(n):
                    o.need("PT_turned")
                    copy(PT[:, n % 2, :], bank[4 + n % 2][:, 0:3 * CH], "PT_copied")
                    if n % 2:
                        o.need("yBD_done")
                        m, t = n // 4, (n % 4) // 2
                        copy(yT[:, (2, 6)[m] + t, 0:SEQ], bank[6 + (n // 2) % 2][:, 0:SEQ], "yBD_copied")
                for n in range(8):
                    soften(n)
                    ada_drain(l, f"att{n}")
                    if n:
                        copy_pt(n - 1)
                ada_drain(l, "att8")
                copy_pt(7)

                o.need("stq_logs")
                o.go(A_(stq[0:NS, 4:12], stq[0:NS, 4:12], ACT.Exp), "stq_ready")
                o.need("turned")
                copy(dtok[0:NS, :, :], bank[2][0:NS, :].rearrange("p (i j) -> p i j", i=4), "dtok_copied")
                o.need("fmj_done")
                copy(fmj[:, :, :], bank[3][:, 0:8 * NS].rearrange("p (j b) -> p j b", j=8), "fmj_copied")
                o.need("tmpA_free")
                for j in range(2):
                    o.need("v_rows")
                    copy(tmpA[:, 8 * j:8 * j + 8, :], bank[6 + j][:, :].rearrange("p (a d) -> p a d", a=8), "v_copied")
                ada_drain(l, "v_rows")
                ada_drain(l, "ks")
                o.need("oTs_done")
                copy(oT[:, :, SEQ:NT], bank[4][:, 0:2 * NS].rearrange("p (t b) -> p t b", t=2), "oTs_copied")
                o.need("qbc_done")
                copy(qbc[:, :, :], bank[2][:, :].rearrange("p (m f) -> p m f", m=2), "qbc_copied")
                ada_drain(l, "keys")
                mod_columns(*MIXER_ADA[l][-1])
                o.need("m_spread_read")
                o.go(A_(scd[:, :, :], scd[:, :, :], ACT.Exp))
                o.go(A_(sself[0:NS, :], sself[0:NS, :], ACT.Exp), "scd_exp")
                o.need("psb_done")
                copy(psb[:, :, :], bank[3][:, 0:4 * NS].rearrange("p (j b) -> p j b", j=4), "psb_copied")
                act_e.wait_ge(tile_done, done_at[index[("v", l, 1)]])
                copy(ypv[0:NS * H, :], bank[4][0:NS * H, :], "ypv_copied")

                o.need("yA_gated")
                o.go(A_(sq[:, 0:2, :], yA[:, :, :], ACT.Square), "head_squares")
                o.need("head_ss")
                o.go(rms(bank[5][:, 0:NT], rstd[:, 2, :], 1.0 / GW, "head_ss_read"), "head_rstd")
                o.settle()
                o.go(A_(sq[:, 0:2, :], oT[:, :, :], ACT.Square), "head_squares")
                for i in range(2):
                    o.need("head_ss")
                    o.go(rms(bank[2 + i][:, 0:NT], rstd[:, i, :], 1.0 / HD, "head_ss_read"), "head_rstd")
                norm()
                if l == 0:
                    mod_rows(*NORM_ADA["ffn", l])
                    mod_columns(*NORM_ADA["ffn", l])
                    t0 = ticks_before(index[("gu", 0, 0)])
                    act_e.wait_ge(sem("ffn_phase"), 1)
                    for half in range(2):
                        act_e.wait_ge(sem("h_ready"), 2 + half + 1)
                        copy(hH[:, 4 * half:4 * half + 4, :], hT[:, 4 * half:4 * half + 4, :], "split_high")
                    for t, (kind, a, col, z, k0, nk) in enumerate(D_PIECES):
                        i = index[(kind, 0) + a]
                        act_e.wait_ge(landed[slot_of[i]], landed_at[i])
                        if t >= SPLITS:
                            act_e.wait_ge(tile_done, t0 + t + 1 - SPLITS)
                        src, split = dense_view(t)
                        copy(split(w_high), src, "split_high")
                        if t in f_made:
                            f = f_made[t]
                            act_e.wait_ge(tile_done, t0 + 2 * f + 1)
                            if f >= 2:
                                act_e.wait_ge(sem("hid_ready"), f - 1)
                            o.go(A_(sg[:, f % 2, :], bank[2 * (f % 2)][:, 0:NT], ACT.Silu), "sg_ready")
                        if t in f_split:
                            f = f_split[t]
                            act_e.wait_ge(sem("hid_ready"), f + 1)
                            copy(fH[:, f, :], ft[:, f % 2, :], "f_high")
                else:
                    act_e.wait_ge(sem("ffn_phase"), 2)
                    o.need("small_rows")
                    copy(lgT[0:NE, :], bank[6][0:NE, 0:NT], "small_rows_copied")
                    o.need("iota_done")
                    o.go(A_(iota[:, :], bank[1][:, 0:P], ACT.Copy))
                    copy(iota_col[:, :], bank[1][:, P:P + 1], "iota_copied")
                    for i in range(6):
                        n = CH if i < 4 else NS
                        o.need("htok_done")
                        copy(htok[0:n, i // 2, i % 2 * 512:i % 2 * 512 + 512], bank[2 + i % 4][0:n, :], "htok_copied")
                    o.need("lg_shift")
                    o.go(A_(gates[:, :, :], lg[:, :, :], ACT.Exp), "lg_exp")
                    for e in range(NE):
                        o.need("gbc_done")
                        copy(gbc[:, e, :], bank[e % 4][:, 0:NT], "gbc_copied")
                    for e in range(NE):
                        o.need("pbc_done")
                        copy(pbc[:, e, :], bank[e % 4][:, 0:NT], "pbc_copied")

                    base = [slot_count[s] for s in range(NSLOT)]

                    def drain_tokens(z, r, q):
                        act_e.wait_ge(sem("hc_done"), pair_count("hc_done", 4, r, q, z + 1))
                        A_(hcH[:, 2 * z:2 * z + 2, :],
                           bank[6 + z % 2][:, 0:4 * CAP].rearrange("p (k c) -> p k c", k=2),
                           ACT.Copy).then_inc(sem("hc_high"), 1)

                    def drain_turned(r, e, c):
                        act_e.wait_ge(sem("hidT_done"), count(start_of("hidT_done"), E_GU, 0, r, e, c + 1))
                        A_(hidH[:, 2 * c:2 * c + 2, :],
                           bank[2 + c % 2][:, 0:2 * CAP].rearrange("p (i c) -> p i c", i=2),
                           ACT.Copy).then_inc(sem("hidT_high"), 1)

                    def drain_down(r, e, c):
                        act_e.wait_ge(tile_done, count(ticks_pre, E_TICKS, 0, r, e, e_ticks[E_GU + c]))
                        act_e.wait_ge(sem("part_done"), count(start_of("part_done"), KD, 0, r, e, 0))
                        A_(yc[0:CAP, c * 256:(c + 1) * 256], bank[4 + c % 2][0:CAP, 0:256], ACT.Copy).then_inc(
                            sem("yc_ready"), 1)

                    def one_round(r):
                        for z in range(4):
                            drain_tokens(z, r, 0)
                        with act_e.Fori(0, PAIRS) as p:
                            for j, (t, (i, kind, c, k0, nk)) in product(range(2), enumerate(E_PIECES)):
                                e = p * 2 + j
                                if k0 == 0:
                                    s = e_slot[i]
                                    act_e.wait_ge(landed[s], count(base[s], per_slot[s], 0, r, e, e_landed[i]))
                                act_e.wait_ge(tile_done, count(ticks_pre, E_TICKS, 0, r, e, t + 1 - SPLITS))
                                src, split = piece_view(t, e_slot[i])
                                A_(split(w_high), src, ACT.Copy).then_inc(sem("w_high_ready"), 1)
                                if t in gu_read:
                                    c = gu_read[t]
                                    act_e.wait_ge(sem("hid_ready"), count(FF // P, E_GU, 0, r, e, max(c - 1, 0)))
                                    act_e.wait_ge(tile_done, count(ticks_pre, E_TICKS, 0, r, e, e_ticks[c]))
                                    A_(sgc[0:CAP, c % 2, :], bank[c % 2][0:CAP, 0:256], ACT.Silu).then_inc(
                                        sem("sg_ready"), 1)
                                    if c == E_GU - 1 and j:
                                        drain_tokens(0, r, p + 1)
                                        drain_tokens(1, r, p + 1)
                                if t in turned_read:
                                    drain_turned(r, e, turned_read[t])
                                if t in down_read:
                                    drain_down(r, e, down_read[t])
                                    if down_read[t] == E_DN - 2 and j:
                                        drain_tokens(2, r, p + 1)
                                if t == E_TICKS - 1:
                                    drain_down(r, e, E_DN - 1)
                                    if j:
                                        drain_tokens(3, r, p + 1)

                    all_rounds(act_e, one_round)
            for i in range(6):
                g, half = i // 2, i % 2
                n = CH if g < 2 else NS
                act_e.wait_ge(sem("out_turned"), i + 1)
                if i == 0:
                    act_e.wait_ge(sem("x_final"), 1)
                A_(stage[0:n, g, half * 512:half * 512 + 512], bank[i % 4][0:n, :], ACT.Copy).then_inc(
                    sem("out_copied"), 1)

        @block.vector
        def _(ve):
            o = Order(ve, "ve_chain")
            TT, TS, STT, CP, RED = (ve.tensor_tensor, ve.tensor_scalar, ve.scalar_tensor_tensor, ve.tensor_copy,
                                    ve.tensor_reduce)

            def v(ins, name=None):
                o.go(ins, name)

            def vs(ins, name=None):
                o.go(ins, name)
                o.settle()

            vs(ve.memset(epsc[:, :], EPS))
            vs(ve.memset(brow[:, :, 8:12], 0.0))
            ve.wait_ge(sem("start_landed"), 16 * STARTS)
            o.need("params_turned", 1)
            v(CP(prm1[:, :], bank[7][:, 0:P]), "params_used")
            for k in range(1, KD, 2):
                ve.wait_ge(sem("x_turned"), k + 1)
                v(CP(xT[:, k, :], bank[3 + k % 4][:, 0:NT]), "x_copied1")
            o.need("params_turned", 1)
            v(CP(prm2[:, :], bank[2][:, 0:102]), "params_used")
            ve.wait_ge(sem("x_copied0"), 4)
            vs(ve.memset(sq[:, 0, 0:1], 0.0), "x_whole")
            ve.wait_ge(sem("small_landed"), 256)
            o.need("nega_exp")
            vs(TS(nega[:, :, :], nega[:, :, :], -1.0, None, ALU.mult))

            def col(m, part=slice(0, P)):
                return modT[part, m, 0:1]

            def modulate(first_shift, gains):
                v(STT(gain1[:, :, :], modT[:, first_shift + 8:first_shift + 16, :], 1.0,
                      gains.unsqueeze(2).broadcast_to([P, KD, 9]), ALU.add, ALU.mult))
                o.need("rstd_ready")
                for half in (slice(0, KD // 2), slice(KD // 2, KD)):
                    vs(TT(hT[:, half, :], xT[:, half, :], rstd[:, 0:1, :].broadcast_to([P, KD // 2, NT]), ALU.mult))
                    for k in range(half.start, half.stop):
                        v(TS(hT[:, k, 0:SEQ], hT[:, k, 0:SEQ], gain1[:, k, 0:1], modT[:, first_shift + k, 0:1],
                             ALU.mult, ALU.add))
                    vs(TT(hT[:, half, SEQ:NT], hT[:, half, SEQ:NT], gain1[:, half, 1:9], ALU.mult))
                    v(TT(hT[:, half, SEQ:NT], hT[:, half, SEQ:NT],
                         modT[:, first_shift + half.start:first_shift + half.stop, 1:9], ALU.add), "h_ready")

            def add_bias(l, lo, hi):
                ve.wait_ge(sem("mod_ready"), hi // 4 + ADA_CHUNKS * l)
                vs(TT(modT[:, lo:hi, :], modT[:, lo:hi, :],
                      prm1[:, 48 * l + lo:48 * l + hi].unsqueeze(2).broadcast_to([P, hi - lo, 9]), ALU.add))

            def convolve(l, first, n, w0, wn, bias):
                p0 = 46 * l
                for i in range(first, first + n):
                    j = i - first
                    if not (l == 0 and i < 2):
                        o.need("cv_used")
                    c = cv[:, i % 2, :]
                    w = [prm2[:, p0 + w0 + wn * k + j:p0 + w0 + wn * k + j + 1] for k in range(CW)]
                    if bias is None:
                        vs(TS(c, u[:, i, 0:CVW], w[0], None, ALU.mult))
                    else:
                        vs(TS(c, u[:, i, 0:CVW], w[0], prm2[:, p0 + bias + j:p0 + bias + j + 1], ALU.mult, ALU.add))
                    for k in range(1, CW):
                        if k < CW - 1:
                            vs(STT(c, u[:, i, k:k + CVW], w[k], c, ALU.mult, ALU.add))
                        else:
                            v(STT(c, u[:, i, k:k + CVW], w[k], c, ALU.mult, ALU.add), "cv_ready")

            def qk_norm(tiles, gains, name):
                for j, i in enumerate(tiles):
                    o.need("head_rstd")
                    v(STT(fm[:, i, :], fm[:, i, :], gains[j], rstd[:, j, :], ALU.mult, ALU.mult), name if j == 3 else None)

            for l in range(DEPTH):
                heads = 92 + 5 * l
                add_bias(l, 0, 4 * MIX_CHUNKS)
                if l == 0:
                    for ll in range(DEPTH):
                        v(TS(prm2[:, 92 + 5 * ll:94 + 5 * ll], prm2[:, 92 + 5 * ll:94 + 5 * ll], HD ** -0.5, None,
                             ALU.mult))
                modulate(0, prm1[:, 96 + 8 * l:104 + 8 * l])
                if l == 0:
                    v(ve.memset(u[:, :, 0:3], 0.0))
                    v(ve.memset(sm[:, 2, :], 0.0))
                else:
                    ve.wait_ge(sem("stored"), 16 * STORES)
                    v(ve.memset(u[:, :, 0:3], 0.0))
                    v(ve.memset(sm[:, 2, :], 0.0))
                o.need("small_done")
                o.settle()
                v(CP(sm[:, 0:2, :], bank[3][:, 0:32].rearrange("p (g c) -> p g c", g=2)))
                vs(CP(sm[0:NS, 2, :], bank[3][0:NS, 32:48]), "small_copied")
                vs(TT(sm[:, :, :], sm[:, :, :], brow[:, l, :].unsqueeze(1).broadcast_to([P, 3, 16]), ALU.add))
                vs(TS(sm[:, :, 4:8], sm[:, :, 4:8], -1.0, None, ALU.mult))
                vs(STT(sma[:, :, :], sm[:, :, :], -1.0, sm[:, :, :], ALU.mult, ALU.max), "sma_ready")
                o.need("softplus_ln")
                vs(STT(smp[:, :, :], sm[:, :, :], 0.0, sme[:, :, :], ALU.max, ALU.add))
                vs(TS(beta[:, :, :], beta[:, :, :], 1.0, None, ALU.add))
                v(ve.reciprocal(beta[:, :, :], beta[:, :, :]))
                v(TT(cin[:, :, 0:4], smp[:, :, 0:4], nega[:, l, 0:4].unsqueeze(1).broadcast_to([P, 3, 4]), ALU.mult))
                v(TT(cin[:, :, 8:12], smp[:, :, 12:16], nega[:, l, 4:8].unsqueeze(1).broadcast_to([P, 3, 4]), ALU.mult))
                v(TS(nlf[:, :, :], smp[:, :, 4:8], -1.0, None, ALU.mult))
                v(CP(cin[:, :, 4:8], smp[:, :, 4:8]), "cin_ready")
                o.need("convrow_turned")
                v(CP(u[:, :, 3 + SEQ:UW].rearrange("p i (b k) -> p i b k", k=CW)[:, :, :, 0:3],
                     bank[2][:, 0:240].rearrange("p (i b k) -> p i b k", i=10, k=3)), "convrow_used")
                ve.wait_ge(sem("tile_copied"), 26 * l + 6)
                o.settle()
                convolve(l, 0, 6, 22, 6, None)
                o.need("cum_summed")
                v(CP(cum[:, :, :], bank[3][:, 0:24].rearrange("p (g c) -> p g c", g=NG)), "cum_ready")
                ve.wait_ge(sem("tile_copied"), 26 * l + 14)
                convolve(l, 6, 4, 2, 4, 18)
                v(CP(tail[:, :, 0:3], u[:, :, SEQ:SEQ + 3]))
                v(CP(tail[:, :, 3:27].rearrange("p i (b k) -> p i b k", k=3),
                     u[:, :, 3 + SEQ:UW].rearrange("p i (b k) -> p i b k", k=CW)[:, :, :, 1:4]), "tails_packed")
                for i in range(4):
                    o.need("head_rstd")
                    if i < 2:
                        v(STT(act[:, i, :], act[:, i, :], HD ** -0.5, rstd[:, i, :], ALU.mult, ALU.mult))
                    else:
                        v(TT(act[:, i, :], act[:, i, :], rstd[:, i, :], ALU.mult),
                          "gdn_normed" if i == 3 else None)
                g_ = [prm2[:, heads + i:heads + i + 1] for i in range(5)]
                qk_norm((0, 1, 4, 5), (g_[0], g_[0], g_[2], g_[2]), "fm_normed")
                qk_norm((2, 3, 6, 7), (g_[1], g_[1], g_[3], g_[3]), None)

                o.need("rows_copied", NG)
                for g in range(NG):
                    o.need("rows_copied")
                    for h in range(H):
                        v(STT(decG[:, g * H + h, :], egG[:, g * H + h, :], cum[:, g, 8 + h:9 + h], C("causal_t"),
                              ALU.subtract, ALU.add), None)
                for g in range(NG):
                    v(TT(sc4[:, g, :], egG[:, g * H:(g + 1) * H, CH - 1], cum[:, g, 8:12], ALU.subtract),
                      "decG_diff" if g else None)
                o.need("decG_ready")
                for g in range(NG):
                    o.need("beta_rows")
                    v(TT(AT[:, g * H:(g + 1) * H, :], decG[:, g * H:(g + 1) * H, :],
                         bank[6 + g][:, :].rearrange("p (h i) -> p h i", h=H), ALU.mult), "AT_beta")
                o.settle()
                for g in range(NG):
                    for r in range(2):
                        o.need("gdn_scored")
                        b = bank[2 + 2 * g + r][:, :].rearrange("p (j t i) -> p j t i", j=2, t=2)
                        hh = slice(g * H + r, g * H + H, 2)
                        v(TT(AT[:, hh, :], AT[:, hh, :], b[:, 0], ALU.mult))
                        v(TT(decG[:, hh, :], decG[:, hh, :], b[:, 1], ALU.mult), "gdn_scaled")
                for g in range(NG):
                    idb = C("ident").unsqueeze(1).broadcast_to([P, H, CH])
                    v(CP(XT[:, g * H:(g + 1) * H, :], idb))
                    v(CP(X[:, g * H:(g + 1) * H, :], idb), "X_ready")
                v(TT(be[:, :, :], be[:, :, :], beta[:, 0:2, :], ALU.mult))
                for g in range(NG):
                    o.need("kvt_copied")
                    kk = kvt[:, g * 4:g * 4 + 2, :].rearrange("p a (b d) -> p (a b) d", d=HD)
                    vv = kvt[:, g * 4 + 2:g * 4 + 4, :].rearrange("p a (b d) -> p (a b) d", d=HD)
                    o.settle()
                    gh = slice(g * H, (g + 1) * H)
                    v(TT(ktail[:, gh, :], kk, sc4[:, g, :].unsqueeze(2).broadcast_to([P, H, HD]), ALU.mult))
                    v(TT(Rk[:, gh, :], kk, be[:, g, :].unsqueeze(2).broadcast_to([P, H, HD]), ALU.mult))
                    v(TT(Rv[:, gh, :], vv, beta[:, g, :].unsqueeze(2).broadcast_to([P, H, HD]), ALU.mult), "R_ready")
                for r in range(2):
                    q = slice(r * HD, (r + 1) * HD)
                    v(TT(qh[q, :, :], act[q, 0:2, CH:SEQ], egG[q, H + r:2 * H:2, :], ALU.mult))
                for n, s in enumerate(LEVELS):
                    last = n == len(LEVELS) - 1
                    for g in range(NG):
                        gh = slice(g * H, (g + 1) * H)
                        o.need("Q_done")
                        v(TT(Qs[:, gh, :], bank[2 + g][:, :].rearrange("p (h i) -> p h i", h=H),
                             C(f"level{s}").unsqueeze(1).broadcast_to([P, H, CH]), ALU.mult), "Q_ready")
                    if n == 0:
                        ve.wait_ge(sem("Q_ready"), 2 * len(LEVELS) * l + 2)
                    for g in range(NG):
                        gh = slice(g * H, (g + 1) * H)
                        if n == 0:
                            v(TT(X[:, gh, :], X[:, gh, :], Qs[:, gh, :], ALU.subtract), "X_ready")
                        o.need("QX_done")
                        v(TT(XT[:, gh, :], XT[:, gh, :], bank[6 + g][:, :].rearrange("p (h i) -> p h i", h=H),
                             ALU.subtract), "XT_ready")
                        if n and not last:
                            o.need("XQ_done")
                            v(TT(X[:, gh, :], X[:, gh, :], bank[4 + g][:, :].rearrange("p (h i) -> p h i", h=H),
                                 ALU.subtract), "X_ready")
                for g in range(NG):
                    o.need("S_done")
                    b = bank[6][:, 0:P].rearrange("p (t d) -> p t d", t=2)
                    if g == 0:
                        v(CP(S0[:, :, :], b), "S_ready")
                    else:
                        o.settle()
                        for t in range(2):
                            for r in range(2):
                                q = slice(r * HD, (r + 1) * HD)
                                h = 2 * t + r
                                v(STT(S1[q, t, :], S0[q, t, :], egG[q, H + h, CH - 1:CH], b[q, t, :], ALU.mult,
                                      ALU.add), "S_ready" if h == 3 else None)
                        ve.wait_ge(sem("oT_ready"), 2 * (l + 1))

                ve.wait_ge(sem("gdn_p_stored"), 32 * (l + 1))
                v(ve.memset(sme[:, 0, 0:1], 0.0), "phase2")
                for g in range(NG):
                    o.need("rows_copied")
                    for h in range(H):
                        v(STT(MT[:, g * H + h, :], egS[:, g * H + h, :], cum[:, g, h:h + 1], C("causal_t"),
                              ALU.subtract, ALU.add))
                    v(TT(ws[:, g, :], egS[:, g * H:(g + 1) * H, CH - 1], cum[:, g, 0:4], ALU.subtract),
                      "MT_diff" if g else None)
                o.need("decS_ready")
                v(TT(Cg[0:HD, :, :], act[0:HD, 9:10, CH:SEQ].broadcast_to([HD, 2, CH]), egS[0:HD, H:H + 2, :], ALU.mult))
                v(TT(Cg[HD:P, :, :], act[HD:P, 9:10, CH:SEQ].broadcast_to([HD, 2, CH]), egS[HD:P, H + 2:H + 4, :],
                     ALU.mult), "Cg_ready")
                for g in range(NG):
                    for t in range(2):
                        o.need("ssd_scored")
                        gh = slice(g * H + 2 * t, g * H + 2 * t + 2)
                        v(TT(MT[:, gh, :], MT[:, gh, :],
                             bank[2 + t][:, 0:CH].unsqueeze(1).broadcast_to([P, 2, CH]), ALU.mult), "MT_ready")
                    o.need("xt_copied")
                    if g:
                        ve.wait_ge(sem("hs_done"), 2 * l + 1)
                    vs(TT(xdt[:, :, :], xt[:, 0:2, :].rearrange("p a (b d) -> p (a b) d", d=HD),
                          smp[:, g, 0:4].unsqueeze(2).broadcast_to([P, H, HD]), ALU.mult))
                    v(TT(xw[:, :, :], xdt[:, :, :], ws[:, g, :].unsqueeze(2).broadcast_to([P, H, HD]), ALU.mult),
                      "xw_ready")
                    for t in range(2):
                        o.need("yA_done")
                        v(STT(yA[:, t, g * CH:(g + 1) * CH], act[:, 6 + t, g * CH:(g + 1) * CH], dcol[:, l, t:t + 1],
                              bank[5 + t][:, 0:CH], ALU.mult, ALU.add), "yA_copied")
                    o.need("hs_done")
                    b = bank[7][:, 0:P].rearrange("p (r d) -> p r d", r=2)
                    if g == 0:
                        v(CP(hs0[:, :, :], b), "hs_ready")
                    else:
                        o.settle()
                        for t in range(2):
                            for r in range(2):
                                q = slice(t * HD, (t + 1) * HD)
                                v(STT(hs1[q, r, :], hs0[q, r, :], egS[q, H + 2 * t + r, CH - 1:CH], b[q, r, :],
                                      ALU.mult, ALU.add), "hs_ready" if t + r == 2 else None)


                def scores(n):
                    m, h = n // 4, n % 4
                    o.need("s_done")
                    s, b = s3[:, n % 2, :], bank[2 + n % 2]
                    if n >= 2:
                        ve.wait_ge(sem("PT_turned"), 8 * l + n - 1)
                    if m == 0:
                        v(STT(s[:, 0:CH], rowF[:, h, 0:CH], cum[:, 0, 4 + h:5 + h], b[:, 0:CH], ALU.subtract, ALU.add))
                        vs(STT(s[:, CH:3 * CH], rowF[:, h, :], cum[:, 1, 4 + h:5 + h], b[:, CH:3 * CH],
                               ALU.subtract, ALU.add), "s_read")
                        vs(TT(s, s, C("mask3"), ALU.add))
                    else:
                        vs(TT(s, b[:, 0:3 * CH], C(f"alibi{h}"), ALU.add), "s_read")
                    v(RED(nmx[:, n, 0:1], s[:, 0:CH], AX.X, ALU.max))
                    vs(RED(nmx[:, n, 1:2], s[:, CH:3 * CH], AX.X, ALU.max))
                    v(TS(nmx[:, n, :], nmx[:, n, :], -1.0, None, ALU.mult), "nmx_ready")

                def shares(n):
                    o.need("exp_done")
                    s = s3[:, n % 2, :]
                    vs(ve.reciprocal(rsum[:, n, :], rsum[:, n, :]))
                    v(TS(s[:, 0:CH], s[:, 0:CH], rsum[:, n, 0:1], None, ALU.mult))
                    v(TS(s[:, CH:3 * CH], s[:, CH:3 * CH], rsum[:, n, 1:2], None, ALU.mult), "P_ready")

                for n in range(8):
                    scores(n)
                    if n:
                        shares(n - 1)
                shares(7)

                v(CP(stq[0:NS, 0:4], smp[0:NS, 2, 0:4]))
                v(CP(stq[0:NS, 4:8], cin[0:NS, 2, 0:4]))
                v(CP(stq[0:NS, 8:12], cin[0:NS, 2, 8:12]))
                v(CP(stq[0:NS, 12:16], beta[0:NS, 2, :]), "stq_logs")
                o.need("fmj_copied")
                ve.wait_ge(sem("state_landed"), 64 * (l + 1))

                def spread_bt(q):
                    return fmj[:, 2 * q:2 * q + 2, :].rearrange("p t b -> p b t").unsqueeze(3).broadcast_to(
                        [P, NS, 2, HD])

                h4 = hst.rearrange("p (b t) n -> p b t n", t=2)
                g4 = gst.rearrange("p (b t) n -> p b t n", t=2)
                a4 = tmpA.rearrange("p (b t) n -> p b t n", t=2)
                b4 = tmpB.rearrange("p (b t) n -> p b t n", t=2)
                v(TT(h4, h4, spread_bt(1), ALU.mult))
                vs(TT(kb[:, :, :].rearrange("p b t -> p t b"), act[:, 6:8, SEQ:NT], fmj[:, 0:2, :], ALU.mult))
                for j in range(4):
                    o.need("bc_rows")
                    bc = bank[4 + j % 2][:, :].rearrange("p (b z t n) -> p b z t n", b=2, z=2, t=2)
                    for i in range(2):
                        b = 2 * j + i
                        vs(TT(a4[:, b], bc[:, i, 0], kb[:, b, :].unsqueeze(2).broadcast_to([P, 2, HD]), ALU.mult))
                        vs(TT(h4[:, b], h4[:, b], a4[:, b], ALU.add))
                        v(TT(b4[:, b], bc[:, i, 1], h4[:, b], ALU.mult), "hst_step" if i else None)
                o.settle()
                vs(RED(yd16[:, :], tmpB[:, :, :], AX.X, ALU.add))
                for t in range(2):
                    v(STT(yA[:, t, SEQ:NT], act[:, 6 + t, SEQ:NT], dcol[:, l, t:t + 1],
                          yd16[:, :].rearrange("p (b t) -> p t b", t=2)[:, t, :], ALU.mult, ALU.add))
                vs(TT(g4, g4, spread_bt(2), ALU.mult), "tmpA_free")
                kbc = act[:, 2:4, SEQ:NT].rearrange("p t b -> p b t").unsqueeze(3).broadcast_to([P, NS, 2, HD])
                v(TT(b4, g4, kbc, ALU.mult), "Sk_ready")
                vs(TT(kb[:, :, :].rearrange("p b t -> p t b"), act[:, 2:4, SEQ:NT], fmj[:, 6:8, :], ALU.mult))
                for j in range(2):
                    o.need("v_copied")
                    o.need("ks_done")
                    vs(TT(tmpA[:, 8 * j:8 * j + 8, :], tmpA[:, 8 * j:8 * j + 8, :],
                          bank[2 + j][:, :].rearrange("p (a d) -> p a d", a=8), ALU.subtract), "ks_read")
                vs(TT(a4, a4, kb[:, :, :].unsqueeze(3).broadcast_to([P, NS, 2, HD]), ALU.mult))
                v(TT(g4, g4, a4, ALU.add), "gst_ready")

                ve.wait_ge(sem("lf_landed"), 256 * (l + 1))
                src, dst = lf, lfb
                for step in (1, 2, 4, 8):
                    v(TT(dst[:, 0:SP_ - step, :], src[:, 0:SP_ - step, :], src[:, step:SP_, :], ALU.add))
                    vs(CP(dst[:, SP_ - step:SP_, :], src[:, SP_ - step:SP_, :]))
                    src, dst = dst, src
                assert src is lf
                v(ve.memset(sme[:, 0, 0:1], 0.0), "lf_ready")
                o.need("qbc_copied")
                for m in range(2):
                    i = index[("k", l, m)]
                    ve.wait_ge(landed[slot_of[i]], landed_at[i])
                    kk = ring[slot_of[i]][:, :].rearrange("p (s f) -> p s f", s=SP_)
                    vs(TT(kk, kk, qbc[:, m:m + 1, :].broadcast_to([P, SP_, GW]), ALU.mult))
                    v(RED(scd[:, :, 4 * m:4 * m + 4], kk.rearrange("p s (h d) -> p s h d", h=H), AX.X, ALU.add), "k_used")
                o.settle()
                v(TT(scd[:, 0:SP_ - 1, 0:4], scd[:, 0:SP_ - 1, 0:4], lf[:, 1:SP_, :], ALU.add))
                v(TT(scd[:, :, 4:8], scd[:, :, 4:8], C("alibi_dec").rearrange("p (s h) -> p s h", h=H), ALU.add))
                o.settle()
                o.need("bias_done")
                vs(TT(scd[:, :, 0:4], scd[:, :, 0:4], bank[3][:, 0:H].unsqueeze(1).broadcast_to([P, SP_, H]),
                      ALU.add), "bias_added")
                vs(RED(mcol[:, :], scd[:, :, :].rearrange("p s h -> p h s"), AX.X, ALU.max))
                ve.wait_ge(sem("stok_copied"), 3 * (l + 1))
                tw = tmpA[0:NS, 0:8, :]
                vs(TT(tw, stok[0:NS, 0:2, :].rearrange("p m (h d) -> p (m h) d", d=HD),
                      stok[0:NS, 2:4, :].rearrange("p m (h d) -> p (m h) d", d=HD), ALU.mult))
                v(RED(sself[0:NS, :], tw, AX.X, ALU.add), "max_ready")
                o.need("max_turned")
                vs(RED(ms8[0:8, :], bank[4][0:8, 0:P].rearrange("p (b c) -> p b c", b=NS), AX.X, ALU.max))
                vs(TT(ms8[0:8, :], ms8[0:8, :], bank[4][0:8, P:P + NS], ALU.max), "mcol_ready")
                o.need("m_turned")
                vs(CP(mtok[0:NS, :], bank[5][0:NS, 0:8]), "mtok_copied")
                vs(TT(sself[0:NS, :], sself[0:NS, :], mtok[0:NS, :], ALU.subtract))
                o.need("m_spread")
                v(TT(scd[:, :, :], scd[:, :, :], bank[6][:, 0:8].unsqueeze(1).broadcast_to([P, SP_, 8]),
                     ALU.subtract), "m_spread_read")
                o.need("scd_exp")
                v(RED(psums[:, :], scd[:, :, :].rearrange("p s h -> p h s"), AX.X, ALU.add), "psums_ready")
                o.need("den_done")
                vs(TT(rden[0:NS, :], sself[0:NS, :], bank[7][0:NS, 0:8], ALU.add))
                vs(ve.reciprocal(rden[0:NS, :], rden[0:NS, :]))
                v(TT(sself[0:NS, :], sself[0:NS, :], rden[0:NS, :], ALU.mult), "rden_ready")
                o.need("rden_spread")
                vs(TT(scd[:, :, :], scd[:, :, :], bank[2][:, 0:8].unsqueeze(1).broadcast_to([P, SP_, 8]), ALU.mult),
                   "Pd_scaled")
                for m in range(2):
                    v(TT(Pd[:, m * SP_:(m + 1) * SP_, :].rearrange("p s (b h) -> p s b h", b=NS),
                         scd[:, :, 4 * m:4 * m + 4].unsqueeze(2).broadcast_to([P, SP_, NS, H]),
                         C("own_col").unsqueeze(1).unsqueeze(3).broadcast_to([P, SP_, NS, H]), ALU.mult),
                      "Pd_ready" if m else None)
                o.need("psb_copied")
                for m in range(2):
                    v(TT(psb[:, 2 * m:2 * m + 2, :], psb[:, 2 * m:2 * m + 2, :],
                         fm[:, 8 + 2 * m:10 + 2 * m, SEQ:NT], ALU.mult))
                o.settle()
                o.need("ypv_turned")
                yd = bank[6][:, 0:4 * NS * H].rearrange("p (j b h) -> p j b h", j=4, b=NS)
                for m in range(2):
                    for t in range(2):
                        for r in range(2):
                            q = slice(r * HD, (r + 1) * HD)
                            v(TT(yT[q, (2, 6)[m] + t, SEQ:NT], psb[q, 2 * m + t, :], yd[q, 2 * m + t, :, 2 * t + r],
                                 ALU.add), "yd_read" if m + t + r == 3 else None)
                o.settle()
                o.need("zz_ready")
                vs(TT(yA[:, :, :], yA[:, :, :], zz[:, 0:2, :], ALU.mult), "yA_gated")
                o.need("head_rstd")
                for t in range(2):
                    v(STT(yT[:, t, :], yA[:, t, :], prm2[:, 46 * l + t:46 * l + t + 1], rstd[:, 2, :], ALU.mult,
                          ALU.mult))
                for t in range(2):
                    o.need("head_rstd")
                    vs(STT(oT[:, t, :], oT[:, t, :], g_[4], rstd[:, t, :], ALU.mult, ALU.mult))
                ve.wait_ge(sem("yBD_copied"), 4 * (l + 1))
                v(TT(yT[:, 4:6, :], oT[:, :, :], zz[:, 2:4, :], ALU.mult), "yT_ready")

                def add_x(src, m, gate, name):
                    v(STT(xT[:, m, 0:SEQ], src[:, 0:SEQ], modT[:, gate + m, 0:1], xT[:, m, 0:SEQ], ALU.mult, ALU.add))
                    vs(TT(sxy[:, :], src[:, SEQ:NT], modT[:, gate + m, 1:9], ALU.mult), name)
                    vs(TT(xT[:, m, SEQ:NT], xT[:, m, SEQ:NT], sxy[:, :], ALU.add))

                add_bias(l, 4 * MIX_CHUNKS, 48)
                t0 = ticks_before(index[("out", l, 0)])
                for m in range(KD):
                    ve.wait_ge(tile_done, t0 + m + 1)
                    add_x(bank[m % 4], m, 16, "x_added")
                v(ve.memset(sme[:, 0, 0:1], 0.0), "x_whole")
                modulate(24, prm1[:, 112 + 8 * l:120 + 8 * l])
                ve.wait_ge(sem("stored"), 16 * STORES * (l + 1))
                if l == 0:
                    v(ve.memset(sg[:, :, 0:1], 0.0), "ffn_phase")
                    t0 = ticks_before(index[("gu", 0, 0)])
                    for half in range(2):
                        k = slice(4 * half, 4 * half + 4)
                        o.need("split_high")
                        v(TT(hL[:, k, :], hT[:, k, :], hH[:, k, :], ALU.subtract), "split_low")
                    for t in range(len(D_PIECES)):
                        o.need("split_high")
                        src, split = dense_view(t)
                        v(TT(split(w_low), src, split(w_high), ALU.subtract), "split_low")
                        if t in f_made:
                            f = f_made[t]
                            ve.wait_ge(tile_done, t0 + 2 * f + 2)
                            o.need("sg_ready")
                            if f >= 2:
                                ve.wait_ge(sem("f_low"), start_of("f_low") + f - 1)
                            v(TT(ft[:, f % 2, :], sg[:, f % 2, :], bank[2 * (f % 2) + 1][:, 0:NT], ALU.mult),
                              "hid_ready")
                        if t in f_split:
                            f = f_split[t]
                            o.need("f_high")
                            v(TT(fL[:, f, :], ft[:, f % 2, :], fH[:, f, :], ALU.subtract), "f_low")
                        if t - SPLITS + 1 in d_out:
                            m = d_out.index(t - SPLITS + 1)
                            ve.wait_ge(tile_done, t0 + d_out[m])
                            add_x(bank[4 + m % 4], m, 40, "acc_ready")
                    for m in range(KD):
                        if d_out[m] + SPLITS - 1 >= len(D_PIECES):
                            ve.wait_ge(tile_done, t0 + d_out[m])
                            add_x(bank[4 + m % 4], m, 40, "acc_ready")
                    v(ve.memset(sxy[:, 0:1], 0.0), "x_whole")
                else:
                    v(ve.memset(sg[:, :, 0:1], 0.0), "ffn_phase")
                    v(ve.memset(lg[:, :, :], 0.0))
                    v(ve.memset(acc[:, :, :], 0.0))
                    v(ve.memset(place[:, :, :], 0.0))
                    o.settle()
                    o.need("lg_done")
                    v(CP(lg[:, 0:2, :], bank[0][:, 0:16].rearrange("p (g e) -> p g e", g=2)))
                    vs(CP(lg[0:NS, 2, :], bank[0][0:NS, 16:24]))
                    mine = lg[:, :, :].rearrange("p g e -> p (g e)").unsqueeze(2).broadcast_to([P, 3 * NE, NE])
                    for g in range(3):
                        row = slice(g * NE, (g + 1) * NE)
                        me = lg[:, g, :].unsqueeze(2).broadcast_to([P, NE, NE])
                        ot = lg[:, g, :].unsqueeze(1).broadcast_to([P, NE, NE])
                        v(TT(cmp[:, row, :], ot, me, ALU.is_gt))
                        vs(TT(cmp2[:, row, :], ot, me, ALU.is_equal))
                        v(TT(cmp2[:, row, :], cmp2[:, row, :], C("tie").rearrange("p (a b) -> p a b", a=NE), ALU.mult))
                    o.settle()
                    vs(TT(cmp[:, :, :], cmp[:, :, :], cmp2[:, :, :], ALU.add))
                    v(RED(rank[:, :, :], cmp.rearrange("p (g e) f -> p g e f", g=3), AX.X, ALU.add))
                    vs(RED(v1[:, :], lg[:, :, :], AX.X, ALU.max))
                    vs(TT(lg[:, :, :], lg[:, :, :], v1[:, :].unsqueeze(2).broadcast_to([P, 3, NE]), ALU.subtract),
                       "lg_shift")
                    vs(TS(rank[:, :, :], rank[:, :, :], 1.5, None, ALU.is_lt))
                    o.need("lg_exp")
                    vs(TT(gates[:, :, :], gates[:, :, :], rank[:, :, :], ALU.mult))
                    vs(RED(v1[:, :], gates[:, :, :], AX.X, ALU.add))
                    vs(ve.reciprocal(v1[:, :], v1[:, :]))
                    v(TT(gates[:, :, :], gates[:, :, :], v1[:, :].unsqueeze(2).broadcast_to([P, 3, NE]), ALU.mult),
                      "gates_ready")
                    o.need("places_done")
                    v(TT(place[:, 0:2, 0:NE], bank[4][:, 0:2 * NE].rearrange("p (g e) -> p g e", g=2),
                         rank[:, 0:2, :], ALU.mult))
                    v(TT(place[0:NS, 2, 0:NE], bank[4][0:NS, 2 * NE:3 * NE], rank[0:NS, 2, :], ALU.mult))
                    vs(RED(most[:, 0:1], bank[4][:, 3 * NE:4 * NE], AX.X, ALU.max), "places_read")
                    vs(ve.memset(most[:, 3:4], 1.0))
                    for k in range(1, ROUNDS):
                        vs(TS(most[:, 1:2], most[:, 0:1], float(k * CAP), None, ALU.is_gt))
                        vs(TT(most[:, 3:4], most[:, 3:4], most[:, 1:2], ALU.add))
                    v(CP(rounds[:, :], most[:, 3:4]), "rounds_ready")
                    o.need("iota_copied")

                    def one_hot(pair):
                        TT(G[:, :, :, :], iota[:, 0:CAP].unsqueeze(1).unsqueeze(1).broadcast_to([P, 3, 2, CAP]),
                           pair.unsqueeze(3).broadcast_to([P, 3, 2, CAP]), ALU.is_equal).then_inc(sem("G_ready"), 1)

                    def low_tokens(z, r, q):
                        ve.wait_ge(sem("hc_high"), pair_count("hc_high", 4, r, q, z + 1))
                        TT(hcL[:, 2 * z:2 * z + 2, :], bank[6 + z % 2][:, 0:4 * CAP].rearrange("p (k c) -> p k c", k=2),
                           hcH[:, 2 * z:2 * z + 2, :], ALU.subtract).then_inc(sem("hc_copied"), 1)

                    def low_turned(r, e, c):
                        ve.wait_ge(sem("hidT_high"), count(start_of("hidT_high"), E_GU, 0, r, e, c + 1))
                        TT(hidL[:, 2 * c:2 * c + 2, :],
                           bank[2 + c % 2][:, 0:2 * CAP].rearrange("p (i c) -> p i c", i=2),
                           hidH[:, 2 * c:2 * c + 2, :], ALU.subtract).then_inc(sem("hidT_copied"), 1)

                    def add_parts(r, e, c):
                        for d in (2 * c, 2 * c + 1):
                            ve.wait_ge(sem("part_done"), count(start_of("part_done"), KD, 0, r, e, d + 1))
                            TT(acc[:, d, :], acc[:, d, :], bank[d % 4][:, 0:NT], ALU.add).then_inc(
                                sem("acc_ready"), 1)

                    def one_round(r):
                        if not isinstance(r, int):
                            ve.wait_ge(sem("G_ready"), pair_count("G_ready", 1, r, 0, 0))
                            ve.wait_ge(sem("hc_done"), pair_count("hc_done", 4, r, 0, 0))
                            TS(iota[:, :], iota[:, :], float(CAP), None, ALU.add).then_inc(sem("shifted"), 1)
                            TS(iota_col[:, :], iota_col[:, :], float(CAP), None, ALU.add).then_inc(sem("shifted"), 1)
                            ve.wait_ge(sem("shifted"), r * 2 + start_of("shifted"))
                        one_hot(place[:, :, 0:2])
                        for z in range(4):
                            low_tokens(z, r, 0)
                        if isinstance(r, int):
                            ve.wait_ge(sem("pbc_copied"), start_of("pbc_copied") + NE)
                        with ve.Fori(0, PAIRS) as p:
                            for j, (t, (i, kind, c, k0, nk)) in product(range(2), enumerate(E_PIECES)):
                                e = p * 2 + j
                                if t == 0:
                                    STT(GwT[:, :], pbc[:, bass.ds(e, 1), :].rearrange("p o n -> p (o n)"),
                                        iota_col[:, 0:1], gbc[:, bass.ds(e, 1), :].rearrange("p o n -> p (o n)"),
                                        ALU.is_equal, ALU.mult)
                                ve.wait_ge(sem("w_high_ready"),
                                           count(start_of("w_high_ready"), E_TICKS, 0, r, e, t + 1))
                                src, split = piece_view(t, e_slot[i])
                                TT(split(w_low), src, split(w_high), ALU.subtract).then_inc(sem("w_low_ready"), 1)
                                if t in gu_read:
                                    c = gu_read[t]
                                    ve.wait_ge(sem("sg_ready"), count(FF // P, E_GU, 0, r, e, c + 1))
                                    ve.wait_ge(sem("hidT_done"),
                                               count(start_of("hidT_done"), E_GU, 0, r, e, max(c - 1, 0)))
                                    TT(hidc[0:CAP, c % 2, :], sgc[0:CAP, c % 2, :], bank[c % 2][0:CAP, 256:512],
                                       ALU.mult).then_inc(sem("hid_ready"), 1)
                                    if j and c == 1:
                                        ve.wait_ge(sem("hc_done"), pair_count("hc_done", 4, r, p, 4))
                                        one_hot(place[:, :, 2:NE + 2][:, :, bass.ds(p * 2, 2)])
                                    if c == E_GU - 1 and j:
                                        low_tokens(0, r, p + 1)
                                        low_tokens(1, r, p + 1)
                                if t in turned_read:
                                    low_turned(r, e, turned_read[t])
                                if t in down_read and down_read[t]:
                                    add_parts(r, e, down_read[t] - 1)
                                    if down_read[t] == E_DN - 2 and j:
                                        low_tokens(2, r, p + 1)
                                if t == E_TICKS - 1:
                                    add_parts(r, e, E_DN - 2)
                                    if j:
                                        low_tokens(3, r, p + 1)
                                    add_parts(r, e, E_DN - 1)
                        ve.wait_ge(sem("acc_ready"), count(KD, KD, 0, r, NE, 0))
                        ve.memset(most[:, 1:2], 0.0)

                    all_rounds(ve, one_round)
                    for m in range(KD):
                        add_x(acc[:, m, :], m, 40, None)
                    v(ve.memset(sxy[:, 0:1], 0.0), "x_final")

        @block.gpsimd
        def _(pool):
            o = Order(pool, "pool_chain")
            stores = [0]

            def store(dst, src):
                pool.dma_start(dst, src).then_inc(sem("stored"), 16)
                stores[0] += 1

            def halves(dst, src, l):
                for r in range(2):
                    store(O[dst][l].rearrange("b (t r) p n -> r p (b t) n", r=2)[r], src[r * HD:(r + 1) * HD])

            def load(dst, src, name):
                pool.dma_start(dst, src).then_inc(sem(name), 16)

            for l in range(DEPTH):
                r = 46 * l
                load(prow2[r:r + 2, :], A["ssd_norm"][l].rearrange("(m p) -> m p", p=P), "params_landed")
                load(prow2[r + 2:r + 18, :], A["ssd_conv_w"][l].rearrange("k (m p) -> (k m) p", p=P), "params_landed")
                load(prow2[r + 18:r + 22, :], A["ssd_conv_b"][l].rearrange("(m p) -> m p", p=P), "params_landed")
                load(prow2[r + 22:r + 46, :], A["gdn_conv_w"][l].rearrange("k (m p) -> (k m) p", p=P), "params_landed")
                for n, name in enumerate(("fox_q_norm", "moba_q_norm", "fox_k_norm", "moba_k_norm", "gdn_norm")):
                    for r in range(2):
                        q = 92 + 5 * l + n
                        load(prow2[q:q + 1, r * HD:(r + 1) * HD], A[name][l:l + 1, :], "params_landed")
            with nc.allow_non_contiguous_dma(reason="small per-head columns"):
                for l in range(DEPTH):
                    for col, n, at in SMALL:
                        load(w_small[:, l, :, at:at + n],
                             A["w_in"][l].rearrange("(k p) n -> p k n", p=P)[:, :, col:col + n], "small_landed")
                for name, at in (("ssd_dt_bias", 0), ("fox_b_f", 4), ("gdn_dt_bias", 12)):
                    load(brow[:, :, at:at + 4], A[name].partition_broadcast(P), "small_landed")
                for name, at in (("ssd_a_log", 0), ("gdn_a_log", 4)):
                    load(alog[:, :, at:at + 4], A[name].partition_broadcast(P), "small_landed")
                for r in range(2):
                    for l in range(DEPTH):
                        load(dcol[r * HD:(r + 1) * HD, l, :],
                             A["ssd_d"][l].rearrange("(t r) -> r t", r=2)[r].partition_broadcast(HD), "small_landed")
                load(router[:, :, :], A["moe_router"][0].rearrange("(k p) e -> p k e", p=P), "small_landed")

            for l in range(DEPTH):
                at = stores[0]
                with nc.allow_non_contiguous_dma(reason="forget gates of four heads"):
                    pool.wait_ge(sem("cin_ready"), l + 1)
                    store(O["fox_logf_p"][l, 0].rearrange("(g p) h -> p g h", p=P), nlf[:, 0:2, :])
                    store(O["fox_logf_s"][l].rearrange("b s h -> (b s) h"), nlf[0:NS, 2, :])
                pool.wait_ge(sem("tail_copied"), 3 * (l + 1))
                for lo, n, name in ((0, QKV, "gdn_conv"), (QKV, XBC, "ssm_conv")):
                    store(O[name + "_p"][l, 0], convrow[0:3, lo:lo + n])
                    store(O[name + "_s"][l].rearrange("b k c -> (b k) c"), convrow[3:27, lo:lo + n])
                pool.wait_ge(sem("S_ready"), 2 * (l + 1))
                for r in range(2):
                    pool.dma_start(O["gdn_p"][l, 0].rearrange("(t r) p n -> r p t n", r=2)[r],
                                   S1[r * HD:(r + 1) * HD]).then_inc(sem("gdn_p_stored"), 16)
                pool.wait_ge(sem("hsout_copied"), l + 1)
                for r in range(2):
                    store(O["ssm_p"][l, 0].rearrange("(t r) p n -> r p t n", r=2)[r],
                          hsout[r * HD:(r + 1) * HD, :].rearrange("p (t n) -> p t n", t=2))
                for i, name in enumerate(("fox_k", "moba_k", "fox_v", "moba_v")):
                    pool.wait_ge(sem("kvp_copied"), 4 * l + i + 1)
                    store(O[name + "_p"][l, 0].rearrange("(g p) h d -> p g (h d)", p=P), kvp[:, i * NG:(i + 1) * NG, :])
                pool.wait_ge(sem("stok_copied"), 3 * (l + 1))
                for i, name in enumerate(("fox_k", "moba_k", "fox_v", "moba_v")):
                    store(O[name + "_s"][l].rearrange("b s h d -> (b s) (h d)"), stok[0:NS, 2 + i, :])
                pool.wait_ge(sem("hst_step"), 4 * (l + 1))
                halves("ssm_s", hst, l)
                pool.wait_ge(sem("gst_ready"), l + 1)
                halves("gdn_s", gst, l)
                assert stores[0] - at == STORES, stores[0] - at
            pool.wait_ge(sem("out_copied"), 6)
            store(O["y_prompt"][0].rearrange("(g p) d -> p g d", p=P), stage[:, 0:2, :])
            store(O["y_sample"].rearrange("b s d -> (b s) d"), stage[0:NS, 2, :])
            pool.wait_ge(sem("stored"), 16 * stores[0])
            pool.wait_ge(sem("gdn_p_stored"), 32 * DEPTH)


_INS = ["x_prompt", "x_sample", "cache_fox_k", "cache_fox_v", "cache_fox_logf", "cache_moba_k", "cache_moba_v",
        "state_ssm", "state_ssm_conv", "state_gdn", "state_gdn_conv", "page_table", "c_prompt", "c_sample",
        "w_ada", "b_ada", "norm_mix", "norm_ffn", "w_in", "w_out", "ssd_conv_w", "ssd_conv_b", "ssd_dt_bias",
        "ssd_a_log", "ssd_d", "ssd_norm", "fox_b_f", "fox_q_norm", "fox_k_norm", "gdn_conv_w", "gdn_a_log",
        "gdn_dt_bias", "gdn_norm", "moba_q_norm", "moba_k_norm", "ffn_w_gate", "ffn_w_up", "ffn_w_down",
        "moe_router", "moe_w_gate", "moe_w_up", "moe_w_down"]


def _outs():
    outs = [("y_prompt", (1, SEQ, D)), ("y_sample", (NS, 1, D))]
    for s, b, n in (("p", 1, SEQ), ("s", NS, 1)):
        outs += [(f"fox_k_{s}", (DEPTH, b, n, H, HD)), (f"fox_v_{s}", (DEPTH, b, n, H, HD)),
                 (f"fox_logf_{s}", (DEPTH, b, n, H)), (f"moba_k_{s}", (DEPTH, b, n, H, HD)),
                 (f"moba_v_{s}", (DEPTH, b, n, H, HD)), (f"ssm_{s}", (DEPTH, b, H, HD, HD)),
                 (f"ssm_conv_{s}", (DEPTH, b, CW - 1, XBC)), (f"gdn_{s}", (DEPTH, b, H, HD, HD)),
                 (f"gdn_conv_{s}", (DEPTH, b, CW - 1, QKV))]
    return outs


def kernel(**inputs):
    import concourse.bacc as bacc
    from concourse.bass_utils import run_bass_kernel_spmd

    nc = bacc.Bacc("TRN2", target_bir_lowering=False, num_devices=1)
    arrays, A, O = {}, {}, {}
    table, const_at = consts()
    for name in _INS + ["consts"]:
        a = table if name == "consts" else np.ascontiguousarray(inputs[name])
        arrays[f"in_{name}"] = a
        A[name] = nc.dram_tensor(f"in_{name}", a.shape, mybir.dt.from_np(a.dtype), kind="ExternalInput").ap()
    outs = _outs()
    for name, shape in outs:
        O[name] = nc.dram_tensor(f"out_{name}", shape, F32, kind="ExternalOutput").ap()
    build(nc, A, O, const_at, table.shape[1])
    r = run_bass_kernel_spmd(nc, [arrays], core_ids=[0])
    return tuple(r.results[0][f"out_{name}"] for name, _ in outs)
```
